# Optimizing a Trainium2 kernel written in Bass

```python
import jax, jax.numpy as jnp
from jax import lax
import numpy as np
import math

D_MODEL = 1024
BATCH = 1
SEQ = 256
DEPTH = 1

CHUNK = 64
D_CONV = D_MODEL
CONV_WIDTH = 31
D_SGU = D_MODEL
SGU_BLOCK = 128
SGU_GROUPS = 8
SGU_GROUP_DIM = D_SGU // SGU_GROUPS
D_IN = 2 * D_CONV + 2 * D_SGU + 2 * D_MODEL
SPLITS = (D_CONV, 2 * D_CONV, 2 * D_CONV + 2 * D_SGU, 2 * D_CONV + 2 * D_SGU + D_MODEL)
N_EXPERTS = 32
TOP_K = 4
D_EXPERT = D_MODEL
SWIGLU_LIMIT = 7.0
SWIGLU_ALPHA = 1.702
MOE_BLOCK = 128
LN_EPS = 1e-5
DEEPNORM_ALPHA = float((2 * DEPTH) ** 0.25)
DEEPNORM_BETA = float((8 * DEPTH) ** -0.25)


def _layer_norm(x, gain=None, bias=None):
    xf = x.astype(jnp.float32)
    mu = jnp.mean(xf, axis=-1, keepdims=True)
    var = jnp.mean(jnp.square(xf - mu), axis=-1, keepdims=True)
    y = (xf - mu) * lax.rsqrt(var + LN_EPS)
    if gain is not None:
        y = y * gain.astype(jnp.float32) + bias.astype(jnp.float32)
    return y.astype(x.dtype)

def _causal_depthwise_conv(x, w, b):
    y = lax.conv_general_dilated(
        x, w[:, None, :], window_strides=(1,), padding=[(CONV_WIDTH - 1, 0)],
        dimension_numbers=('NWC', 'WIO', 'NWC'), feature_group_count=x.shape[-1])
    return y + b

def _spatial_gating(u, v, ln_g, ln_b, w_s, b_s):
    B, S, _ = v.shape
    n_blk = S // SGU_BLOCK
    v = _layer_norm(v, ln_g, ln_b).reshape(B, n_blk, SGU_BLOCK, SGU_GROUPS, SGU_GROUP_DIM)
    chunk_id = jnp.arange(SGU_BLOCK) // CHUNK
    mask = chunk_id[:, None] >= chunk_id[None, :]
    w = jnp.where(mask[None], w_s, 0)
    mixed = jnp.einsum('gij,bnjgc->bnigc', w, v) + jnp.transpose(b_s)[None, None, :, :, None]
    return u * mixed.reshape(B, S, D_SGU)

def _token_mixer(h, w_in, b_in, conv_w, conv_b, ln_a_g, ln_a_b, w_a, b_a,
                 ln_v_g, ln_v_b, w_s, b_s, w_b, b_b, w_out, b_out):
    z = h @ w_in + b_in
    a_val, a_gate, sgu, g_a, g_b = jnp.split(z, SPLITS, axis=-1)
    ya = a_val * jax.nn.sigmoid(a_gate)
    ya = _causal_depthwise_conv(ya, conv_w, conv_b)
    ya = jax.nn.silu(_layer_norm(ya, ln_a_g, ln_a_b))
    ya = ya @ w_a + b_a
    u, v = jnp.split(jax.nn.gelu(sgu, approximate=False), 2, axis=-1)
    yb = _spatial_gating(u, v, ln_v_g, ln_v_b, w_s, b_s) @ w_b + b_b
    m = jax.nn.sigmoid(g_a) * ya + jax.nn.sigmoid(g_b) * yb
    return m @ w_out + b_out

def _moe(h, w_router, b_router, w_gu, b_gu, w_dn, b_dn):
    B, S, D = h.shape
    T = B * S
    xt = h.reshape(T, D)
    logits = (xt @ w_router + b_router).astype(jnp.float32)
    top_logits, top_idx = lax.top_k(logits, TOP_K)
    top_w = jax.nn.softmax(top_logits, axis=-1)
    flat_e = top_idx.reshape(-1)
    order = jnp.argsort(flat_e)
    sorted_e = flat_e[order]
    counts = jnp.bincount(flat_e, length=N_EXPERTS)
    padded = (counts + MOE_BLOCK - 1) // MOE_BLOCK * MOE_BLOCK
    start = jnp.cumsum(counts) - counts
    pad_end = jnp.cumsum(padded)
    pad_start = pad_end - padded
    dest = pad_start[sorted_e] + jnp.arange(T * TOP_K) - start[sorted_e]
    n_slots = T * TOP_K + N_EXPERTS * MOE_BLOCK
    n_blocks = n_slots // MOE_BLOCK
    slot_tok = jnp.full((n_slots,), T, jnp.int32).at[dest].set((order // TOP_K).astype(jnp.int32))
    slot_w = jnp.zeros((n_slots,), jnp.float32).at[dest].set(top_w.reshape(-1)[order])
    block_e = jnp.minimum(
        jnp.searchsorted(pad_end, jnp.arange(n_blocks) * MOE_BLOCK, side='right'), N_EXPERTS - 1)
    xt_pad = jnp.concatenate([xt, jnp.zeros((1, D), xt.dtype)], axis=0)

    def expert_block(args):
        tok, e = args
        xb = xt_pad[tok]
        gate, up = jnp.split(xb @ w_gu[e] + b_gu[e], 2, axis=-1)
        gate = jnp.minimum(gate, SWIGLU_LIMIT)
        up = jnp.clip(up, -SWIGLU_LIMIT, SWIGLU_LIMIT)
        act = (up + 1) * (gate * jax.nn.sigmoid(SWIGLU_ALPHA * gate))
        return act @ w_dn[e] + b_dn[e]

    yb = lax.map(expert_block, (slot_tok.reshape(n_blocks, MOE_BLOCK), block_e))
    y = jnp.zeros((T + 1, D), jnp.float32).at[slot_tok].add(
        yb.reshape(n_slots, D).astype(jnp.float32) * slot_w[:, None])
    return y[:T].reshape(B, S, D).astype(h.dtype)

def _normal(k, shape, scale):
    return jax.random.normal(k, shape, jnp.float32) * scale

def first_inputs(seed: int = 0) -> dict:
    key = jax.random.key(seed)
    ks = jax.random.split(key, 32)
    L, D = DEPTH, D_MODEL
    return {
        "x": _normal(ks[0], (BATCH, SEQ, D), 1.0),
        "c": _normal(ks[1], (BATCH, D), 1.0),
        "w_mod": _normal(ks[2], (L, D, 6 * D), 0.5 * D ** -0.5),
        "b_mod": _normal(ks[3], (L, 6 * D), 0.02),
        "w_in": _normal(ks[4], (L, D, D_IN), D ** -0.5),
        "b_in": _normal(ks[5], (L, D_IN), 0.02),
        "conv_w": _normal(ks[6], (L, CONV_WIDTH, D_CONV), CONV_WIDTH ** -0.5),
        "conv_b": _normal(ks[7], (L, D_CONV), 0.02),
        "ln_a_g": 1.0 + _normal(ks[8], (L, D_CONV), 0.05),
        "ln_a_b": _normal(ks[9], (L, D_CONV), 0.02),
        "w_a": _normal(ks[10], (L, D_CONV, D), D_CONV ** -0.5),
        "b_a": _normal(ks[11], (L, D), 0.02),
        "ln_v_g": 1.0 + _normal(ks[12], (L, D_SGU), 0.05),
        "ln_v_b": _normal(ks[13], (L, D_SGU), 0.02),
        "w_s": _normal(ks[14], (L, SGU_GROUPS, SGU_BLOCK, SGU_BLOCK), SGU_BLOCK ** -0.5),
        "b_s": 1.0 + _normal(ks[15], (L, SGU_GROUPS, SGU_BLOCK), 0.1),
        "w_b": _normal(ks[16], (L, D_SGU, D), D_SGU ** -0.5),
        "b_b": _normal(ks[17], (L, D), 0.02),
        "w_out": _normal(ks[18], (L, D, D), DEEPNORM_BETA * D ** -0.5),
        "b_out": _normal(ks[19], (L, D), 0.02),
        "post1_g": 1.0 + _normal(ks[20], (L, D), 0.05),
        "post1_b": _normal(ks[21], (L, D), 0.02),
        "w_router": _normal(ks[22], (L, D, N_EXPERTS), D ** -0.5),
        "b_router": _normal(ks[23], (L, N_EXPERTS), 0.01),
        "w_gu": _normal(ks[24], (L, N_EXPERTS, D, 2 * D_EXPERT), D ** -0.5),
        "b_gu": _normal(ks[25], (L, N_EXPERTS, 2 * D_EXPERT), 0.02),
        "w_dn": _normal(ks[26], (L, N_EXPERTS, D_EXPERT, D), DEEPNORM_BETA * D_EXPERT ** -0.5),
        "b_dn": _normal(ks[27], (L, N_EXPERTS, D), 0.02),
        "post2_g": 1.0 + _normal(ks[28], (L, D), 0.05),
        "post2_b": _normal(ks[29], (L, D), 0.02),
    }

def first_block(x, c, w_mod, b_mod, w_in, b_in, conv_w, conv_b, ln_a_g, ln_a_b, w_a, b_a,
              ln_v_g, ln_v_b, w_s, b_s, w_b, b_b, w_out, b_out, post1_g, post1_b,
              w_router, b_router, w_gu, b_gu, w_dn, b_dn, post2_g, post2_b):
    cond = jax.nn.silu(c)
    for l in range(DEPTH):
        mod = cond @ w_mod[l] + b_mod[l]
        sh1, sc1, g1, sh2, sc2, g2 = [m[:, None, :] for m in jnp.split(mod, 6, axis=-1)]
        h = _layer_norm(x) * (1 + sc1) + sh1
        y = _token_mixer(h, w_in[l], b_in[l], conv_w[l], conv_b[l], ln_a_g[l], ln_a_b[l],
                         w_a[l], b_a[l], ln_v_g[l], ln_v_b[l], w_s[l], b_s[l], w_b[l], b_b[l],
                         w_out[l], b_out[l])
        x = _layer_norm(DEEPNORM_ALPHA * x + g1 * y, post1_g[l], post1_b[l])
        h = _layer_norm(x) * (1 + sc2) + sh2
        y = _moe(h, w_router[l], b_router[l], w_gu[l], b_gu[l], w_dn[l], b_dn[l])
        x = _layer_norm(DEEPNORM_ALPHA * x + g2 * y, post2_g[l], post2_b[l])
    return x


RET_WIDTH = D_MODEL
RET_HEADS = 8
RET_HEAD_DIM = RET_WIDTH // RET_HEADS
RET_CHUNK = 128
ROPE_BASE = 10000.0
LRU_WIDTH = D_MODEL
LRU_BLOCKS = 8
LRU_BLOCK_DIM = LRU_WIDTH // LRU_BLOCKS
LRU_C = 8.0
CONV_WIDTH_2 = 4
MIX_WIDTH = RET_WIDTH + LRU_WIDTH
IN_SPLITS = (RET_WIDTH, 2 * RET_WIDTH, 3 * RET_WIDTH, 4 * RET_WIDTH, 4 * RET_WIDTH + LRU_WIDTH)
IN_WIDTH = 4 * RET_WIDTH + 2 * LRU_WIDTH
NORM_EPS = 1e-6


def rms_norm(x, g):
    x32 = x.astype(jnp.float32)
    y = x32 * lax.rsqrt(jnp.mean(x32 * x32, axis=-1, keepdims=True) + NORM_EPS)
    return (y * g.astype(jnp.float32)).astype(x.dtype)

def rotary(x):
    T, d = x.shape[1], x.shape[-1]
    inv_freq = ROPE_BASE ** (-jnp.arange(0, d, 2, dtype=jnp.float32) / d)
    ang = jnp.arange(T, dtype=jnp.float32)[:, None] * inv_freq[None, :]
    cos = jnp.cos(ang)[None, :, None, :]
    sin = jnp.sin(ang)[None, :, None, :]
    x1, x2 = x[..., : d // 2], x[..., d // 2:]
    return jnp.concatenate([x1 * cos - x2 * sin, x1 * sin + x2 * cos], axis=-1)

def chunkwise_retention(q, k, v):
    B, T, H, d = q.shape
    C = RET_CHUNK
    nc = T // C
    log_g = jnp.log1p(-jnp.exp2(-5.0 - jnp.arange(H, dtype=jnp.float32)))
    idx = jnp.arange(C, dtype=jnp.float32)
    rel = idx[:, None] - idx[None, :]
    decay_mat = jnp.where(rel[None] >= 0,
                          jnp.exp(jnp.maximum(rel, 0.0)[None] * log_g[:, None, None]), 0.0)
    zeta = jnp.exp((C - 1 - idx)[None, :] * log_g[:, None])
    xi = jnp.exp((idx + 1)[None, :] * log_g[:, None])
    chunk_decay = jnp.exp(C * log_g)

    qc = q.reshape(B, nc, C, H, d)
    kc = k.reshape(B, nc, C, H, d)
    vc = v.reshape(B, nc, C, H, d)

    scores = jnp.einsum('bnqhd,bnkhd->bnhqk', qc, kc) * decay_mat[None, None]
    intra = jnp.einsum('bnhqk,bnkhe->bnqhe', scores, vc)

    kv = jnp.einsum('bnkhd,hk,bnkhe->nbhde', kc, zeta, vc)

    def step(state, kv_n):
        new_state = chunk_decay[None, :, None, None] * state + kv_n
        return new_state, state

    _, prev_states = lax.scan(step, jnp.zeros((B, H, d, d), jnp.float32), kv)
    prev_states = jnp.moveaxis(prev_states, 0, 1)
    cross = jnp.einsum('bnqhd,bnhde->bnqhe', qc, prev_states) * xi.T[None, None, :, :, None]
    return (intra + cross).reshape(B, T, H, d)

def group_norm_heads(o):
    mu = jnp.mean(o, axis=-1, keepdims=True)
    var = jnp.mean(jnp.square(o - mu), axis=-1, keepdims=True)
    return (o - mu) * lax.rsqrt(var + NORM_EPS)

def causal_depthwise_conv(x, w, b):
    T = x.shape[1]
    xp = jnp.pad(x, ((0, 0), (CONV_WIDTH_2 - 1, 0), (0, 0)))
    out = b[None, None, :]
    for j in range(CONV_WIDTH_2):
        out = out + xp[:, j:j + T, :] * w[j][None, None, :]
    return out

def block_diag_linear(x, w, b):
    B, T, _ = x.shape
    xb = x.reshape(B, T, LRU_BLOCKS, LRU_BLOCK_DIM)
    y = jnp.einsum('btni,nio->btno', xb, w) + b[None, None]
    return y.reshape(B, T, LRU_WIDTH)

def rg_lru(x, gate_a_w, gate_a_b, gate_x_w, gate_x_b, lru_lambda):
    r = jax.nn.sigmoid(block_diag_linear(x, gate_a_w, gate_a_b))
    i = jax.nn.sigmoid(block_diag_linear(x, gate_x_w, gate_x_b))
    log_a = -LRU_C * r * jax.nn.softplus(-lru_lambda)[None, None, :]
    a = jnp.exp(log_a)
    mult = jnp.sqrt(jnp.maximum(1.0 - jnp.exp(2.0 * log_a), 0.0))
    b = mult * (i * x)

    def combine(left, right):
        a_l, b_l = left
        a_r, b_r = right
        return a_l * a_r, a_r * b_l + b_r

    _, h = lax.associative_scan(combine, (a, b), axis=1)
    return h

def second_inputs(seed: int = 0) -> dict:
    key = jax.random.key(seed)
    ks = jax.random.split(key, 14)
    f32 = jnp.float32
    x = jax.random.normal(ks[0], (BATCH, SEQ, D_MODEL), f32)
    norm_in_g = 1.0 + 0.05 * jax.random.normal(ks[1], (D_MODEL,), f32)
    w_in = jax.random.normal(ks[2], (D_MODEL, IN_WIDTH), f32) * D_MODEL ** -0.5
    conv_w = jax.random.normal(ks[3], (CONV_WIDTH_2, LRU_WIDTH), f32) * CONV_WIDTH_2 ** -0.5
    conv_b = 0.01 * jax.random.normal(ks[4], (LRU_WIDTH,), f32)
    gate_a_w = jax.random.normal(ks[5], (LRU_BLOCKS, LRU_BLOCK_DIM, LRU_BLOCK_DIM), f32) * LRU_BLOCK_DIM ** -0.5
    gate_a_b = 0.01 * jax.random.normal(ks[6], (LRU_BLOCKS, LRU_BLOCK_DIM), f32)
    gate_x_w = jax.random.normal(ks[7], (LRU_BLOCKS, LRU_BLOCK_DIM, LRU_BLOCK_DIM), f32) * LRU_BLOCK_DIM ** -0.5
    gate_x_b = 0.01 * jax.random.normal(ks[8], (LRU_BLOCKS, LRU_BLOCK_DIM), f32)
    a_c = jax.random.uniform(ks[9], (LRU_WIDTH,), f32, minval=0.9, maxval=0.999)
    a0 = a_c ** (1.0 / LRU_C)
    lru_lambda = jnp.log(a0) - jnp.log1p(-a0)
    w_out = jax.random.normal(ks[10], (MIX_WIDTH, D_MODEL), f32) * MIX_WIDTH ** -0.5
    norm_out_g = 1.0 + 0.05 * jax.random.normal(ks[11], (D_MODEL,), f32)
    return {"x": x, "norm_in_g": norm_in_g, "w_in": w_in, "conv_w": conv_w, "conv_b": conv_b,
            "gate_a_w": gate_a_w, "gate_a_b": gate_a_b, "gate_x_w": gate_x_w, "gate_x_b": gate_x_b,
            "lru_lambda": lru_lambda, "w_out": w_out, "norm_out_g": norm_out_g}

def second_block(x, norm_in_g, w_in, conv_w, conv_b, gate_a_w, gate_a_b, gate_x_w, gate_x_b,
              lru_lambda, w_out, norm_out_g):
    B, T, _ = x.shape
    f32 = jnp.float32
    h = x
    for _layer in range(DEPTH):
        xn = rms_norm(h, norm_in_g)
        proj = jnp.einsum('btd,de->bte', xn, w_in).astype(f32)
        q, k, v, g_ret, x_lru, g_lru = jnp.split(proj, IN_SPLITS, axis=-1)

        q = rotary(q.reshape(B, T, RET_HEADS, RET_HEAD_DIM))
        k = rotary(k.reshape(B, T, RET_HEADS, RET_HEAD_DIM)) * RET_HEAD_DIM ** -0.5
        v = v.reshape(B, T, RET_HEADS, RET_HEAD_DIM)
        o_ret = group_norm_heads(chunkwise_retention(q, k, v)).reshape(B, T, RET_WIDTH)
        y_ret = o_ret * jax.nn.silu(g_ret)

        xc = causal_depthwise_conv(x_lru, conv_w.astype(f32), conv_b.astype(f32))
        o_lru = rg_lru(xc, gate_a_w.astype(f32), gate_a_b.astype(f32), gate_x_w.astype(f32),
                       gate_x_b.astype(f32), lru_lambda.astype(f32))
        y_lru = o_lru * jax.nn.silu(g_lru)

        mixed = jnp.concatenate([y_ret, y_lru], axis=-1).astype(x.dtype)
        h = h + jnp.einsum('bte,ed->btd', mixed, w_out)
    return rms_norm(h, norm_out_g)


DEPTH_3 = 2

N_MIXERS = 2
EXPAND = 2
D_INNER = EXPAND * D_MODEL
EPS = 1e-6
GLA_HEADS = 4
GLA_KEY_DIM = D_MODEL // 2
GLA_DK = GLA_KEY_DIM // GLA_HEADS
GLA_DV = D_INNER // GLA_HEADS
GLA_GATE_RANK = 16
GLA_GATE_TAU = 16.0
GLA_CHUNK = 64
GLA_IN = 2 * GLA_KEY_DIM + 2 * D_INNER + GLA_GATE_RANK
S5_GROUP = 16
S5_GROUPS = D_INNER // S5_GROUP
S5_STATE = 64
S5_DT_MIN = 1e-3
S5_DT_MAX = 1e-1
S5_IN = 2 * D_INNER
N_GLA = (DEPTH_3 + 1) // 2
N_S5 = DEPTH_3 // 2


def _rmsnorm(x, g):
    x32 = x.astype(jnp.float32)
    y = x32 * lax.rsqrt(jnp.mean(x32 * x32, axis=-1, keepdims=True) + EPS) * g.astype(jnp.float32)
    return y.astype(x.dtype)

def _gla_mixer(h, w_in, w_gate_up, b_gate, head_gain, w_out):
    bsz, seqlen, _ = h.shape
    n_chunks = seqlen // GLA_CHUNK
    f32 = jnp.float32
    proj = h @ w_in
    q, k, v, z, r = jnp.split(
        proj,
        [GLA_KEY_DIM, 2 * GLA_KEY_DIM, 2 * GLA_KEY_DIM + D_INNER, 2 * GLA_KEY_DIM + 2 * D_INNER],
        axis=-1)
    log_a = jax.nn.log_sigmoid((r @ w_gate_up + b_gate).astype(f32)) / GLA_GATE_TAU

    def to_chunks(t, d):
        return t.astype(f32).reshape(bsz, n_chunks, GLA_CHUNK, GLA_HEADS, d).transpose(0, 3, 1, 2, 4)

    qc = to_chunks(q, GLA_DK) * (GLA_DK ** -0.5)
    kc = to_chunks(k, GLA_DK)
    vc = to_chunks(v, GLA_DV)
    bcum = jnp.cumsum(to_chunks(log_a, GLA_DK), axis=3)
    b_last = bcum[:, :, :, -1:, :]

    q_g = qc * jnp.exp(bcum)
    k_g = kc * jnp.exp(-bcum)
    k_end = kc * jnp.exp(b_last - bcum)

    causal = jnp.tril(jnp.ones((GLA_CHUNK, GLA_CHUNK), dtype=bool))
    att = jnp.einsum('bhncd,bhnsd->bhncs', q_g, k_g)
    att = jnp.where(causal, att, 0.0)
    o_intra = jnp.einsum('bhncs,bhnse->bhnce', att, vc)

    kv_chunk = jnp.einsum('bhnsd,bhnse->bhnde', k_end, vc)
    decay_chunk = jnp.exp(b_last[:, :, :, 0, :])

    def step(state, inp):
        dec, kv = inp
        return dec[..., None] * state + kv, state

    s0 = jnp.zeros((bsz, GLA_HEADS, GLA_DK, GLA_DV), f32)
    _, s_prev = lax.scan(step, s0, (jnp.moveaxis(decay_chunk, 2, 0), jnp.moveaxis(kv_chunk, 2, 0)))
    s_prev = jnp.moveaxis(s_prev, 0, 2)
    o = o_intra + jnp.einsum('bhncd,bhnde->bhnce', q_g, s_prev)

    o = o.transpose(0, 2, 3, 1, 4).reshape(bsz, seqlen, GLA_HEADS, GLA_DV)
    o = o * lax.rsqrt(jnp.mean(o * o, axis=-1, keepdims=True) + EPS) * head_gain.astype(f32)
    o = o.reshape(bsz, seqlen, D_INNER) * jax.nn.silu(z.astype(f32))
    return o.astype(h.dtype) @ w_out

def _s5_mixer(h, w_in, lam_re, lam_im, log_dt, b_re, b_im, c_re, c_im, d_skip, w_glu, b_glu, w_out):
    bsz, seqlen, _ = h.shape
    f32 = jnp.float32
    proj = h @ w_in
    u, z = jnp.split(proj, [D_INNER], axis=-1)
    u32 = u.astype(f32).reshape(bsz, seqlen, S5_GROUPS, S5_GROUP)

    lam = lax.complex(lam_re.astype(f32), lam_im.astype(f32))
    dt = jnp.exp(log_dt.astype(f32))[:, None]
    lam_bar = jnp.exp(lam * dt)
    b_coef = (lam_bar - 1.0) / lam
    b_cplx = lax.complex(b_re.astype(f32), b_im.astype(f32))
    b_bar = b_coef[..., None] * b_cplx
    bu = lax.complex(jnp.einsum('blgi,gpi->blgp', u32, jnp.real(b_bar)),
                     jnp.einsum('blgi,gpi->blgp', u32, jnp.imag(b_bar)))
    a = jnp.broadcast_to(lam_bar[None, None], (1, seqlen, S5_GROUPS, S5_STATE))

    def combine(left, right):
        a_l, b_l = left
        a_r, b_r = right
        return a_l * a_r, a_r * b_l + b_r

    _, states = lax.associative_scan(combine, (a, bu), axis=1)
    y = (jnp.einsum('blgp,gip->blgi', jnp.real(states), c_re.astype(f32))
         - jnp.einsum('blgp,gip->blgi', jnp.imag(states), c_im.astype(f32)))
    y = y + d_skip.astype(f32) * u32
    y = jax.nn.gelu(y.reshape(bsz, seqlen, D_INNER))
    y = y * jax.nn.sigmoid(y @ w_glu.astype(f32) + b_glu.astype(f32))
    y = y * jax.nn.silu(z.astype(f32))
    return y.astype(h.dtype) @ w_out

def third_inputs(seed: int = 0) -> dict:
    key = jax.random.key(seed)
    ks = jax.random.split(key, 24)
    nrm = jax.random.normal
    f32 = jnp.float32
    x = nrm(ks[0], (BATCH, SEQ, D_MODEL), f32)
    gla_norm = 1.0 + 0.01 * nrm(ks[1], (N_GLA, D_MODEL), f32)
    gla_w_in = nrm(ks[2], (N_GLA, D_MODEL, GLA_IN), f32) * D_MODEL ** -0.5
    gla_w_gate_up = nrm(ks[3], (N_GLA, GLA_GATE_RANK, GLA_KEY_DIM), f32) * GLA_GATE_RANK ** -0.5
    gla_b_gate = 0.1 * nrm(ks[4], (N_GLA, GLA_KEY_DIM), f32)
    gla_head_gain = 1.0 + 0.01 * nrm(ks[5], (N_GLA, GLA_DV), f32)
    gla_w_out = nrm(ks[6], (N_GLA, D_INNER, D_MODEL), f32) * D_INNER ** -0.5
    s5_norm = 1.0 + 0.01 * nrm(ks[7], (N_S5, D_MODEL), f32)
    s5_w_in = nrm(ks[8], (N_S5, D_MODEL, S5_IN), f32) * D_MODEL ** -0.5
    s5_lam_re = -0.5 + 1e-3 * nrm(ks[9], (N_S5, S5_GROUPS, S5_STATE), f32)
    s5_lam_im = (math.pi * jnp.arange(S5_STATE, dtype=f32))[None, None, :] \
        + 1e-3 * nrm(ks[10], (N_S5, S5_GROUPS, S5_STATE), f32)
    s5_log_dt = jax.random.uniform(ks[11], (N_S5, S5_GROUPS), f32,
                                   minval=math.log(S5_DT_MIN), maxval=math.log(S5_DT_MAX))
    s5_b_re = nrm(ks[12], (N_S5, S5_GROUPS, S5_STATE, S5_GROUP), f32) * (2 * S5_GROUP) ** -0.5
    s5_b_im = nrm(ks[13], (N_S5, S5_GROUPS, S5_STATE, S5_GROUP), f32) * (2 * S5_GROUP) ** -0.5
    s5_c_re = nrm(ks[14], (N_S5, S5_GROUPS, S5_GROUP, S5_STATE), f32) * S5_STATE ** -0.5
    s5_c_im = nrm(ks[15], (N_S5, S5_GROUPS, S5_GROUP, S5_STATE), f32) * S5_STATE ** -0.5
    s5_d = nrm(ks[16], (N_S5, S5_GROUPS, S5_GROUP), f32)
    s5_w_glu = nrm(ks[17], (N_S5, D_INNER, D_INNER), f32) * D_INNER ** -0.5
    s5_b_glu = 0.01 * nrm(ks[18], (N_S5, D_INNER), f32)
    s5_w_out = nrm(ks[19], (N_S5, D_INNER, D_MODEL), f32) * D_INNER ** -0.5
    final_norm = 1.0 + 0.01 * nrm(ks[20], (D_MODEL,), f32)
    return {
        "x": x,
        "gla_norm": gla_norm, "gla_w_in": gla_w_in, "gla_w_gate_up": gla_w_gate_up,
        "gla_b_gate": gla_b_gate, "gla_head_gain": gla_head_gain, "gla_w_out": gla_w_out,
        "s5_norm": s5_norm, "s5_w_in": s5_w_in, "s5_lam_re": s5_lam_re, "s5_lam_im": s5_lam_im,
        "s5_log_dt": s5_log_dt, "s5_b_re": s5_b_re, "s5_b_im": s5_b_im,
        "s5_c_re": s5_c_re, "s5_c_im": s5_c_im, "s5_d": s5_d,
        "s5_w_glu": s5_w_glu, "s5_b_glu": s5_b_glu, "s5_w_out": s5_w_out,
        "final_norm": final_norm,
    }

def third_block(x, gla_norm, gla_w_in, gla_w_gate_up, gla_b_gate, gla_head_gain, gla_w_out,
              s5_norm, s5_w_in, s5_lam_re, s5_lam_im, s5_log_dt, s5_b_re, s5_b_im,
              s5_c_re, s5_c_im, s5_d, s5_w_glu, s5_b_glu, s5_w_out, final_norm):
    for i in range(DEPTH_3):
        j = i // N_MIXERS
        if i % N_MIXERS == 0:
            h = _rmsnorm(x, gla_norm[j])
            out = _gla_mixer(h, gla_w_in[j], gla_w_gate_up[j], gla_b_gate[j],
                             gla_head_gain[j], gla_w_out[j])
        else:
            h = _rmsnorm(x, s5_norm[j])
            out = _s5_mixer(h, s5_w_in[j], s5_lam_re[j], s5_lam_im[j], s5_log_dt[j],
                            s5_b_re[j], s5_b_im[j], s5_c_re[j], s5_c_im[j], s5_d[j],
                            s5_w_glu[j], s5_b_glu[j], s5_w_out[j])
        x = x + out.astype(x.dtype)
    return _rmsnorm(x, final_norm)


def setup_inputs(seed=0):
    out = dict(first_inputs(seed))
    for name, value in second_inputs(seed + 1).items():
        if name != "x":
            out[name + "_2"] = value
    for name, value in third_inputs(seed + 2).items():
        if name != "x":
            out[name + "_3"] = value
    return out


def reference(
    x, c, w_mod, b_mod, w_in, b_in, conv_w, conv_b, ln_a_g, ln_a_b, w_a, b_a, ln_v_g, ln_v_b,
    w_s, b_s, w_b, b_b, w_out, b_out, post1_g, post1_b, w_router, b_router, w_gu, b_gu, w_dn,
    b_dn, post2_g, post2_b, norm_in_g_2, w_in_2, conv_w_2, conv_b_2, gate_a_w_2, gate_a_b_2,
    gate_x_w_2, gate_x_b_2, lru_lambda_2, w_out_2, norm_out_g_2, gla_norm_3, gla_w_in_3,
    gla_w_gate_up_3, gla_b_gate_3, gla_head_gain_3, gla_w_out_3, s5_norm_3, s5_w_in_3,
    s5_lam_re_3, s5_lam_im_3, s5_log_dt_3, s5_b_re_3, s5_b_im_3, s5_c_re_3, s5_c_im_3, s5_d_3,
    s5_w_glu_3, s5_b_glu_3, s5_w_out_3, final_norm_3,
):
    x = first_block(
        x, c, w_mod, b_mod, w_in, b_in, conv_w, conv_b, ln_a_g, ln_a_b, w_a, b_a, ln_v_g,
        ln_v_b, w_s, b_s, w_b, b_b, w_out, b_out, post1_g, post1_b, w_router, b_router, w_gu,
        b_gu, w_dn, b_dn, post2_g, post2_b,
    )
    x = second_block(
        x, norm_in_g_2, w_in_2, conv_w_2, conv_b_2, gate_a_w_2, gate_a_b_2, gate_x_w_2,
        gate_x_b_2, lru_lambda_2, w_out_2, norm_out_g_2,
    )
    return third_block(
        x, gla_norm_3, gla_w_in_3, gla_w_gate_up_3, gla_b_gate_3, gla_head_gain_3, gla_w_out_3,
        s5_norm_3, s5_w_in_3, s5_lam_re_3, s5_lam_im_3, s5_log_dt_3, s5_b_re_3, s5_b_im_3,
        s5_c_re_3, s5_c_im_3, s5_d_3, s5_w_glu_3, s5_b_glu_3, s5_w_out_3, final_norm_3,
    )


_drawn_inputs = setup_inputs


def setup_inputs(seed=0):
    import zlib

    import numpy as np

    out = dict(_drawn_inputs(seed))
    spreads = {}
    factors = {'b_in': 6.262,
     'conv_b': 8.0,
     'ln_a_g': 7.749,
     'ln_a_b': 8.0,
     'b_a': 8.0,
     'ln_v_g': 8.0,
     'ln_v_b': 8.0,
     'b_s': 4.489,
     'b_b': 8.0,
     'b_out': 3.607,
     'b_router': 7.708,
     'b_gu': 5.667,
     'b_dn': 8.0,
     'conv_b_2': 2.85,
     'gate_a_b_2': 33.825,
     'gate_x_b_2': 8.0,
     'gla_norm_3': 5.39,
     'gla_head_gain_3': 37.019,
     's5_norm_3': 48.888,
     's5_lam_re_3': 64.0,
     's5_lam_im_3': 32.232,
     's5_log_dt_3': 32.832,
     's5_b_re_3': 45.808,
     's5_b_im_3': 45.088,
     's5_c_re_3': 44.368,
     's5_c_im_3': 45.592,
     's5_b_glu_3': 59.282,
     'final_norm_3': 30.79}
    for name, (base, spread) in spreads.items():
        noise = np.random.default_rng([zlib.crc32(name.encode()), seed]).standard_normal(out[name].shape)
        drawn = base * np.exp(spread * noise) if base else spread * noise
        out[name] = __import__('jax').numpy.asarray(drawn.astype(out[name].dtype))
    for name, factor in factors.items():
        out[name] = (out[name] * factor).astype(out[name].dtype)
    return out
```

```python
from contextlib import ExitStack

import numpy as np

import concourse.bass as bass
from concourse import mybir

F32 = mybir.dt.float32
I32 = mybir.dt.int32
U32 = mybir.dt.uint32
ALU = mybir.AluOpType
ACT = mybir.ActivationFunctionType

P = 128
T = 256
TT = T // P
D = 1024
KT = D // P
CH = 512
RING = 6
NV = 2
ROW = TT * D

CONV1, CONV2 = 31, 4
NE, TOPK = 32, 4
BLK = 64
ALPHA = float(2 ** 0.25)
LN_EPS, RMS_EPS = 1e-5, 1e-6
GLA_H, GLA_DK, GLA_DV, GLA_C, GLA_R = 4, 128, 512, 64, 16
GLA_TAU = 16.0
S5_CT, S5_P, S5_I = 16, 64, 16
PAIRS = 4
MAGIC = 12582912.0
TWO_PI = 6.283185
INV_2PI = 0.15915494309189535
HALF_PI = 1.5707963

C_ID, C_TRI, C_SLOT, C_E, C_T = 0, 128, 256, 256 + 4 * P, 256 + 4 * P + NE
C_N = C_T + T
R_C, R_AV, R_AG, R_CB, R_BS = 0, 8, 16, 24, 32
R_CW2, R_CB2, R_GAB, R_GXB, R_LAM, R_BG, R_GLU = 40, 72, 80, 88, 96, 104, 108
R_N0 = 124
N_PARAM = 18


def constants():
    c = np.zeros((P, C_N), np.float32)
    c[:, C_ID:C_ID + P] = np.eye(P)
    c[:, C_TRI:C_TRI + P] = np.triu(np.ones((P, P)), 1)
    c[:, C_SLOT:C_SLOT + 4 * P] = (np.arange(4)[:, None] * BLK + np.arange(P) % BLK).reshape(-1)
    c[:, C_E:C_E + NE] = np.arange(NE)
    c[:, C_T:C_T + T] = np.arange(T)
    half = P // 2
    inv = 10000.0 ** (-np.arange(0, P, 2, dtype=np.float32) / P)
    ang = np.arange(T, dtype=np.float32)[:, None] * inv[None, :].astype(np.float32)
    rot = np.concatenate([np.cos(ang), np.sin(ang)], 1).astype(np.float32)
    log_g = np.log1p(-np.exp2(-5.0 - np.arange(8, dtype=np.float64)))
    k = np.arange(P)[:, None]
    q = np.arange(T)[None, :]
    dec = np.zeros((P, 8, T + P))
    for h in range(8):
        full = np.where(q >= k, np.exp(np.maximum(q - k, 0) * log_g[h]), 0.0) * P ** -0.5
        dec[:, h, 0:T] = full
        dec[:, h, T:] = full[:, 0:P]
    s = np.arange(P)[:, None] % GLA_C
    m = (np.arange(GLA_C)[None, :] >= s).astype(np.int32)
    seg = (np.arange(T) % GLA_C != 0).astype(np.float32)
    seg = np.broadcast_to(seg, (P, T)).copy()
    assert half == 64
    return {"k_const": c, "k_rot": rot, "k_decay": dec.astype(np.float32).reshape(P, -1),
            "k_causal": np.ascontiguousarray(m), "k_seg": seg}


def plan():
    units = []

    def add(name, kind, mat, cols, rows=1):
        units.append((name, kind, [(mat, r * D, c) for c in cols for r in range(rows)]))

    def mod(name, i):
        add(name, "mod", "w_mod", [i * D, i * D + CH])

    mod("sc1", 1)
    mod("sh1", 0)
    for i in range(2):
        add(f"ag{i}", "col", "w_in", [D + i * CH])
        add(f"av{i}", "col", "w_in", [i * CH])
    for n, base in (("v", 3), ("u", 2), ("ga", 4), ("gb", 5)):
        for i in range(2):
            add(f"{n}{i}", "row", "w_in", [base * D + i * CH])
    for n, m in (("wb", "w_b"), ("wa", "w_a")):
        for i in range(2):
            add(f"{n}{i}", "row", m, [i * CH])
    mod("g1", 2)
    for i in range(2):
        add(f"wo{i}", "row", "w_out", [i * CH])
    mod("sc2", 4)
    mod("sh2", 3)
    mod("g2", 5)
    units.append(("moe", "moe", []))
    for n, base in (("xl", 4), ("gl", 5)):
        for i in range(2):
            add(f"{n}{i}", "col", "w_in_2", [base * D + i * CH])
    for n, base in (("q2", 0), ("k2", 1), ("v2", 2), ("gr", 3)):
        for i in range(2):
            add(f"{n}{i}", "row", "w_in_2", [base * D + i * CH])
    for i in range(2):
        add(f"w2o{i}", "row", "w_out_2", [i * CH], rows=2)
    add("gq", "col", "gla_w_in_3", [0])
    add("gk", "col", "gla_w_in_3", [CH])
    for i in range(4):
        add(f"gv{i}", "row", "gla_w_in_3", [D + i * CH])
    for i in range(4):
        add(f"gz{i}", "row", "gla_w_in_3", [3 * D + i * CH])
    for i in range(2):
        add(f"go{i}", "row", "gla_w_out_3", [i * CH], rows=2)
    for i in range(4):
        add(f"su{i}", "col", "s5_w_in_3", [i * CH])
    for i in range(4):
        add(f"sz{i}", "col", "s5_w_in_3", [2 * D + i * CH])
    for i in range(4):
        add(f"sg{i}", "col", "s5_w_glu_3", [i * CH], rows=2)
    for i in range(2):
        add(f"so{i}", "row", "s5_w_out_3", [i * CH], rows=2)
    return units


TRANSPOSES = [("params", 2), ("ws", 2), ("h1", 4), ("conv", 4), ("yb", 4), ("ya", 4), ("m", 4), ("h2", 4),
              ("xn", 4), ("q", 4), ("k", 4), ("yr", 4), ("hg", 4), ("kend", 2), ("og", 8), ("hs", 4)]

VECTORS = [("b_mod", D, D), ("b_mod", 0, D),
           ("b_in", 3 * D, D), ("b_in", 2 * D, D), ("b_in", 4 * D, D), ("b_in", 5 * D, D),
           ("ln_v_g", 0, D), ("ln_v_b", 0, D), ("b_b", 0, D), ("ln_a_g", 0, D), ("ln_a_b", 0, D), ("b_a", 0, D),
           ("b_mod", 2 * D, D), ("b_out", 0, D), ("post1_g", 0, D), ("post1_b", 0, D),
           ("b_mod", 4 * D, D), ("b_mod", 3 * D, D), ("b_mod", 5 * D, D),
           ("post2_g", 0, D), ("post2_b", 0, D), ("norm_in_g_2", 0, D), ("norm_out_g_2", 0, D),
           ("gla_norm_3", 0, D), ("gla_head_gain_3", 0, GLA_DV), ("s5_norm_3", 0, D), ("final_norm_3", 0, D)]


def build(nc, A, out, upto=99):
    units = plan()
    if upto == 1:
        units = units[:[u[0] for u in units].index("moe") + 1]
    if upto == 3:
        units = units[:[u[0] for u in units].index("go1") + 1]
    if upto == 2:
        units = units[:[u[0] for u in units].index("w2o1") + 1]
    pre = sum(len(u[2]) for u in units[:[u[0] for u in units].index("moe")])
    assert pre % RING == 0
    UNIT, first_chunk, no, n = {}, {}, 0, 0
    for name, kind, chunks in units:
        if kind == "moe":
            n += 6 * NE
            continue
        UNIT[name] = (no, kind, chunks, n)
        no += 1
        n += len(chunks)
    TB, n = {}, 0
    for name, banks in TRANSPOSES:
        TB[name] = n
        n += banks

    mats = {k: A[k][0] for k in ("w_mod", "w_in", "w_b", "w_a", "w_out", "gla_w_in_3", "gla_w_out_3",
                                 "s5_w_in_3", "s5_w_glu_3", "s5_w_out_3")}
    mats["w_in_2"], mats["w_out_2"] = A["w_in_2"], A["w_out_2"]

    with ExitStack() as ctx:
        def sb(name, shape, dt=F32):
            return ctx.enter_context(nc.sbuf_tensor(name, shape, dt))

        def sem(name):
            return ctx.enter_context(nc.semaphore(name))

        W = sb("W", [P, RING, KT, CH])
        V = sb("V", [P, NV, D])
        BIG = sb("BIG", [P, 10 * ROW])
        X = sb("X", [P, TT, D])[:]
        K = sb("K", [P, C_N])
        PC = sb("PC", [P, 5, P])
        ST = sb("ST", [P, TT, 12])
        MV = sb("MV", [P, TT, 2])
        VE = sb("VE", [P, TT])
        SD = sb("SD", [P, TT])
        RS = sb("RS", [P, TT])
        HST = sb("HST", [P, 16, 6])
        HMV = sb("HMV", [P, 16, 2])
        HVE = sb("HVE", [P, 16])
        HSD = sb("HSD", [P, 16])
        HRS = sb("HRS", [P, 16])
        ONES = sb("ONES", [P, P])
        TAB2 = sb("TAB2", [P, D])
        CTW = sb("CTW", [P, 3, PAIRS, 2, S5_I])
        LS = sb("LS", [P, 6, KT])
        WGR = sb("WGR", [P, KT, GLA_R])
        MASK = sb("MASK", [P, GLA_C], I32)
        DC4 = sb("DC4", [P, GLA_H, T // GLA_C])
        PS = ctx.enter_context(nc.psum_tensor("PS", [P, 8, CH], F32))

        def flat(i, n=1):
            return BIG[:, i * ROW:(i + n) * ROW]

        def row(i):
            return flat(i).rearrange("p (t d) -> p t d", t=TT)

        def col(i, n=1):
            return flat(i, n).rearrange("p (k t) -> p k t", t=T)

        def half(i, h):
            return BIG[:, i * ROW + h * D:i * ROW + (h + 1) * D]

        ident = K[:, C_ID:C_ID + P]

        def pcol(r, n=1):
            return PC[:, r // P, r % P:r % P + n]

        x_landed, const_landed, param_landed = sem("x_landed"), sem("const_landed"), sem("param_landed")
        w_landed = [sem(f"w_landed{i}") for i in range(RING)]
        v_landed = [sem(f"v_landed{i}") for i in range(NV)]
        v_used = sem("v_used")
        chunk_done = sem("chunk_done")
        unit_free = [sem("unit_free0"), sem("unit_free1")]
        tp_ready, tp_copied = sem("tp_ready"), sem("tp_copied")
        var_ready, std_ready = sem("var_ready"), sem("std_ready")
        S = {}

        def ev(name):
            if name not in S:
                S[name] = sem(name)
            return S[name]

        block = ctx.enter_context(nc.Block())

        def slot(n):
            return W[:, n % RING]

        def unit_ps(name):
            u = UNIT[name][0]
            return PS[:, 2 * (u % 2):2 * (u % 2) + 2, :]

        def wait_unit(eng, name):
            _, _, chunks, c0 = UNIT[name]
            eng.wait_ge(chunk_done, c0 + len(chunks))

        def free_unit(ins, name):
            ins.then_inc(unit_free[UNIT[name][0] % 2], 1)

        vec_at = [0]

        def vector(dve, name):
            n = vec_at[0]
            assert VECTORS[n][0] == name, (VECTORS[n], name)
            vec_at[0] += 1
            dve.wait_ge(v_landed[n % NV], 16 * (n // NV + 1))
            return V[:, n % NV, 0:VECTORS[n][2]]

        def bt(v):
            return v.unsqueeze(1).to_broadcast([P, TT, v.shape[1]])

        ln_no = [0, 0]

        def norm_stats(dve, src):
            for t in range(TT):
                for h in range(2):
                    dve.bn_stats(ST[:, t, 6 * h:6 * h + 6], src[:, t, h * CH:(h + 1) * CH])
            dve.drain()
            for t in range(TT):
                dve.bn_aggr(MV[:, t, :], ST[:, t, :])
            dve.drain()

        def layer_norm(dve, dst, src):
            norm_stats(dve, src)
            dve.tensor_scalar_add(VE[:], MV[:, :, 1], LN_EPS).then_inc(var_ready, 1)
            ln_no[0] += 1
            dve.wait_ge(std_ready, ln_no[0])
            dve.reciprocal(RS[:], SD[:])
            dve.drain()
            for t in range(TT):
                dve.tensor_scalar(dst[:, t, :], src[:, t, :], MV[:, t, 0:1], RS[:, t:t + 1],
                                  ALU.subtract, ALU.mult)
            dve.drain()

        def rms_norm(dve, dst, src, gain):
            norm_stats(dve, src)
            dve.tensor_tensor(VE[:], MV[:, :, 0], MV[:, :, 0], ALU.mult)
            dve.drain()
            dve.scalar_tensor_tensor(VE[:], VE[:], RMS_EPS, MV[:, :, 1], ALU.add, ALU.add).then_inc(var_ready, 1)
            ln_no[0] += 1
            dve.wait_ge(std_ready, ln_no[0])
            dve.reciprocal(RS[:], SD[:])
            dve.drain()
            for t in range(TT):
                ins = dve.scalar_tensor_tensor(dst[:, t, :], src[:, t, :], RS[:, t:t + 1], gain, ALU.mult, ALU.mult)
            return ins

        def act_std(act):
            ln_no[1] += 1
            act.wait_ge(var_ready, ln_no[1])
            act.activation(SD[:], VE[:], ACT.Sqrt).then_inc(std_ready, 1)

        def copy_columns(act, name, dst, kts=KT):
            per = kts // 4
            for b in range(TT * per):
                t, h = b // per, b % per
                act.wait_ge(tp_ready, TB[name] + b + 1)
                act.activation(dst[:, 4 * h:4 * h + 4, t * P:(t + 1) * P],
                               PS[:, 4 + (TB[name] + b) % 2, :].rearrange("p (k t) -> p k t", k=4),
                               ACT.Copy).then_inc(tp_copied, 1)

        @block.sync
        def _(sp):
            sp.dma_start(K[:], A["k_const"]).then_inc(const_landed, 16)
            sp.dma_start(X, A["x"][0].rearrange("(t p) d -> p t d", p=P)).then_inc(x_landed, 16)
            for name, kind, chunks in units:
                if kind == "moe":
                    with sp.Fori(0, NE) as e:
                        gu = A["w_gu"][0, bass.ds(e, 1)].rearrange("e (k p) n -> p (e k) n", p=P)
                        dn = A["w_dn"][0, bass.ds(e, 1)].rearrange("e (k p) n -> p (e k) n", p=P)
                        for j in range(6):
                            sp.wait_ge(chunk_done, e * 6 + (pre + j - RING + 1))
                            src = gu[:, :, j * CH:(j + 1) * CH] if j < 4 else dn[:, :, (j - 4) * CH:(j - 3) * CH]
                            sp.dma_start(W[:, j], src).then_inc(w_landed[j], 16)
                    continue
                c0 = UNIT[name][3]
                for i, (mat, r, c) in enumerate(chunks):
                    n = c0 + i
                    if n >= RING:
                        sp.wait_ge(chunk_done, n - RING + 1)
                    sp.dma_start(slot(n), mats[mat][r:r + D, c:c + CH].rearrange("(k p) n -> p k n", p=P)) \
                        .then_inc(w_landed[n % RING], 16)
            sp.wait_ge(ev("result_ready"), 1)
            sp.dma_start(out[0].rearrange("(t p) d -> p t d", p=P), X).then_inc(ev("result_stored"), 16)
            sp.wait_ge(ev("result_stored"), 16)

        HT, HT2, HN, AUX, CV, U, VV, GA, GB = 0, 1, 2, 3, 4, 5, 6, 7, 8
        WST = half(AUX, 0).rearrange("p (g i) -> p g i", g=8)
        CB = half(AUX, 1).rearrange("p (k m) -> p k m", k=KT)
        WSR = half(GB, 0).rearrange("p (g i) -> p g i", g=8)
        PVR = BIG[:, CV * ROW:CV * ROW + 5 * P].rearrange("p (a b) -> p a b", a=5)
        LDT = BIG[:, CV * ROW + 5 * P:CV * ROW + 5 * P + 2]
        MA, MB = half(9, 0), half(9, 1)
        H2, H2T, YACC = row(0), col(1), row(2)
        BGU = BIG[0:NE, 4 * ROW:5 * ROW]
        E5 = 5 * ROW
        XET = BIG[:, E5:E5 + 512].rearrange("p (k s) -> p k s", k=KT)
        ACTT = BIG[:, E5 + 512:E5 + 1024].rearrange("p (k s) -> p k s", k=KT)
        YE = BIG[:, E5 + 1024:E5 + 1536]
        G = BIG[:, E5 + 1536:E5 + 1664].rearrange("p (t s) -> p t s", t=TT)
        GW = BIG[:, E5 + 1664:E5 + 1920].rearrange("p (t s) -> p t s", t=TT)
        SELB = BIG[0:NE, E5 + 1920:E5 + 1984]
        E6 = 6 * ROW
        GT, SG, UP = (BIG[:, E6 + i * 512:E6 + (i + 1) * 512] for i in range(3))
        SC = BIG[:, E6 + 1536:E6 + 1792]
        WR = BIG[:, E6 + 1792:E6 + 2048].rearrange("p (k e) -> p k e", k=KT)
        BDN = BIG[0:NE, 7 * ROW:7 * ROW + D]
        E7 = 7 * ROW + D

        def small(i, n=NE, tt=TT):
            return BIG[:, E7 + 64 * i:E7 + 64 * i + n * tt].rearrange("p (t e) -> p t e", t=tt)
        LG, SEL, WM, POS, OH, BRT = (small(i) for i in range(6))
        SUMS, PW, V8, F8 = small(6), small(7, 2, 2), small(8, 8), small(9, 8)
        I8 = BIG[:, E7 + 640:E7 + 656].rearrange("p (t e) -> p t e", t=TT).bitcast(U32)
        NM, ES, ER = (BIG[:, E7 + 660 + 4 * i:E7 + 662 + 4 * i] for i in range(3))
        E4 = small(11, 4)
        TABF = BIG[0:1, E7 + 768:E7 + 768 + 3 * NE].rearrange("p (a e) -> p a e", a=3)
        TABI = BIG[0:1, E7 + 896:E7 + 896 + 2 * NE].rearrange("p (a e) -> p a e", a=2).bitcast(I32)
        WMT = BIG[0:NE, 8 * ROW:8 * ROW + T].rearrange("p (t s) -> p t s", t=TT)
        XC, R2, I2, QT, GLC = col(8), col(9), col(1), col(1), col(7)
        XLC, Q2, K2, V2 = col(5), row(2), row(3), row(4)
        GW2 = BIG[:, 6 * ROW:7 * ROW].rearrange("p (a n o) -> p a n o", a=2, n=8)
        KT2, GR, O2, YRT = col(8), row(5), row(0), col(3)
        DEC = BIG[:, 6 * ROW:6 * ROW + 8 * 384].rearrange("p (h q) -> p h q", h=8)
        SCT = BIG[:, 6 * ROW + 3072:6 * ROW + 3072 + 768].rearrange("p (b q) -> p b q", b=2)
        GQ = BIG[:, ROW:ROW + D].rearrange("p (h t) -> p h t", h=4)
        GK = BIG[:, ROW + D:2 * ROW].rearrange("p (h t) -> p h t", h=4)
        GV = BIG[:, 2 * ROW:4 * ROW].rearrange("p (t d) -> p t d", t=TT)
        GZ = BIG[:, 4 * ROW:6 * ROW].rearrange("p (t d) -> p t d", t=TT)
        LA = half(6, 0).rearrange("p (h t) -> p h t", h=4)
        BC = half(6, 1).rearrange("p (h t) -> p h t", h=4)
        TE = half(7, 0).rearrange("p (h t) -> p h t", h=4)
        KE = half(7, 1).rearrange("p (h t) -> p h t", h=4)
        KR = half(8, 0).rearrange("p (t f) -> p t f", t=TT)
        ATT = BIG[:, 8 * ROW + D:8 * ROW + D + 512].rearrange("p (t h c) -> p t h c", t=TT, h=4)
        GS = BIG[:, 9 * ROW:10 * ROW].rearrange("p (h e) -> p h e", h=4)
        OG = [BIG[:, 0:ROW], BIG[:, ROW:2 * ROW]]
        OGT = BIG[:, 2 * ROW:4 * ROW].rearrange("p (k t) -> p k t", t=T)
        ROT = TAB2[:, 0:2 * P].rearrange("p (t c) -> p t c", t=TT)
        SEG = TAB2[:, 256:512]
        WGU = TAB2[0:GLA_R, 512:1024]
        RT = BIG[0:GLA_R, 7 * ROW:7 * ROW + T]
        U16, Z16, Y16 = col(1, 2), col(3, 2), col(5, 2)
        BB = BIG[:, 7 * ROW:8 * ROW].rearrange("p (a g i) -> p a g i", a=2, g=64)
        CC = BIG[:, 8 * ROW:9 * ROW].rearrange("p (a c q) -> p a c q", a=2, c=S5_CT)
        B9 = 9 * ROW

        def cell(i):
            return BIG[:, B9 + 64 * i:B9 + 64 * i + 64]
        TH, RR, CRE, CIM = (cell(i) for i in range(4))
        UC = BIG[:, B9 + 256:B9 + 512]
        BTW = BIG[:, B9 + 512:B9 + 768].rearrange("p (a m) -> p a m", a=2)
        TC = BIG[:, B9 + 768:B9 + 776].rearrange("p (a q) -> p a q", a=2)
        DCOL = BIG[:, B9 + 776:B9 + 777]
        BD = K[:, C_SLOT:C_SLOT + 256].rearrange("p (a q b i) -> p a q b i", a=2, q=PAIRS, b=2)
        CS = K[:, C_SLOT + 256:C_SLOT + 512].rearrange("p (a b q) -> p a b q", a=2, b=2)
        SA1, SA2, SCOS, SSIN, SB1, SB2 = (o.rearrange("p (q t) -> p q t", q=2) for o in
                                          [BIG[:, i * 512:(i + 1) * 512] for i in range(4)] +
                                          [BIG[:, B9 + D + i * 512:B9 + D + (i + 1) * 512] for i in range(2)])
        work = [BIG[:, i * 64:(i + 1) * 64] for i in range(16)]

        @block.gpsimd
        def _(pool):
            for n, (name, off, length) in enumerate(VECTORS[:{1: 21, 2: 23, 3: 25}.get(upto)]):
                src = A[name] if len(A[name].shape) == 1 else A[name][0]
                if n >= NV:
                    pool.wait_ge(v_used, n - NV + 1)
                pool.dma_start(V[:, n % NV, 0:length], src[off:off + length].unsqueeze(0).to_broadcast([P, length])) \
                    .then_inc(v_landed[n % NV], 16)
                if n == 16:
                    pool.wait_ge(ev("x1_ready"), 1)
                    pool.dma_start(BGU, A["b_gu"][0]).then_inc(ev("moe_small_landed"), 16)
                    pool.dma_start(BDN, A["b_dn"][0]).then_inc(ev("moe_small_landed"), 16)
                    pool.dma_start(WR, A["w_router"][0].rearrange("(k p) e -> p k e", p=P)).then_inc(ev("moe_small_landed"), 16)
                    pool.dma_start(BRT[:, 0, :], A["b_router"][0].unsqueeze(0).to_broadcast([P, NE])) \
                        .then_inc(ev("moe_small_landed"), 16)
                if n == 21:
                    pool.wait_ge(ev("block1_done"), 1)
                    for a, w in enumerate(("gate_a_w_2", "gate_x_w_2")):
                        pool.dma_start(GW2[:, a], A[w].rearrange("n i o -> i n o")).then_inc(ev("gate_w_landed"), 16)
                    pool.dma_start(ROT, A["k_rot"].rearrange("(t p) c -> p t c", p=P)).then_inc(ev("tables_landed"), 16)
                    pool.dma_start(SEG, A["k_seg"]).then_inc(ev("tables_landed"), 16)
                    pool.dma_start(WGU, A["gla_w_gate_up_3"][0]).then_inc(ev("tables_landed"), 16)
                    pool.dma_start(WGR[:], A["gla_w_in_3"][0][:, 5 * D:5 * D + GLA_R].rearrange("(k p) r -> p k r", p=P)) \
                        .then_inc(ev("tables_landed"), 16)
                    pool.dma_start(MASK[:], A["k_causal"]).then_inc(ev("tables_landed"), 16)
                if n == 22:
                    pool.wait_ge(ev("yl_ready"), 1)
                    pool.dma_start(DEC, A["k_decay"].rearrange("p (h q) -> p h q", h=8)).then_inc(ev("decay_landed"), 16)
                if n == 25:
                    pool.wait_ge(ev("og_ready"), 1)
                    for a, w in enumerate(("s5_b_re_3", "s5_b_im_3")):
                        for g in range(2):
                            pool.dma_start(BB[64 * g:64 * g + 64, a], A[w][0].rearrange("(a b) p i -> b p a i", b=2)[g]) \
                                .then_inc(ev("s5_bc_landed"), 16)
                    for a, w in enumerate(("s5_c_re_3", "s5_c_im_3")):
                        pool.dma_start(CC[:, a], A[w][0].rearrange("(c g) i q -> (g i) c q", g=8)).then_inc(ev("s5_bc_landed"), 16)
            if upto < 4:
                return
            pool.wait_ge(ev("coef_ready"), 1)
            pool.memset(K[:, C_SLOT:C_SLOT + 256], 0.0)
            pool.memset(CTW[:].rearrange("p a q b i -> p (a q b i)"), 0.0).then_inc(ev("zeroed"), 1)
            pool.wait_ge(ev("zeroed"), 1)
            with pool.Fori(0, S5_CT) as ct:
                pool.wait_ge(ev("s5_turned"), ct + 1)
                for a in range(2):
                    pool.tensor_copy(CS[:, a], CC[:, a, bass.ds(ct, 1), :].to_broadcast([P, 2, 64]))
                pool.wait_ge(ev("s5_gelu"), ct + 1)
                pool.tensor_copy(UC, U16[:, bass.ds(ct, 1), :].rearrange("p a t -> p (a t)"))
                pool.tensor_copy(TC[:, 0, :], TH[:, bass.ds(ct * PAIRS, PAIRS)])
                pool.tensor_copy(TC[:, 1, :], RR[:, bass.ds(ct * PAIRS, PAIRS)])
                pool.tensor_copy(DCOL, PC[:, 4, bass.ds(ct + 64, 1)]).then_inc(ev("s5_in_ready"), 1)

        @block.tensor
        def _(pe):
            def dense(name, lhs):
                u, kind, chunks, c0 = UNIT[name]
                ps = unit_ps(name)
                if u >= 2:
                    pe.wait_ge(unit_free[u % 2], u // 2)
                if kind == "col":
                    for i in range(len(chunks)):
                        pe.wait_ge(w_landed[(c0 + i) % RING], 16 * ((c0 + i) // RING + 1))
                    for m in range(4):
                        for i in range(len(chunks)):
                            for k in range(KT):
                                ins = pe.matmul(ps[:, m // 2, (m % 2) * T:(m % 2 + 1) * T],
                                                slot(c0 + i)[:, k, m * P:(m + 1) * P], lhs(i * KT + k), start=i + k == 0,
                                                stop=i == len(chunks) - 1 and k == KT - 1, skip_group_check=True)
                    ins.then_inc(chunk_done, len(chunks))
                    return
                for i in range(len(chunks)):
                    n = c0 + i
                    pe.wait_ge(w_landed[n % RING], 16 * (n // RING + 1))
                    w = slot(n)
                    last_chunk = i == len(chunks) - 1
                    if kind == "mod":
                        for k in range(KT):
                            ins = pe.matmul(ps[:, i, :], CB[:, k, :], w[:, k, :], start=k == 0, stop=k == KT - 1)
                    else:
                        for t in range(TT):
                            for k in range(KT):
                                ins = pe.matmul(ps[:, t, :], lhs(i * KT + k)[:, t * P:(t + 1) * P], w[:, k, :],
                                                start=i + k == 0, stop=last_chunk and k == KT - 1)
                    ins.then_inc(chunk_done, 1)

            def turn(name, tiles):
                for b, bank in enumerate(tiles):
                    n = TB[name] + b
                    if n >= 2:
                        pe.wait_ge(tp_copied, n - 1)
                    for j, a in enumerate(bank):
                        r, c = a.shape
                        ins = pe.transpose(PS[0:c, 4 + n % 2, j * P:j * P + r], a, ident[0:r, 0:r])
                    ins.then_inc(tp_ready, 1)

            def rows_to_columns(name, src, kts=KT):
                turn(name, [[src[t][:, (4 * h + j) * P:(4 * h + j + 1) * P] for j in range(4)]
                            for t in range(TT) for h in range(kts // 4)])

            def columns_ready(name):
                pe.wait_ge(tp_copied, TB[name] + dict(TRANSPOSES)[name])

            pe.wait_ge(const_landed, 16)
            pe.wait_ge(param_landed, 16 * N_PARAM)
            pe.wait_ge(ev("log_dt_ready"), 1)
            turn("params", [[PVR[0:R_N0, 0, :], PVR[:, 1, :], PVR[0:120, 2, :], PVR[:, 3, :]], [PVR[0:80, 4, :]]])
            pe.wait_ge(ev("ws_landed"), 16)
            turn("ws", [[WSR[:, 4 * b + j, :] for j in range(4)] for b in range(2)])
            pe.wait_ge(ev("cond_ready"), 1)
            dense("sc1", None)
            dense("sh1", None)
            pe.wait_ge(ev("h1_ready"), 1)
            h1 = row(HN)
            rows_to_columns("h1", [h1[:, 0], h1[:, 1]])
            columns_ready("h1")
            hT = col(HT)
            lhs = lambda k: hT[:, k, :]
            for i in range(2):
                dense(f"ag{i}", lhs)
                dense(f"av{i}", lhs)
            for n_ in ("v", "u", "ga", "gb"):
                for i in range(2):
                    dense(f"{n_}{i}", lhs)
            pe.wait_ge(ev("wst_ready"), 1)
            pe.wait_ge(ev("vn_ready"), 1)
            vv = row(VV)
            for t in range(TT):
                if t:
                    pe.wait_ge(ev("mix_read"), t)
                for g in range(8):
                    ins = pe.matmul(PS[:, 6 + g // 4, (g % 4) * P:(g % 4 + 1) * P], WST[:, g, :],
                                    vv[:, t, g * P:(g + 1) * P], start=True, stop=True)
                ins.then_inc(ev("mix_done"), 1)
            pe.wait_ge(ev("conv_done"), 1)
            cv = col(CV)
            turn("conv", [[cv[:, 4 * h + j, t * P:(t + 1) * P] for j in range(4)] for t in range(TT) for h in range(2)])
            pe.wait_ge(ev("yb_ready"), 1)
            u = row(U)
            rows_to_columns("yb", [u[:, 0], u[:, 1]])
            columns_ready("yb")
            for i in range(2):
                dense(f"wb{i}", lhs)
            pe.wait_ge(ev("ya_ready"), 1)
            rows_to_columns("ya", [vv[:, 0], vv[:, 1]])
            columns_ready("ya")
            hT2 = col(HT2)
            for i in range(2):
                dense(f"wa{i}", lambda k: hT2[:, k, :])
            dense("g1", None)
            pe.wait_ge(ev("m_ready"), 1)
            ga = row(GA)
            rows_to_columns("m", [ga[:, 0], ga[:, 1]])
            columns_ready("m")
            for i in range(2):
                dense(f"wo{i}", lhs)
            dense("sc2", None)
            dense("sh2", None)
            dense("g2", None)
            pe.wait_ge(ev("h2_ready"), 1)
            rows_to_columns("h2", [H2[:, 0], H2[:, 1]])
            columns_ready("h2")
            pe.wait_ge(ev("moe_small_landed"), 64)
            for t in range(TT):
                for k in range(KT):
                    ins = pe.matmul(PS[:, 6, t * NE:(t + 1) * NE], H2T[:, k, t * P:(t + 1) * P], WR[:, k, :],
                                    start=k == 0, stop=k == KT - 1)
            ins.then_inc(ev("logits_done"), 1)
            pe.wait_ge(ev("sel_ready"), 1)
            pos = PS[:, 7, 0:3 * NE].rearrange("p (a e) -> p a e", a=3)
            pe.matmul(pos[:, 0, :], K[:, C_TRI:C_TRI + P], SEL[:, 0, :], start=True, stop=True)
            pe.matmul(pos[:, 1, :], K[:, C_TRI:C_TRI + P], SEL[:, 1, :], start=True, stop=False)
            pe.matmul(pos[:, 1, :], ONES[:], SEL[:, 0, :], start=False, stop=True)
            pe.matmul(pos[:, 2, :], ONES[:], SEL[:, 0, :], start=True, stop=False)
            pe.matmul(pos[:, 2, :], ONES[:], SEL[:, 1, :], start=False, stop=True)
            for t in range(TT):
                ins = pe.transpose(PS[0:NE, 7, P + t * P:P + (t + 1) * P], WM[:, t, :], ident)
            ins.then_inc(ev("pos_done"), 1)
            pe.wait_ge(ev("wmt_ready"), 1)
            pe.wait_ge(ev("table_ready"), 1)
            for t in range(TT):
                if t:
                    pe.wait_ge(ev("acc_started"), t)
                for h in range(2):
                    ins = pe.matmul(PS[:, 6 + h, :], WMT[:, t, :], BDN[:, h * CH:(h + 1) * CH], start=True, stop=True)
                ins.then_inc(ev("bias_sum_done"), 1)

            def expert_block(b, e, final):
                pe.wait_ge(ev("gather_ready"), b + 1)
                for k in range(KT):
                    for t in range(TT):
                        ins = pe.matmul(PS[:, 4, k * BLK:(k + 1) * BLK], H2[:, t, k * P:(k + 1) * P], G[:, t, :],
                                        start=t == 0, stop=t == TT - 1, skip_group_check=True)
                ins.then_inc(ev("gathered"), 1)
                for t in range(TT):
                    ins = pe.transpose(PS[:, 5, t * P:(t + 1) * P], GW[:, t, :], ident)
                ins.then_inc(ev("scatter_turned"), 1)
                pe.wait_ge(ev("xe_copied"), b + 1)
                for part in range(2):
                    for h in range(2):
                        if final:
                            pe.wait_ge(w_landed[2 * part + h], e * 16 + 16 * (pre // RING + 1))
                        else:
                            pe.wait_ge(w_landed[2 * part + h], e * 16 + 16 * (pre // RING + 1))
                    if part == 0:
                        pe.wait_ge(ev("acc_added"), b * 2 + 1)
                    for h in range(2):
                        c = part * D + h * CH
                        ins = pe.matmul(PS[h * BLK:(h + 1) * BLK, part, :], SELB, BGU[:, c:c + CH], start=True, stop=False,
                                        skip_group_check=True)
                        if final and part == 1 and h == 0:
                            ins.then_inc(chunk_done, 2)
                    for k in range(KT):
                        for h in range(2):
                            ins = pe.matmul(PS[h * BLK:(h + 1) * BLK, part, :], XET[:, k, :], W[:, 2 * part + h, k, :],
                                            start=False, stop=k == KT - 1, skip_group_check=True)
                    ins.then_inc(ev("gate_up_done"), 1)
                pe.wait_ge(ev("act_ready"), b + 1)
                for c in range(4):
                    ins = pe.transpose(PS[:, 2, c * P:(c + 1) * P], GT[:, c * P:(c + 1) * P], ident)
                    if final and c == 0:
                        ins.then_inc(chunk_done, 2)
                ins.then_inc(ev("act_turned"), 1)
                pe.wait_ge(ev("actt_copied"), b + 1)
                for h in range(2):
                    pe.wait_ge(w_landed[4 + h], e * 16 + 16 * (pre // RING + 1))
                for k in range(KT):
                    for h in range(2):
                        ins = pe.matmul(PS[h * BLK:(h + 1) * BLK, 3, :], ACTT[:, k, :], W[:, 4 + h, k, :],
                                        start=k == 0, stop=k == KT - 1, skip_group_check=True)
                ins.then_inc(ev("down_done"), 1)
                pe.wait_ge(ev("ye_copied"), b + 1)
                for t in range(TT):
                    for h in range(2):
                        bank = 6 + h if t == 0 else h
                        if t == 0 and h == 0:
                            pe.wait_ge(ev("acc_added"), b * 2 + 1)
                        ins = pe.matmul(PS[:, bank, :], SC[h * BLK:(h + 1) * BLK, t * P:(t + 1) * P],
                                        YE[h * BLK:(h + 1) * BLK, :], start=True, stop=True)
                        if final and t == 0 and h == 0:
                            ins.then_inc(chunk_done, 2)
                    ins.then_inc(ev("scattered"), 1)

            for name in ("scatter_turned", "gate_up_done", "down_done", "scattered", "act_turned"):
                pe.sem_inc(ev(name), 1)
            with pe.Fori(0, NE) as e:
                lo = pe.value_load(TABI[0:1, 0, bass.ds(e, 1)], min_val=0, max_val=64)
                hi = pe.value_load(TABI[0:1, 1, bass.ds(e, 1)], min_val=0, max_val=64)
                with pe.If(hi - lo > 0):
                    with pe.Fori(lo, hi) as b:
                        expert_block(b, e, False)
                expert_block(hi, e, True)
            if upto == 1:
                return
            pe.wait_ge(ev("xn_ready"), 1)
            rows_to_columns("xn", [row(2)[:, 0], row(2)[:, 1]])
            columns_ready("xn")
            for n_ in ("xl0", "xl1", "gl0", "gl1", "q20", "q21"):
                dense(n_, lhs)
            pe.wait_ge(ev("gate_w_landed"), 32)
            pe.wait_ge(ev("xc_ready"), 1)
            for g in range(8):
                if g >= 2:
                    pe.wait_ge(ev("gates_read"), g - 1)
                for j in range(2):
                    n_ = 2 * (g % 4) + j
                    ins = pe.matmul(PS[:, 6 + g % 2, j * T:(j + 1) * T], GW2[:, g // 4, n_, :], XC[:, n_, :], start=True, stop=True)
                ins.then_inc(ev("gates_done"), 1)
            for n_ in ("k20", "k21", "v20", "v21", "gr0", "gr1"):
                dense(n_, lhs)
            pe.wait_ge(ev("q_ready"), 1)
            rows_to_columns("q", [Q2[:, 0], Q2[:, 1]])
            pe.wait_ge(ev("k_ready"), 1)
            rows_to_columns("k", [K2[:, 0], K2[:, 1]])
            columns_ready("k")
            pe.wait_ge(ev("v_ready"), 1)

            def scores(h):
                if h >= 2:
                    pe.wait_ge(ev("scores_masked"), h - 1)
                b = 6 + h % 2
                pe.matmul(PS[:, b, 0:T], KT2[:, h, 0:P], QT[:, h, :], start=True, stop=True)
                pe.matmul(PS[:, b, T:T + P], KT2[:, h, P:T], QT[:, h, P:T], start=True, stop=True) \
                    .then_inc(ev("scores_done"), 1)

            scores(0)
            for h in range(8):
                if h + 1 < 8:
                    scores(h + 1)
                pe.wait_ge(ev("scores_masked"), h + 1)
                if h >= 2:
                    pe.wait_ge(ev("o_copied"), h - 1)
                s_ = SCT[:, h % 2, :]
                o = PS[:, 4 + h % 2, 0:T]
                c = slice(h * P, (h + 1) * P)
                pe.matmul(o[:, 0:P], s_[:, 0:P], V2[:, 0, c], start=True, stop=True)
                pe.matmul(o[:, P:T], s_[:, P:T], V2[:, 0, c], start=True, stop=False)
                pe.matmul(o[:, P:T], s_[:, T:T + P], V2[:, 1, c], start=False, stop=True).then_inc(ev("o_done"), 1)
            pe.wait_ge(ev("o_copied"), 8)
            pe.wait_ge(ev("yr_ready"), 1)
            rows_to_columns("yr", [O2[:, 0], O2[:, 1]])
            columns_ready("yr")
            pe.wait_ge(ev("yl_ready"), 1)
            for i in range(2):
                dense(f"w2o{i}", lambda k: YRT[:, k, :] if k < KT else R2[:, k - KT, :])
            if upto == 2:
                return
            pe.wait_ge(ev("hg_ready"), 1)
            rows_to_columns("hg", [row(9)[:, 0], row(9)[:, 1]])
            columns_ready("hg")
            pe.wait_ge(ev("tables_landed"), 80)
            for k in range(KT):
                ins = pe.matmul(PS[0:GLA_R, 6, 0:T], WGR[:, k, :], hT[:, k, :], start=k == 0, stop=k == KT - 1)
            ins.then_inc(ev("r_done"), 1)
            dense("gq", lhs)
            pe.wait_ge(ev("r_copied"), 1)
            for h in range(GLA_H):
                ins = pe.matmul(PS[:, 6 + h // 2, (h % 2) * T:(h % 2 + 1) * T], WGU[:, h * P:(h + 1) * P], RT,
                                start=True, stop=True)
            ins.then_inc(ev("gate_done"), 1)
            dense("gk", lhs)
            for i in range(4):
                dense(f"gv{i}", lhs)
            pe.wait_ge(ev("kend_ready"), 1)
            turn("kend", [[KE[:, h, t * P:(t + 1) * P] for h in range(GLA_H)] for t in range(TT)])
            pe.wait_ge(ev("qk_ready"), 1)
            for n_ in range(4):
                t, r = n_ // 2, (n_ % 2) * GLA_C
                c = slice(n_ * GLA_C, (n_ + 1) * GLA_C)
                for h in range(GLA_H):
                    o = PS[r:r + GLA_C, 6, (t * 4 + h) * GLA_C:(t * 4 + h + 1) * GLA_C]
                    ins = pe.matmul(o, GK[:, h, c], GQ[:, h, c], start=True, stop=True, skip_group_check=True)
            ins.then_inc(ev("att_done"), 1)
            for i in range(4):
                dense(f"gz{i}", lhs)
            columns_ready("kend")
            pe.wait_ge(ev("att_masked"), 1)
            pe.wait_ge(ev("gv_ready"), 4)
            pe.wait_ge(ev("gz_ready"), 4)
            for n_ in range(4):
                t, r = n_ // 2, (n_ % 2) * GLA_C
                c = slice(n_ * GLA_C, (n_ + 1) * GLA_C)
                if n_ == 2:
                    pe.wait_ge(ev("og_copied"), 4)
                for h in range(GLA_H):
                    vh = GV[r:r + GLA_C, t, h * GLA_DV:(h + 1) * GLA_DV]
                    ins = pe.matmul(PS[r:r + GLA_C, h, :], ATT[r:r + GLA_C, t, h, :], vh, start=True, stop=n_ == 0,
                                    skip_group_check=True)
                    if n_ > 0:
                        pe.wait_ge(ev("state_ready"), (n_ - 1) * GLA_H + h + 1)
                        ins = pe.matmul(PS[r:r + GLA_C, h, :], GQ[:, h, c], GS[:, h, :], start=False, stop=True,
                                        skip_group_check=True)
                    if n_ == 3:
                        ins.then_inc(ev("go_done"), 1)
                    if n_ < 3:
                        ins = pe.matmul(PS[:, 4 + h, :], KR[r:r + GLA_C, t, h * P:(h + 1) * P], vh, start=True, stop=True)
                        ins.then_inc(ev("kv_done"), 1)
            pe.wait_ge(ev("og_ready"), 1)
            rows_to_columns("og", OG, 16)
            columns_ready("og")
            for i in range(2):
                dense(f"go{i}", lambda k: OGT[:, k, :])
            if upto == 3:
                return
            pe.wait_ge(ev("hs_ready"), 1)
            rows_to_columns("hs", [row(9)[:, 0], row(9)[:, 1]])
            columns_ready("hs")
            for i in range(4):
                dense(f"su{i}", lhs)
            for i in range(4):
                dense(f"sz{i}", lhs)
            for n_ in ("sz2", "sz3"):
                pe.wait_ge(unit_free[UNIT[n_][0] % 2], UNIT[n_][0] // 2 + 1)
            pe.sem_inc(ev("s5_turned"), 1)
            pe.sem_inc(ev("s5_half_done"), 1)
            with pe.Fori(0, S5_CT) as ct:
                pe.wait_ge(ev("s5_in_ready"), ct + 1)
                pe.wait_ge(ev("s5_bd_ready"), ct + 1)
                pe.wait_ge(ev("s5_lhs_ready"), ct + 1)
                for a in range(2):
                    pe.transpose(PS[:, 4, a * P:(a + 1) * P], BD[:, a].rearrange("p q b i -> p (q b i)"), ident)
                for a in range(2):
                    ins = pe.transpose(PS[:, 4, (2 + a) * P:(3 + a) * P], CS[:, a].rearrange("p b q -> p (b q)"), ident)
                ins.then_inc(ev("s5_turned"), 1)
                pe.wait_ge(ev("s5_lhs_ready"), ct + 2)
                pe.wait_ge(ev("s5_bu_read"), ct + 1)
                for q in range(PAIRS):
                    r = slice(32 * q, 32 * q + 32)
                    for a in range(2):
                        ins = pe.matmul(PS[:, q, a * T:(a + 1) * T], BTW[r, a, :], UC[r, :], start=True, stop=True)
                ins.then_inc(ev("s5_bu_done"), 1)
                for hb in range(2):
                    pe.wait_ge(ev("s5_prod_ready"), ct * 2 + hb + 1)
                    for j in range(2):
                        q = 2 * hb + j
                        for m, (w_, r_) in enumerate(((0, SA1), (1, SB2), (2, SA2), (2, SB1))):
                            ins = pe.matmul(PS[32 * q:32 * q + 32, 6, 0:T], CTW[:, w_, q].rearrange("p b i -> p (b i)"),
                                            r_[:, j, :], start=m == 0, stop=m == 3, skip_group_check=True)
                    ins.then_inc(ev("s5_half_done"), 1)
            for i in range(4):
                if i == 0:
                    pe.wait_ge(ev("s5_gelu"), S5_CT + 1)
                dense(f"sg{i}", lambda k: Y16[:, k, :])
            pe.wait_ge(ev("glu_ready"), 1)
            for i in range(2):
                dense(f"so{i}", lambda k: U16[:, k, :])

        @block.scalar
        def _(act):

            def param(dst, src):
                act.dma_start(dst, src).then_inc(param_landed, 16)

            def v128(a):
                return a.rearrange("(r q) -> r q", q=P)

            param(PVR[R_C:R_C + 8, 0, :], v128(A["c"][0]))
            param(PVR[R_AV:R_AV + 8, 0, :], v128(A["b_in"][0, 0:D]))
            param(PVR[R_AG:R_AG + 8, 0, :], v128(A["b_in"][0, D:2 * D]))
            param(PVR[R_CB:R_CB + 8, 0, :], v128(A["conv_b"][0]))
            param(PVR[R_BS:R_BS + 8, 0, :], A["b_s"][0])
            param(PVR[R_CW2:R_CW2 + 32, 0, :], A["conv_w_2"].rearrange("j (k q) -> (j k) q", q=P))
            param(PVR[R_CB2:R_CB2 + 8, 0, :], v128(A["conv_b_2"]))
            param(PVR[R_GAB:R_GAB + 8, 0, :], A["gate_a_b_2"])
            param(PVR[R_GXB:R_GXB + 8, 0, :], A["gate_x_b_2"])
            param(PVR[R_LAM:R_LAM + 8, 0, :], v128(A["lru_lambda_2"]))
            param(PVR[R_BG:R_BG + 4, 0, :], v128(A["gla_b_gate_3"][0]))
            param(PVR[R_GLU:R_GLU + 16, 0, :], v128(A["s5_b_glu_3"][0]))
            param(PVR[:, 1, :], A["conv_w"][0, 0:16].rearrange("j (k q) -> (j k) q", q=P))
            param(PVR[0:120, 2, :], A["conv_w"][0, 16:31].rearrange("j (k q) -> (j k) q", q=P))
            param(PVR[0:64, 3, :], A["s5_lam_re_3"][0].rearrange("(a b) p -> a (b p)", b=2))
            param(PVR[64:128, 3, :], A["s5_lam_im_3"][0].rearrange("(a b) p -> a (b p)", b=2))
            param(LDT[0:64], A["s5_log_dt_3"][0].rearrange("(a b) -> a b", b=2))
            param(PVR[64:80, 4, :], A["s5_d_3"][0].rearrange("(a b) i -> a (b i)", b=8))
            act.dma_start(WSR, A["w_s"][0].rearrange("g i j -> i g j")).then_inc(ev("ws_landed"), 16)

            def unit_act(name, dst, func, **kw):
                wait_unit(act, name)
                free_unit(act.activation(dst, unit_ps(name), func, **kw), name)

            for b in range(2):
                act.wait_ge(tp_ready, TB["params"] + b + 1)
                n_ = 4 if b == 0 else 1
                if b == 0:
                    act.activation(PC[:, 0, 0:R_N0], PS[:, 4, 0:R_N0], ACT.Copy)
                    act.activation(PC[:, 1, :], PS[:, 4, P:2 * P], ACT.Copy)
                    act.activation(PC[:, 2, 0:120], PS[:, 4, 2 * P:2 * P + 120], ACT.Copy)
                    act.activation(PC[:, 3, :], PS[:, 4, 3 * P:4 * P], ACT.Copy).then_inc(tp_copied, 1)
                else:
                    act.activation(PC[:, 4, 0:80], PS[:, 5, 0:80], ACT.Copy).then_inc(tp_copied, 1)
            act.drain()
            act.activation(pcol(R_C, 8), pcol(R_C, 8), ACT.Silu).then_inc(ev("silu_c_ready"), 1)
            for b in range(2):
                act.wait_ge(tp_ready, TB["ws"] + b + 1)
                act.activation(WST[:, 4 * b:4 * b + 4, :], PS[:, 4 + b, :].rearrange("p (k t) -> p k t", k=4),
                               ACT.Copy).then_inc(tp_copied, 1)
            act_std(act)
            copy_columns(act, "h1", col(HT))
            sg = col(U)
            for i in range(2):
                name = f"ag{i}"
                wait_unit(act, name)
                for m in range(4):
                    k = 4 * i + m
                    ins = act.activation(sg[:, k, :], unit_ps(name)[:, m // 2, (m % 2) * T:(m % 2 + 1) * T], ACT.Sigmoid,
                                         bias=pcol(R_AG + k))
                    if m == 3:
                        free_unit(ins, name)
            act.drain()
            act.wait_ge(ev("v_raw"), 1)
            act.activation(row(VV), row(VV), ACT.Gelu).then_inc(ev("v_gelu"), 1)
            act.wait_ge(ev("u_raw"), 1)
            act.activation(row(U), row(U), ACT.Gelu).then_inc(ev("u_gelu"), 1)
            act.wait_ge(ev("ga_raw"), 1)
            act.activation(row(GA), row(GA), ACT.Sigmoid).then_inc(ev("ga_sig"), 1)
            act.wait_ge(ev("gb_raw"), 1)
            act.activation(row(GB), row(GB), ACT.Sigmoid).then_inc(ev("gb_sig"), 1)
            act_std(act)
            act.wait_ge(ev("mix_done"), 2)
            vv = row(VV)
            for b in range(4):
                act.wait_ge(tp_ready, TB["conv"] + b + 1)
                ins = act.activation(vv[:, b // 2, (b % 2) * CH:(b % 2 + 1) * CH], PS[:, 4 + (TB["conv"] + b) % 2, :], ACT.Copy)
                ins.then_inc(tp_copied, 1)
            copy_columns(act, "yb", col(HT))
            act_std(act)
            act.wait_ge(ev("ya_norm"), 1)
            act.activation(vv, vv, ACT.Silu).then_inc(ev("ya_ready"), 1)
            copy_columns(act, "ya", col(HT2))
            copy_columns(act, "m", col(HT))
            act_std(act)
            act_std(act)
            copy_columns(act, "h2", H2T)
            act.wait_ge(ev("neg_max"), 1)
            for t in range(TT):
                ins = act.activation(E4[:, t, :], V8[:, t, 0:4], ACT.Exp, bias=NM[:, t:t + 1], accum_out=ES[:, t:t + 1])
            ins.then_inc(ev("exp_ready"), 1)
            act.wait_ge(ev("pos_done"), 1)
            act.activation(WMT, PS[0:NE, 7, P:P + T].rearrange("p (t s) -> p t s", t=TT), ACT.Copy).then_inc(ev("wmt_ready"), 1)
            act.wait_ge(ev("table_ready"), 1)

            def expert_block(b):
                act.wait_ge(ev("gathered"), b + 1)
                act.wait_ge(ev("gate_up_done"), b * 2 + 1)
                act.activation(XET, PS[:, 4, :].rearrange("p (k s) -> p k s", k=KT), ACT.Copy).then_inc(ev("xe_copied"), 1)
                act.wait_ge(ev("gate_ready"), b + 1)
                act.activation(SG, GT, ACT.Sigmoid, scale=1.702).then_inc(ev("sig_gate"), 1)
                act.wait_ge(ev("act_turned"), b + 2)
                act.wait_ge(ev("down_done"), b + 1)
                act.activation(ACTT.rearrange("p (h c) s -> p c h s", h=2),
                               PS[:, 2, :].rearrange("p (c h s) -> p c h s", c=4, h=2), ACT.Copy).then_inc(ev("actt_copied"), 1)
                act.wait_ge(ev("scattered"), b * 2 + 1)
                act.wait_ge(ev("scatter_turned"), b + 2)
                act.activation(SC, PS[:, 5, 0:T], ACT.Copy)
                act.wait_ge(ev("down_done"), b + 2)
                act.activation(YE, PS[:, 3, :], ACT.Copy).then_inc(ev("ye_copied"), 1)

            with act.Fori(0, NE) as e:
                lo = act.value_load(TABI[0:1, 0, bass.ds(e, 1)], min_val=0, max_val=64)
                hi = act.value_load(TABI[0:1, 1, bass.ds(e, 1)], min_val=0, max_val=64)
                with act.If(hi - lo > 0):
                    with act.Fori(lo, hi) as b:
                        expert_block(b)
                expert_block(hi)
            act_std(act)
            if upto == 1:
                return
            act.wait_ge(ev("lam_in"), 1)
            act.activation(LS[:, 0], pcol(R_LAM, 8), ACT.Abs)
            act.drain()
            act.activation(LS[:, 0], LS[:, 0], ACT.Exp, scale=-1.0)
            act.drain()
            act.activation(LS[:, 1], LS[:, 0], ACT.Ln, bias=1.0).then_inc(ev("lam_ln"), 1)
            act_std(act)
            copy_columns(act, "xn", col(HT))

            def quarter(name):
                return unit_ps(name).rearrange("p a (b t) -> p (a b) t", b=2)

            for i in range(2):
                wait_unit(act, f"xl{i}")
                ins = act.activation(XLC[:, 4 * i:4 * i + 4, :], quarter(f"xl{i}"), ACT.Copy)
                free_unit(ins, f"xl{i}")
            for i in range(2):
                wait_unit(act, f"gl{i}")
                free_unit(act.activation(GLC[:, 4 * i:4 * i + 4, :], quarter(f"gl{i}"), ACT.Silu), f"gl{i}")
            for g in range(8):
                act.wait_ge(ev("gates_done"), g + 1)
                for j in range(2):
                    n_ = 2 * (g % 4) + j
                    dst = (R2 if g < 4 else I2)[:, n_, :]
                    ins = act.activation(dst, PS[:, 6 + g % 2, j * T:(j + 1) * T], ACT.Sigmoid,
                                         bias=pcol((R_GAB if g < 4 else R_GXB) + n_))
                ins.then_inc(ev("gates_read"), 1)
            act.wait_ge(ev("rates_ready"), 1)
            act.wait_ge(ev("ix_ready"), 1)
            for k in range(KT):
                act.activation(XC[:, k, :], R2[:, k, :], ACT.Exp, scale=LS[:, 4, k:k + 1])
            act.drain()
            for k in range(KT):
                ins = act.activation(R2[:, k, :], R2[:, k, :], ACT.Exp, scale=LS[:, 5, k:k + 1])
            ins.then_inc(ev("a_ready"), 1)
            act.wait_ge(ev("a2_clipped"), 1)
            act.activation(R2, R2, ACT.Sqrt, scale=-1.0, bias=1.0).then_inc(ev("mult_ready"), 1)
            act.wait_ge(ev("k_ready"), 1)
            for i in range(2):
                wait_unit(act, f"v2{i}")
                ins = act.activation(V2[:, :, i * CH:(i + 1) * CH], unit_ps(f"v2{i}"), ACT.Copy)
                free_unit(ins, f"v2{i}")
            for i in range(2):
                wait_unit(act, f"gr{i}")
                ins = act.activation(GR[:, :, i * CH:(i + 1) * CH], unit_ps(f"gr{i}"), ACT.Silu)
                free_unit(ins, f"gr{i}")
            act.drain()
            act.sem_inc(ev("v_ready"), 1)
            act.wait_ge(ev("yl_ready"), 1)
            copy_columns(act, "q", QT)
            copy_columns(act, "k", KT2)
            for h in range(8):
                act.wait_ge(ev("o_done"), h + 1)
                act.activation(O2[:, :, h * P:(h + 1) * P], PS[:, 4 + h % 2, 0:T].rearrange("p (t e) -> p t e", t=TT),
                               ACT.Copy).then_inc(ev("o_copied"), 1)
            act.wait_ge(ev("hvar_ready"), 1)
            act.activation(HSD[:], HVE[:], ACT.Sqrt).then_inc(ev("hstd_ready"), 1)
            copy_columns(act, "yr", YRT)
            act_std(act)
            if upto == 2:
                return
            act_std(act)
            copy_columns(act, "hg", col(HT))
            act.wait_ge(ev("r_done"), 1)
            act.activation(RT, PS[0:GLA_R, 6, 0:T], ACT.Copy).then_inc(ev("r_copied"), 1)
            wait_unit(act, "gq")
            free_unit(act.activation(GQ, quarter("gq"), ACT.Copy, scale=GLA_DK ** -0.5), "gq")
            wait_unit(act, "gk")
            free_unit(act.activation(GK, quarter("gk"), ACT.Copy), "gk")
            act.wait_ge(ev("gate_x"), 1)
            act.activation(BC, LA, ACT.Abs)
            act.drain()
            act.activation(BC, BC, ACT.Exp, scale=-1.0)
            act.drain()
            act.activation(BC, BC, ACT.Ln, bias=1.0).then_inc(ev("gate_ln"), 1)
            act.wait_ge(ev("bcum_ready"), 1)
            act.activation(TE, BC, ACT.Exp)
            act.activation(DC4[:], BC[:, :, GLA_C - 1:T:GLA_C], ACT.Exp)
            act.activation(LA, LA, ACT.Exp).then_inc(ev("exps_ready"), 1)
            act.wait_ge(ev("qg_ready"), 1)
            act.activation(TE, BC, ACT.Exp, scale=-1.0).then_inc(ev("expn_ready"), 1)
            for i in range(4):
                wait_unit(act, f"gv{i}")
                free_unit(act.activation(GV[:, :, i * CH:(i + 1) * CH], unit_ps(f"gv{i}"), ACT.Copy), f"gv{i}")
            act.drain()
            act.sem_inc(ev("gv_ready"), 4)
            for b in range(TT):
                act.wait_ge(tp_ready, TB["kend"] + b + 1)
                act.activation(KR[:, b, :], PS[:, 4 + (TB["kend"] + b) % 2, :], ACT.Copy).then_inc(tp_copied, 1)
            for i in range(4):
                wait_unit(act, f"gz{i}")
                free_unit(act.activation(GZ[:, :, i * CH:(i + 1) * CH], unit_ps(f"gz{i}"), ACT.Silu), f"gz{i}")
            act.drain()
            act.sem_inc(ev("gz_ready"), 4)
            for t in range(TT):
                for h in range(GLA_H):
                    if t == 0:
                        act.wait_ge(ev("kv_done"), GLA_H + h + 1)
                    else:
                        act.wait_ge(ev("go_done"), GLA_H)
                    act.activation(OG[t][:, h * GLA_DV:(h + 1) * GLA_DV], PS[:, h, :], ACT.Copy).then_inc(ev("og_copied"), 1)
            act.wait_ge(ev("hvar_ready"), 2)
            act.activation(HSD[:, 0:8], HVE[:, 0:8], ACT.Sqrt).then_inc(ev("hstd_ready"), 1)
            copy_columns(act, "og", OGT, 16)
            if upto == 3:
                return
            act_std(act)
            copy_columns(act, "hs", col(HT))
            for i in range(4):
                wait_unit(act, f"su{i}")
                free_unit(act.activation(U16[:, 4 * i:4 * i + 4, :], quarter(f"su{i}"), ACT.Copy), f"su{i}")
            for i in range(4):
                wait_unit(act, f"sz{i}")
                free_unit(act.activation(Z16[:, 4 * i:4 * i + 4, :], quarter(f"sz{i}"), ACT.Silu), f"sz{i}")
            act.drain()
            act.sem_inc(ev("uz_ready"), 1)
            act.activation(work[0], PC[:, 4, 0:64], ACT.Exp).then_inc(ev("dt_ready"), 1)
            act.wait_ge(ev("turns_ready"), 1)
            act.activation(work[3], work[1], ACT.Exp)
            act.activation(work[4], TH, ACT.Sin, scale=TWO_PI)
            act.activation(work[5], TH, ACT.Sin, scale=TWO_PI / 2).then_inc(ev("coef_trig"), 1)
            act.wait_ge(ev("zeroed"), 1)
            act.sem_inc(ev("s5_gelu"), 1)
            act.sem_inc(ev("s5_lhs_ready"), 1)
            with act.Fori(0, S5_CT) as ct:
                act.wait_ge(ev("s5_turned"), ct + 1)
                for a in range(2):
                    for g in range(2):
                        r = slice(64 * g, 64 * g + 64)
                        ins = act.activation(BD[r, a, :, g, :], BB[r, a, bass.ds(ct * PAIRS, PAIRS), :], ACT.Copy)
                ins.then_inc(ev("s5_bd_ready"), 1)
                act.wait_ge(ev("s5_turned"), ct + 2)
                act.wait_ge(ev("s5_half_done"), ct * 2 + 1)
                act.activation(BTW, PS[:, 4, 0:T].rearrange("p (a m) -> p a m", a=2), ACT.Copy)
                cps = PS[:, 4, T:2 * T].rearrange("p (a q b i) -> p a q b i", a=2, q=PAIRS, b=2)
                for g in range(2):
                    r = slice(64 * g, 64 * g + 64)
                    act.activation(CTW[r, 0, :, g, :], cps[r, 0, :, g, :], ACT.Copy)
                    act.activation(CTW[r, 1, :, g, :], cps[r, 0, :, g, :], ACT.Copy, scale=-1.0)
                    ins = act.activation(CTW[r, 2, :, g, :], cps[r, 1, :, g, :], ACT.Copy, scale=-1.0)
                ins.then_inc(ev("s5_lhs_ready"), 1)
                for hb in range(2):
                    act.wait_ge(ev("s5_turns"), ct * 2 + hb + 1)
                    act.activation(SA2, SA1, ACT.Abs)
                    act.activation(SSIN, SA1, ACT.Sin, scale=TWO_PI)
                    act.drain()
                    act.activation(SCOS, SA2, ACT.Sin, scale=-TWO_PI, bias=HALF_PI).then_inc(ev("s5_trig"), 1)
                act.wait_ge(ev("s5_y_ready"), ct + 1)
                act.activation(Y16[:, bass.ds(ct, 1), :].rearrange("p a t -> p (a t)"), SA1[:, 0, :], ACT.Gelu_apprx_tanh) \
                    .then_inc(ev("s5_gelu"), 1)
            for i in range(4):
                wait_unit(act, f"sg{i}")
                for m in range(4):
                    ins = act.activation(U16[:, 4 * i + m, :], quarter(f"sg{i}")[:, m, :], ACT.Sigmoid, bias=pcol(R_GLU + 4 * i + m))
                free_unit(ins, f"sg{i}")
            act.drain()
            act.sem_inc(ev("glu_sig"), 1)
            act_std(act)

        @block.vector
        def _(dve):
            def rows_from(name, dst, vec, j):
                wait_unit(dve, name)
                free_unit(dve.tensor_tensor(dst[:, :, j * CH:(j + 1) * CH], unit_ps(name),
                                            bt(vec[:, j * CH:(j + 1) * CH]), ALU.add), name)

            def mod_from(name, dst):
                vec = vector(dve, "b_mod")
                wait_unit(dve, name)
                free_unit(dve.tensor_tensor(dst, unit_ps(name).rearrange("p a b -> p (a b)"), vec, ALU.add), name)
                dve.drain()

            def used(ins):
                ins.then_inc(v_used, 1)

            dve.memset(ONES[:], 1.0)
            dve.wait_ge(param_landed, 16 * N_PARAM)
            dve.tensor_copy(PVR[0:64, 4, :].rearrange("p (b q) -> p b q", b=2),
                            LDT[0:64].unsqueeze(2).to_broadcast([64, 2, 64])).then_inc(ev("log_dt_ready"), 1)
            dve.wait_ge(ev("silu_c_ready"), 1)
            dve.tensor_copy(CB, pcol(R_C, 8).unsqueeze(2).to_broadcast([P, KT, P])).then_inc(ev("cond_ready"), 1)
            dve.wait_ge(tp_copied, TB["ws"] + 2)
            dve.memset(WST[64:128, :, 0:64], 0.0).then_inc(ev("wst_ready"), 1)
            dve.wait_ge(x_landed, 16)
            h1 = row(HN)
            layer_norm(dve, h1, X)

            def modulate(dst, src, sc_name, sh_name, done):
                vec = vector(dve, "b_mod")
                wait_unit(dve, sc_name)
                ins = dve.scalar_tensor_tensor(MA, unit_ps(sc_name).rearrange("p a b -> p (a b)"), 1.0, vec, ALU.add, ALU.add)
                free_unit(ins, sc_name)
                dve.drain()
                used(dve.tensor_tensor(dst, src, bt(MA), ALU.mult))
                vec = vector(dve, "b_mod")
                wait_unit(dve, sh_name)
                ins = dve.tensor_tensor(MB, unit_ps(sh_name).rearrange("p a b -> p (a b)"), vec, ALU.add)
                free_unit(ins, sh_name)
                dve.drain()
                used(dve.tensor_tensor(dst[:, 0], dst[:, 0], MB, ALU.add))
                dve.tensor_tensor(dst[:, 1], dst[:, 1], MB, ALU.add).then_inc(done, 1)

            modulate(h1, h1, "sc1", "sh1", ev("h1_ready"))
            ya, sg = col(HN), col(U)
            dve.wait_ge(tp_ready, TB["h1"] + 4)
            for i in range(2):
                name = f"av{i}"
                wait_unit(dve, name)
                dve.wait_ge(unit_free[UNIT[f"ag{i}"][0] % 2], UNIT[f"ag{i}"][0] // 2 + 1)
                for m in range(4):
                    k = 4 * i + m
                    ins = dve.scalar_tensor_tensor(ya[:, k, :], unit_ps(name)[:, m // 2, (m % 2) * T:(m % 2 + 1) * T],
                                                   pcol(R_AV + k), sg[:, k, :], ALU.add, ALU.mult)
                free_unit(ins, name)
            dve.drain()
            cv = col(CV)
            raw = [("v0", VV, 0), ("v1", VV, 1), ("u0", U, 0), ("u1", U, 1), ("ga0", GA, 0), ("ga1", GA, 1),
                   ("gb0", GB, 0), ("gb1", GB, 1)]
            vec = None
            for lag in range(CONV1):
                for k in range(KT):
                    r = P + (CONV1 - 1 - lag) * KT + k
                    if lag == 0:
                        dve.tensor_scalar(cv[:, k, :], ya[:, k, :], pcol(r), pcol(R_CB + k), ALU.mult, ALU.add)
                    else:
                        ins = dve.scalar_tensor_tensor(cv[:, k, lag:], ya[:, k, 0:T - lag], pcol(r), cv[:, k, lag:],
                                                       ALU.mult, ALU.add)
                if lag == CONV1 - 1:
                    ins.then_inc(ev("conv_done"), 1)
                if lag >= 3 and lag % 3 == 0 and lag // 3 <= 8:
                    name, area, j = raw[lag // 3 - 1]
                    if j == 0:
                        vec = vector(dve, "b_in")
                    rows_from(name, row(area), vec, j)
                    dve.drain()
                    if j == 1:
                        dve.sem_inc(v_used, 1)
                        dve.sem_inc(ev({VV: "v_raw", U: "u_raw", GA: "ga_raw", GB: "gb_raw"}[area]), 1)
                else:
                    dve.drain()
            vv, u = row(VV), row(U)
            dve.wait_ge(ev("v_gelu"), 1)
            layer_norm(dve, vv, vv)

            def gain_bias(dst, gname, bname, done):
                vec = vector(dve, gname)
                used(dve.tensor_tensor(dst, dst, bt(vec), ALU.mult))
                dve.drain()
                vec = vector(dve, bname)
                used(dve.tensor_tensor(dst, dst, bt(vec), ALU.add))
                dve.drain()
                if done is not None:
                    dve.sem_inc(done, 1)

            gain_bias(vv, "ln_v_g", "ln_v_b", ev("vn_ready"))
            dve.wait_ge(ev("u_gelu"), 1)
            for t in range(TT):
                dve.wait_ge(ev("mix_done"), t + 1)
                for g in range(8):
                    ins = dve.scalar_tensor_tensor(u[:, t, g * P:(g + 1) * P], PS[:, 6 + g // 4, (g % 4) * P:(g % 4 + 1) * P],
                                                   pcol(R_BS + g), u[:, t, g * P:(g + 1) * P], ALU.add, ALU.mult)
                ins.then_inc(ev("mix_read"), 1)
            dve.drain()
            dve.sem_inc(ev("yb_ready"), 1)
            dve.wait_ge(tp_copied, TB["conv"] + 4)
            layer_norm(dve, vv, vv)
            gb = row(GB)
            ga = row(GA)
            vec = vector(dve, "b_b")
            dve.wait_ge(ev("gb_sig"), 1)
            cvr = row(CV)
            for i in range(2):
                rows_from(f"wb{i}", cvr, vec, i)
            dve.drain()
            used(dve.tensor_tensor(gb, gb, cvr, ALU.mult))
            gain_bias(vv, "ln_a_g", "ln_a_b", ev("ya_norm"))
            vec = vector(dve, "b_a")
            dve.wait_ge(ev("ga_sig"), 1)
            for i in range(2):
                rows_from(f"wa{i}", cvr, vec, i)
            dve.drain()
            used(dve.tensor_tensor(ga, ga, cvr, ALU.mult))
            dve.drain()
            dve.tensor_tensor(ga, ga, gb, ALU.add).then_inc(ev("m_ready"), 1)
            vec = vector(dve, "b_mod")
            wait_unit(dve, "g1")
            free_unit(dve.tensor_tensor(MA, unit_ps("g1").rearrange("p a b -> p (a b)"), vec, ALU.add), "g1")
            dve.drain()
            dve.sem_inc(v_used, 1)
            vec = vector(dve, "b_out")
            for i in range(2):
                rows_from(f"wo{i}", cvr, vec, i)
            dve.drain()
            used(dve.tensor_tensor(cvr, cvr, bt(MA), ALU.mult))
            dve.drain()

            def residual(y):
                dve.scalar_tensor_tensor(X[:, 0], X[:, 0], ALPHA, y[:, 0], ALU.mult, ALU.add)
                dve.scalar_tensor_tensor(X[:, 1], X[:, 1], ALPHA, y[:, 1], ALU.mult, ALU.add)
                dve.drain()

            residual(cvr)
            layer_norm(dve, X, X)
            gain_bias(X, "post1_g", "post1_b", ev("x1_ready"))
            layer_norm(dve, H2, X)
            modulate(H2, H2, "sc2", "sh2", ev("h2_ready"))
            vec = vector(dve, "b_mod")
            wait_unit(dve, "g2")
            free_unit(dve.tensor_tensor(MA, unit_ps("g2").rearrange("p a b -> p (a b)"), vec, ALU.add), "g2")
            dve.drain()
            dve.sem_inc(v_used, 1)
            dve.wait_ge(ev("moe_small_landed"), 64)
            dve.wait_ge(ev("logits_done"), 1)
            dve.tensor_tensor(LG, PS[:, 6, 0:2 * NE].rearrange("p (t e) -> p t e", t=TT),
                              BRT[:, 0:1, :].to_broadcast([P, TT, NE]), ALU.add)
            dve.drain()
            for t in range(TT):
                dve.max(V8[:, t, :], LG[:, t, :])
            dve.drain()
            for t in range(TT):
                dve.max_index(I8[:, t, :], V8[:, t, :], LG[:, t, :])
            dve.tensor_scalar(NM, V8[:, :, 0], -1.0, None, ALU.mult)
            dve.drain()
            dve.tensor_copy(F8, I8).then_inc(ev("neg_max"), 1)
            dve.wait_ge(ev("exp_ready"), 1)
            dve.reciprocal(ER, ES)
            dve.drain()
            for t in range(TT):
                dve.tensor_scalar(E4[:, t, :], E4[:, t, :], ER[:, t:t + 1], None, ALU.mult)
            dve.drain()
            iota_e = K[:, C_E:C_E + NE]
            for j in range(TOPK):
                for t in range(TT):
                    if j == 0:
                        dve.tensor_scalar(SEL[:, t, :], iota_e, F8[:, t, j:j + 1], None, ALU.is_equal)
                        dve.tensor_scalar(WM[:, t, :], iota_e, F8[:, t, j:j + 1], E4[:, t, j:j + 1], ALU.is_equal, ALU.mult)
                    else:
                        dve.tensor_scalar(OH[:, t, :], iota_e, F8[:, t, j:j + 1], None, ALU.is_equal)
                dve.drain()
                if j:
                    dve.tensor_tensor(SEL, SEL, OH, ALU.add)
                    for t in range(TT):
                        dve.scalar_tensor_tensor(WM[:, t, :], OH[:, t, :], E4[:, t, j:j + 1], WM[:, t, :], ALU.mult, ALU.add)
                    dve.drain()
            dve.sem_inc(ev("sel_ready"), 1)
            dve.wait_ge(ev("pos_done"), 1)
            dve.wait_ge(ev("wmt_ready"), 1)
            pos = PS[:, 7, 0:3 * NE].rearrange("p (a e) -> p a e", a=3)
            dve.scalar_tensor_tensor(POS, pos[:, 0:2, :], 1.0, SEL, ALU.add, ALU.mult)
            cnt, nx, one_nx = pos[0:1, 2, :], TABF[:, 0, :], TABF[:, 1, :]
            dve.tensor_scalar(nx, cnt, float(BLK), 1.0, ALU.is_gt, ALU.add)
            dve.tensor_scalar(TABF[:, 1, :], cnt, float(2 * BLK), None, ALU.is_gt)
            dve.tensor_scalar(TABF[:, 2, :], cnt, float(3 * BLK), None, ALU.is_gt)
            dve.drain()
            dve.tensor_scalar_add(POS, POS, -1.0)
            dve.tensor_tensor(nx, nx, TABF[:, 1, :], ALU.add)
            dve.drain()
            dve.tensor_tensor(nx, nx, TABF[:, 2, :], ALU.add)
            dve.drain()
            dve.tensor_tensor_scan(TABF[:, 1, :], ONES[0:1, 0:NE], nx, 0.0, ALU.mult, ALU.add)
            dve.drain()
            dve.tensor_tensor(TABI[:, 0, :], TABF[:, 1, :], nx, ALU.subtract)
            dve.tensor_scalar_add(TABI[:, 1, :], TABF[:, 1, :], -1.0)
            dve.drain()
            dve.sem_inc(ev("table_ready"), 1)
            for t in range(TT):
                dve.wait_ge(ev("bias_sum_done"), t + 1)
                dve.tensor_copy(YACC[:, t, :], PS[:, 6:8, :].rearrange("p a b -> p (a b)")).then_inc(ev("acc_started"), 1)
            dve.drain()

            def expert_block(b, e, slots):
                dve.wait_ge(ev("scatter_turned"), b + 1)
                dve.tensor_copy(PW[:, 0, :], POS[:, :, bass.ds(e, 1)].rearrange("p t e -> p (t e)"))
                dve.tensor_copy(PW[:, 1, :], WM[:, :, bass.ds(e, 1)].rearrange("p t e -> p (t e)"))
                dve.tensor_copy(SELB, ident[0:NE, bass.ds(e, 1)].to_broadcast([NE, BLK]))
                dve.drain()
                io = K[:, bass.ds(slots * P + C_SLOT, P)]
                for t in range(TT):
                    dve.tensor_scalar(G[:, t, :], io[:, 0:BLK], PW[:, 0, t:t + 1], None, ALU.is_equal)
                    ins = dve.tensor_scalar(GW[:, t, :], io, PW[:, 0, t:t + 1], PW[:, 1, t:t + 1], ALU.is_equal, ALU.mult)
                ins.then_inc(ev("gather_ready"), 1)
                dve.wait_ge(ev("gate_up_done"), b * 2 + 2)
                dve.wait_ge(ev("act_turned"), b + 1)
                dve.tensor_scalar(GT, PS[:, 0, :], 7.0, None, ALU.min).then_inc(ev("gate_ready"), 1)
                dve.wait_ge(ev("gate_up_done"), b * 2 + 3)
                dve.tensor_scalar(UP, PS[:, 1, :], -7.0, 7.0, ALU.max, ALU.min)
                dve.drain()
                dve.wait_ge(ev("sig_gate"), b + 1)
                dve.scalar_tensor_tensor(UP, UP, 1.0, SG, ALU.add, ALU.mult)
                dve.drain()
                dve.tensor_tensor(GT, GT, UP, ALU.mult).then_inc(ev("act_ready"), 1)
                for t in range(TT):
                    dve.wait_ge(ev("scattered"), b * 2 + (t + 2))
                    bank = 6 if t == 0 else 0
                    dve.tensor_tensor(YACC[:, t, :], YACC[:, t, :], PS[:, bank:bank + 2, :].rearrange("p a b -> p (a b)"),
                                      ALU.add).then_inc(ev("acc_added"), 1)
                dve.drain()

            dve.sem_inc(ev("acc_added"), 1)
            with dve.Fori(0, NE) as e:
                lo = dve.value_load(TABI[0:1, 0, bass.ds(e, 1)], min_val=0, max_val=64)
                hi = dve.value_load(TABI[0:1, 1, bass.ds(e, 1)], min_val=0, max_val=64)
                with dve.If(hi - lo > 0):
                    with dve.Fori(lo, hi) as b:
                        expert_block(b, e, nc.s_assert_within(b - lo, 0, 3))
                expert_block(hi, e, nc.s_assert_within(hi - lo, 0, 3))
            dve.tensor_tensor(YACC, YACC, bt(MA), ALU.mult)
            dve.drain()
            residual(YACC)
            layer_norm(dve, X, X)
            gain_bias(X, "post2_g", "post2_b", None)
            if upto == 1:
                dve.sem_inc(ev("result_ready"), 1)
                return
            dve.sem_inc(ev("block1_done"), 1)
            dve.sem_inc(ev("lam_in"), 1)
            used(rms_norm(dve, row(2), X, vector(dve, "norm_in_g_2")))
            dve.drain()
            dve.sem_inc(ev("xn_ready"), 1)
            dve.wait_ge(ev("lam_ln"), 1)
            dve.tensor_scalar(LS[:, 2], LS[:, 0], 1.0, -1.0, ALU.add, ALU.add)
            dve.tensor_tensor(LS[:, 1], LS[:, 1], LS[:, 0], ALU.mult)
            dve.drain()
            dve.tensor_scalar(LS[:, 3], LS[:, 2], 0.0, None, ALU.is_equal)
            dve.drain()
            dve.tensor_tensor(LS[:, 2], LS[:, 2], LS[:, 3], ALU.add)
            dve.tensor_tensor(LS[:, 3], LS[:, 3], LS[:, 0], ALU.mult)
            dve.drain()
            dve.reciprocal(LS[:, 2], LS[:, 2])
            dve.drain()
            dve.tensor_tensor(LS[:, 1], LS[:, 1], LS[:, 2], ALU.mult)
            dve.tensor_scalar(LS[:, 4], pcol(R_LAM, 8), -1.0, 0.0, ALU.mult, ALU.max)
            dve.drain()
            dve.tensor_tensor(LS[:, 1], LS[:, 1], LS[:, 3], ALU.add)
            dve.drain()
            dve.tensor_tensor(LS[:, 1], LS[:, 1], LS[:, 4], ALU.add)
            dve.drain()
            dve.tensor_scalar(LS[:, 4], LS[:, 1], -8.0, None, ALU.mult)
            dve.tensor_scalar(LS[:, 5], LS[:, 1], -16.0, None, ALU.mult).then_inc(ev("rates_ready"), 1)
            dve.wait_ge(unit_free[UNIT["xl0"][0] % 2], UNIT["xl0"][0] // 2 + 1)
            dve.wait_ge(unit_free[UNIT["xl1"][0] % 2], UNIT["xl1"][0] // 2 + 1)
            for lag in range(CONV2):
                for k in range(KT):
                    w_ = pcol(R_CW2 + (CONV2 - 1 - lag) * KT + k)
                    if lag == 0:
                        ins = dve.tensor_scalar(XC[:, k, :], XLC[:, k, :], w_, pcol(R_CB2 + k), ALU.mult, ALU.add)
                    else:
                        ins = dve.scalar_tensor_tensor(XC[:, k, lag:], XLC[:, k, 0:T - lag], w_, XC[:, k, lag:],
                                                       ALU.mult, ALU.add)
                if lag == CONV2 - 1:
                    ins.then_inc(ev("xc_ready"), 1)
                dve.drain()
            dve.wait_ge(ev("tables_landed"), 80)

            def rotary(name, dst, i):
                wait_unit(dve, name)
                for t in range(TT):
                    x = unit_ps(name)[:, t, :].rearrange("p (h d) -> p h d", h=4)
                    d = dst[:, t, i * CH:(i + 1) * CH].rearrange("p (h d) -> p h d", h=4)
                    tm = V2[:, t, :].rearrange("p (a h d) -> p a h d", a=4, h=4)
                    cos = ROT[:, t, 0:64].unsqueeze(1).to_broadcast([P, 4, 64])
                    sin = ROT[:, t, 64:128].unsqueeze(1).to_broadcast([P, 4, 64])
                    dve.tensor_tensor(tm[:, 0], x[:, :, 0:64], cos, ALU.mult)
                    dve.tensor_tensor(tm[:, 1], x[:, :, 64:128], sin, ALU.mult)
                    dve.tensor_tensor(tm[:, 2], x[:, :, 0:64], sin, ALU.mult)
                    ins = dve.tensor_tensor(tm[:, 3], x[:, :, 64:128], cos, ALU.mult)
                    if t == 1:
                        free_unit(ins, name)
                    dve.drain()
                    dve.tensor_tensor(d[:, :, 0:64], tm[:, 0], tm[:, 1], ALU.subtract)
                    dve.tensor_tensor(d[:, :, 64:128], tm[:, 2], tm[:, 3], ALU.add)
                    dve.drain()

            rotary("q20", Q2, 0)
            rotary("q21", Q2, 1)
            dve.sem_inc(ev("q_ready"), 1)
            dve.wait_ge(ev("gates_read"), 8)
            dve.tensor_tensor(I2, I2, XC, ALU.mult).then_inc(ev("ix_ready"), 1)
            rotary("k20", K2, 0)
            dve.wait_ge(ev("a_ready"), 1)
            dve.tensor_scalar(R2, R2, 1.0, None, ALU.min).then_inc(ev("a2_clipped"), 1)
            rotary("k21", K2, 1)
            dve.sem_inc(ev("k_ready"), 1)
            dve.wait_ge(ev("mult_ready"), 1)
            dve.tensor_tensor(I2, I2, R2, ALU.mult)
            dve.drain()
            for k in range(KT):
                dve.tensor_tensor_scan(R2[:, k, :], XC[:, k, :], I2[:, k, :], 0.0, ALU.mult, ALU.add)
            dve.drain()
            dve.tensor_tensor(R2, R2, GLC, ALU.mult).then_inc(ev("yl_ready"), 1)
            dve.wait_ge(ev("decay_landed"), 16)
            for h in range(8):
                dve.wait_ge(ev("scores_done"), h + 1)
                if h >= 2:
                    dve.wait_ge(ev("o_done"), h - 1)
                dve.tensor_tensor(SCT[:, h % 2, :], PS[:, 6 + h % 2, 0:T + P], DEC[:, h, :], ALU.mult) \
                    .then_inc(ev("scores_masked"), 1)
                if h >= 1:
                    dve.wait_ge(ev("o_copied"), h)
                    for t in range(TT):
                        dve.bn_stats(HST[:, 2 * (h - 1) + t, :], O2[:, t, (h - 1) * P:h * P])
            dve.wait_ge(ev("o_copied"), 8)
            for t in range(TT):
                dve.bn_stats(HST[:, 14 + t, :], O2[:, t, 7 * P:8 * P])
            dve.drain()
            for j in range(16):
                dve.bn_aggr(HMV[:, j, :], HST[:, j, :])
            dve.drain()
            dve.tensor_scalar_add(HVE[:], HMV[:, :, 1], RMS_EPS).then_inc(ev("hvar_ready"), 1)
            dve.wait_ge(ev("hstd_ready"), 1)
            dve.reciprocal(HRS[:], HSD[:])
            dve.drain()
            for j in range(16):
                o = O2[:, j % 2, (j // 2) * P:(j // 2 + 1) * P]
                dve.tensor_scalar(o, o, HMV[:, j, 0:1], HRS[:, j:j + 1], ALU.subtract, ALU.mult)
            dve.drain()
            dve.tensor_tensor(O2, O2, GR, ALU.mult).then_inc(ev("yr_ready"), 1)

            def add_to_x(name, i):
                wait_unit(dve, name)
                xs = X[:, :, i * CH:(i + 1) * CH]
                free_unit(dve.tensor_tensor(xs, xs, unit_ps(name), ALU.add), name)

            add_to_x("w2o0", 0)
            add_to_x("w2o1", 1)
            dve.drain()
            used(rms_norm(dve, X, X, vector(dve, "norm_out_g_2")))
            dve.drain()
            if upto == 2:
                dve.sem_inc(ev("result_ready"), 1)
                return
            used(rms_norm(dve, row(9), X, vector(dve, "gla_norm_3")))
            dve.drain()
            dve.sem_inc(ev("hg_ready"), 1)
            dve.memset(ATT, 0.0)
            dve.wait_ge(ev("gate_done"), 1)
            for h in range(GLA_H):
                ins = dve.tensor_scalar(LA[:, h, :], PS[:, 6 + h // 2, (h % 2) * T:(h % 2 + 1) * T], pcol(R_BG + h), None, ALU.add)
            ins.then_inc(ev("gate_x"), 1)
            dve.wait_ge(ev("gate_ln"), 1)
            dve.scalar_tensor_tensor(LA, LA, 0.0, BC, ALU.min, ALU.subtract)
            dve.drain()
            dve.tensor_scalar(LA, LA, 1.0 / GLA_TAU, None, ALU.mult)
            dve.drain()
            for h in range(GLA_H):
                dve.tensor_tensor_scan(BC[:, h, :], SEG, LA[:, h, :], 0.0, ALU.mult, ALU.add)
            dve.drain()
            for h in range(GLA_H):
                b = BC[:, h, :].rearrange("p (n c) -> p n c", c=GLA_C)
                ins = dve.tensor_tensor(LA[:, h, :].rearrange("p (n c) -> p n c", c=GLA_C),
                                        b[:, :, GLA_C - 1:GLA_C].to_broadcast([P, 4, GLA_C]), b, ALU.subtract)
            ins.then_inc(ev("bcum_ready"), 1)
            dve.wait_ge(ev("exps_ready"), 1)
            dve.tensor_tensor(GQ, GQ, TE, ALU.mult).then_inc(ev("qg_ready"), 1)
            dve.tensor_tensor(KE, GK, LA, ALU.mult).then_inc(ev("kend_ready"), 1)
            dve.wait_ge(ev("expn_ready"), 1)
            dve.tensor_tensor(GK, GK, TE, ALU.mult).then_inc(ev("qk_ready"), 1)
            dve.wait_ge(ev("att_done"), 1)
            dve.copy_predicated(ATT.rearrange("p t h c -> p (t h) c"), MASK[:].unsqueeze(1).to_broadcast([P, 8, GLA_C]),
                                PS[:, 6, :].rearrange("p (a c) -> p a c", a=8)).then_inc(ev("att_masked"), 1)
            for n_ in range(3):
                for h in range(GLA_H):
                    dve.wait_ge(ev("kv_done"), n_ * GLA_H + h + 1)
                    if n_ == 0:
                        ins = dve.tensor_copy(GS[:, h, :], PS[:, 4 + h, :])
                    else:
                        ins = dve.scalar_tensor_tensor(GS[:, h, :], GS[:, h, :], DC4[:, h, n_:n_ + 1], PS[:, 4 + h, :],
                                                       ALU.mult, ALU.add)
                    ins.then_inc(ev("state_ready"), 1)
                dve.drain()
            for t in range(TT):
                for h in range(GLA_H):
                    dve.wait_ge(ev("og_copied"), t * GLA_H + h + 1)
                    dve.bn_stats(HST[:, t * GLA_H + h, :], OG[t][:, h * GLA_DV:(h + 1) * GLA_DV])
            dve.drain()
            for j in range(8):
                dve.bn_aggr(HMV[:, j, :], HST[:, j, :])
            dve.drain()
            dve.tensor_tensor(HVE[:, 0:8], HMV[:, 0:8, 0], HMV[:, 0:8, 0], ALU.mult)
            dve.drain()
            dve.scalar_tensor_tensor(HVE[:, 0:8], HVE[:, 0:8], RMS_EPS, HMV[:, 0:8, 1], ALU.add, ALU.add) \
                .then_inc(ev("hvar_ready"), 1)
            dve.wait_ge(ev("hstd_ready"), 2)
            dve.reciprocal(HRS[:, 0:8], HSD[:, 0:8])
            dve.drain()
            vec = vector(dve, "gla_head_gain_3")
            for t in range(TT):
                for h in range(GLA_H):
                    o = OG[t][:, h * GLA_DV:(h + 1) * GLA_DV]
                    j = t * GLA_H + h
                    ins = dve.scalar_tensor_tensor(o, o, HRS[:, j:j + 1], vec, ALU.mult, ALU.mult)
            used(ins)
            dve.drain()
            dve.wait_ge(ev("gz_ready"), 4)
            for t in range(TT):
                ins = dve.tensor_tensor(OG[t], OG[t], GZ[:, t, :], ALU.mult)
            ins.then_inc(ev("og_ready"), 1)
            add_to_x("go0", 0)
            add_to_x("go1", 1)
            dve.drain()
            if upto == 3:
                dve.sem_inc(ev("result_ready"), 1)
                return
            used(rms_norm(dve, row(9), X, vector(dve, "s5_norm_3")))
            dve.drain()
            dve.sem_inc(ev("hs_ready"), 1)
            dve.wait_ge(ev("uz_ready"), 1)
            dve.wait_ge(ev("dt_ready"), 1)
            dt, xr, xt, ex, s1, sh = work[0:6]
            re, im = PC[:, 3, 0:64], PC[:, 3, 64:128]
            dve.tensor_tensor(xr, re, dt, ALU.mult)
            dve.tensor_tensor(xt, im, dt, ALU.mult)
            dve.drain()
            dve.tensor_scalar(xt, xt, INV_2PI, None, ALU.mult)
            dve.drain()
            dve.tensor_scalar(TH, xt, MAGIC, None, ALU.add)
            dve.drain()
            dve.tensor_scalar(TH, TH, MAGIC, None, ALU.subtract)
            dve.drain()
            dve.tensor_tensor(TH, xt, TH, ALU.subtract).then_inc(ev("turns_ready"), 1)
            xc, po, mk = work[6], work[7], work[8]
            dve.tensor_scalar(xc, xr, -0.5, 0.5, ALU.max, ALU.min)
            dve.drain()
            dve.tensor_scalar(po, xc, 1.0 / 9, 1.0, ALU.mult, ALU.add)
            dve.drain()
            for j in range(8, 1, -1):
                dve.tensor_tensor(po, po, xc, ALU.mult)
                dve.drain()
                dve.tensor_scalar(po, po, 1.0 / j, 1.0, ALU.mult, ALU.add)
                dve.drain()
            dve.tensor_tensor(po, po, xc, ALU.mult)
            dve.tensor_tensor(mk, xr, xc, ALU.is_equal)
            dve.wait_ge(ev("coef_trig"), 1)
            dve.tensor_scalar_add(ex, ex, -1.0)
            dve.drain()
            dve.copy_predicated(ex, mk.bitcast(I32), po)
            dve.drain()
            dve.tensor_scalar_add(RR, ex, 1.0)
            s2, a_, b_, m_, t_ = work[9:14]
            dve.tensor_tensor(s2, sh, sh, ALU.mult)
            dve.drain()
            dve.tensor_tensor(b_, RR, s1, ALU.mult)
            dve.tensor_tensor(a_, RR, s2, ALU.mult)
            dve.drain()
            dve.scalar_tensor_tensor(a_, a_, -2.0, ex, ALU.mult, ALU.add)
            dve.tensor_tensor(m_, re, re, ALU.mult)
            dve.tensor_tensor(t_, im, im, ALU.mult)
            dve.drain()
            dve.tensor_tensor(m_, m_, t_, ALU.add)
            dve.drain()
            dve.reciprocal(m_, m_)
            dve.tensor_tensor(CRE, a_, re, ALU.mult)
            dve.tensor_tensor(t_, b_, im, ALU.mult)
            dve.tensor_tensor(CIM, b_, re, ALU.mult)
            dve.tensor_tensor(a_, a_, im, ALU.mult)
            dve.drain()
            dve.tensor_tensor(CRE, CRE, t_, ALU.add)
            dve.tensor_tensor(CIM, CIM, a_, ALU.subtract)
            dve.drain()
            dve.tensor_tensor(CRE, CRE, m_, ALU.mult)
            dve.tensor_tensor(CIM, CIM, m_, ALU.mult)
            dve.drain()
            dve.wait_ge(ev("s5_bc_landed"), 96)
            b3 = [CRE.unsqueeze(2).to_broadcast([P, 64, S5_I]), CIM.unsqueeze(2).to_broadcast([P, 64, S5_I])]
            t1 = BIG[:, 0:D].rearrange("p (g i) -> p g i", g=64)
            t2 = BIG[:, D:2 * D].rearrange("p (g i) -> p g i", g=64)
            dve.tensor_tensor(t1, BB[:, 0], b3[1], ALU.mult)
            dve.tensor_tensor(t2, BB[:, 1], b3[1], ALU.mult)
            dve.tensor_tensor(BB[:, 0], BB[:, 0], b3[0], ALU.mult)
            dve.tensor_tensor(BB[:, 1], BB[:, 1], b3[0], ALU.mult)
            dve.drain()
            dve.tensor_tensor(BB[:, 0], BB[:, 0], t2, ALU.subtract)
            dve.tensor_tensor(BB[:, 1], BB[:, 1], t1, ALU.add)
            dve.drain()
            dve.sem_inc(ev("coef_ready"), 1)
            iota_t = K[:, C_T:C_T + T]
            dve.sem_inc(ev("s5_bu_read"), 1)
            with dve.Fori(0, S5_CT) as ct:
                dve.wait_ge(ev("s5_in_ready"), ct + 1)
                for hb in range(2):
                    dve.wait_ge(ev("s5_half_done"), ct * 2 + (hb + 1))
                    if hb == 0:
                        dve.wait_ge(ev("s5_gelu"), ct + 1)
                    for j in range(2):
                        dve.tensor_scalar(SA1[:, j, :], iota_t, TC[:, 0, 2 * hb + j:2 * hb + j + 1], MAGIC, ALU.mult, ALU.add)
                    dve.drain()
                    dve.tensor_scalar(SA2, SA1, MAGIC, None, ALU.subtract)
                    dve.drain()
                    for j in range(2):
                        ins = dve.scalar_tensor_tensor(SA1[:, j, :], iota_t, TC[:, 0, 2 * hb + j:2 * hb + j + 1], SA2[:, j, :],
                                                       ALU.mult, ALU.subtract)
                    ins.then_inc(ev("s5_turns"), 1)
                    dve.wait_ge(ev("s5_bu_done"), ct + 1)
                    dve.wait_ge(ev("s5_trig"), ct * 2 + hb + 1)
                    bre, bim = PS[:, 2 * hb:2 * hb + 2, 0:T], PS[:, 2 * hb:2 * hb + 2, T:2 * T]
                    dve.tensor_tensor(SA1, bre, SCOS, ALU.mult)
                    dve.tensor_tensor(SA2, bim, SSIN, ALU.mult)
                    dve.tensor_tensor(SB1, bim, SCOS, ALU.mult)
                    ins = dve.tensor_tensor(SB2, bre, SSIN, ALU.mult)
                    if hb == 1:
                        ins.then_inc(ev("s5_bu_read"), 1)
                    dve.drain()
                    dve.tensor_tensor(SA1, SA1, SA2, ALU.add)
                    dve.tensor_tensor(SB1, SB1, SB2, ALU.subtract)
                    dve.drain()
                    for j in range(2):
                        r_ = TC[:, 1, 2 * hb + j:2 * hb + j + 1].to_broadcast([P, T])
                        dve.tensor_tensor_scan(SA2[:, j, :], r_, SA1[:, j, :], 0.0, ALU.mult, ALU.add)
                        dve.tensor_tensor_scan(SB2[:, j, :], r_, SB1[:, j, :], 0.0, ALU.mult, ALU.add)
                    dve.drain()
                    dve.tensor_tensor(SA1, SCOS, SA2, ALU.mult)
                    dve.tensor_tensor(SB1, SCOS, SB2, ALU.mult)
                    dve.drain()
                    dve.tensor_tensor(SA2, SSIN, SA2, ALU.mult)
                    dve.tensor_tensor(SB2, SSIN, SB2, ALU.mult).then_inc(ev("s5_prod_ready"), 1)
                dve.wait_ge(ev("s5_half_done"), ct * 2 + 3)
                dve.scalar_tensor_tensor(SA1[:, 0, :], UC, DCOL, PS[:, 6, 0:T], ALU.mult, ALU.add).then_inc(ev("s5_y_ready"), 1)
            dve.wait_ge(ev("glu_sig"), 1)
            dve.tensor_tensor(U16, U16, Y16, ALU.mult)
            dve.drain()
            dve.tensor_tensor(U16, U16, Z16, ALU.mult).then_inc(ev("glu_ready"), 1)
            add_to_x("so0", 0)
            add_to_x("so1", 1)
            dve.drain()
            used(rms_norm(dve, X, X, vector(dve, "final_norm_3")))
            dve.drain()
            dve.sem_inc(ev("result_ready"), 1)


INPUTS = ["x", "c", "w_mod", "b_mod", "w_in", "b_in", "conv_w", "conv_b", "ln_a_g", "ln_a_b", "w_a", "b_a",
          "ln_v_g", "ln_v_b", "w_s", "b_s", "w_b", "b_b", "w_out", "b_out", "post1_g", "post1_b", "w_router",
          "b_router", "w_gu", "b_gu", "w_dn", "b_dn", "post2_g", "post2_b", "norm_in_g_2", "w_in_2", "conv_w_2",
          "conv_b_2", "gate_a_w_2", "gate_a_b_2", "gate_x_w_2", "gate_x_b_2", "lru_lambda_2", "w_out_2",
          "norm_out_g_2", "gla_norm_3", "gla_w_in_3", "gla_w_gate_up_3", "gla_b_gate_3", "gla_head_gain_3",
          "gla_w_out_3", "s5_norm_3", "s5_w_in_3", "s5_lam_re_3", "s5_lam_im_3", "s5_log_dt_3", "s5_b_re_3",
          "s5_b_im_3", "s5_c_re_3", "s5_c_im_3", "s5_d_3", "s5_w_glu_3", "s5_b_glu_3", "s5_w_out_3", "final_norm_3"]


def kernel(**inputs):
    import concourse.bacc as bacc
    from concourse.bass_utils import run_bass_kernel_spmd

    nc = bacc.Bacc("TRN2", target_bir_lowering=False, num_devices=1)
    arrays, A = {}, {}
    for name, a in [(n, inputs[n]) for n in INPUTS] + list(constants().items()):
        a = np.ascontiguousarray(a)
        arrays[f"in_{name}"] = a
        A[name] = nc.dram_tensor(f"in_{name}", a.shape, mybir.dt.from_np(a.dtype), kind="ExternalInput").ap()
    out = nc.dram_tensor("out", (1, T, D), F32, kind="ExternalOutput").ap()
    build(nc, A, out)
    r = run_bass_kernel_spmd(nc, [arrays], core_ids=[0])
    return r.results[0]["out"]
```

```python
from contextlib import ExitStack

import numpy as np

import concourse.bass as bass
from concourse import mybir

F32 = mybir.dt.float32
I32 = mybir.dt.int32
U32 = mybir.dt.uint32
ALU = mybir.AluOpType
ACT = mybir.ActivationFunctionType

P = 128
T = 256
TT = T // P
D = 1024
KT = D // P
CH = 512
RING = 6
NV = 2
ROW = TT * D

CONV1, CONV2 = 31, 4
NE, TOPK = 32, 4
BLK = 64
ALPHA = float(2 ** 0.25)
LN_EPS, RMS_EPS = 1e-5, 1e-6
GLA_H, GLA_DK, GLA_DV, GLA_C, GLA_R = 4, 128, 512, 64, 16
GLA_TAU = 16.0
S5_CT, S5_P, S5_I = 16, 64, 16
PAIRS = 4
MAGIC = 12582912.0
TWO_PI = 6.283185
INV_2PI = 0.15915494309189535
HALF_PI = 1.5707963

C_ID, C_TRI, C_SLOT, C_E, C_T = 0, 128, 256, 256 + 4 * P, 256 + 4 * P + NE
C_N = C_T + T
R_C, R_AV, R_AG, R_CB, R_BS = 0, 8, 16, 24, 32
R_CW2, R_CB2, R_GAB, R_GXB, R_LAM, R_BG, R_GLU = 40, 72, 80, 88, 96, 104, 108
R_N0 = 124
N_PARAM = 18


def constants():
    c = np.zeros((P, C_N), np.float32)
    c[:, C_ID:C_ID + P] = np.eye(P)
    c[:, C_TRI:C_TRI + P] = np.triu(np.ones((P, P)), 1)
    c[:, C_SLOT:C_SLOT + 4 * P] = (np.arange(4)[:, None] * BLK + np.arange(P) % BLK).reshape(-1)
    c[:, C_E:C_E + NE] = np.arange(NE)
    c[:, C_T:C_T + T] = np.arange(T)
    half = P // 2
    inv = 10000.0 ** (-np.arange(0, P, 2, dtype=np.float32) / P)
    ang = np.arange(T, dtype=np.float32)[:, None] * inv[None, :].astype(np.float32)
    rot = np.concatenate([np.cos(ang), np.sin(ang)], 1).astype(np.float32)
    log_g = np.log1p(-np.exp2(-5.0 - np.arange(8, dtype=np.float64)))
    k = np.arange(P)[:, None]
    q = np.arange(T)[None, :]
    dec = np.zeros((P, 8, T + P))
    for h in range(8):
        full = np.where(q >= k, np.exp(np.maximum(q - k, 0) * log_g[h]), 0.0) * P ** -0.5
        dec[:, h, 0:T] = full
        dec[:, h, T:] = full[:, 0:P]
    s = np.arange(P)[:, None] % GLA_C
    m = (np.arange(GLA_C)[None, :] >= s).astype(np.int32)
    seg = (np.arange(T) % GLA_C != 0).astype(np.float32)
    seg = np.broadcast_to(seg, (P, T)).copy()
    assert half == 64
    return {"k_const": c, "k_rot": rot, "k_decay": dec.astype(np.float32).reshape(P, -1),
            "k_causal": np.ascontiguousarray(m), "k_seg": seg}


def plan():
    units = []

    def add(name, kind, mat, cols, rows=1):
        units.append((name, kind, [(mat, r * D, c) for c in cols for r in range(rows)]))

    def mod(name, i):
        add(name, "mod", "w_mod", [i * D, i * D + CH])

    mod("sc1", 1)
    mod("sh1", 0)
    for i in range(2):
        add(f"ag{i}", "col", "w_in", [D + i * CH])
        add(f"av{i}", "col", "w_in", [i * CH])
    for n, base in (("v", 3), ("u", 2), ("ga", 4), ("gb", 5)):
        for i in range(2):
            add(f"{n}{i}", "row", "w_in", [base * D + i * CH])
    for n, m in (("wb", "w_b"), ("wa", "w_a")):
        for i in range(2):
            add(f"{n}{i}", "row", m, [i * CH])
    mod("g1", 2)
    for i in range(2):
        add(f"wo{i}", "row", "w_out", [i * CH])
    mod("sc2", 4)
    mod("sh2", 3)
    mod("g2", 5)
    units.append(("moe", "moe", []))
    for n, base in (("xl", 4), ("gl", 5)):
        for i in range(2):
            add(f"{n}{i}", "col", "w_in_2", [base * D + i * CH])
    for n, base in (("q2", 0), ("k2", 1), ("v2", 2), ("gr", 3)):
        for i in range(2):
            add(f"{n}{i}", "row", "w_in_2", [base * D + i * CH])
    for i in range(2):
        add(f"w2o{i}", "row", "w_out_2", [i * CH], rows=2)
    add("gq", "col", "gla_w_in_3", [0])
    add("gk", "col", "gla_w_in_3", [CH])
    for i in range(4):
        add(f"gv{i}", "row", "gla_w_in_3", [D + i * CH])
    for i in range(4):
        add(f"gz{i}", "row", "gla_w_in_3", [3 * D + i * CH])
    for i in range(2):
        add(f"go{i}", "row", "gla_w_out_3", [i * CH], rows=2)
    for i in range(4):
        add(f"su{i}", "col", "s5_w_in_3", [i * CH])
    for i in range(4):
        add(f"sz{i}", "col", "s5_w_in_3", [2 * D + i * CH])
    for i in range(4):
        add(f"sg{i}", "col", "s5_w_glu_3", [i * CH], rows=2)
    for i in range(2):
        add(f"so{i}", "row", "s5_w_out_3", [i * CH], rows=2)
    return units


TRANSPOSES = [("params", 2), ("ws", 2), ("h1", 4), ("conv", 4), ("yb", 4), ("ya", 4), ("m", 4), ("h2", 4),
              ("xn", 4), ("q", 4), ("k", 4), ("yr", 4), ("hg", 4), ("kend", 2), ("og", 8), ("hs", 4)]

VECTORS = [("b_mod", D, D), ("b_mod", 0, D),
           ("b_in", 3 * D, D), ("b_in", 2 * D, D), ("b_in", 4 * D, D), ("b_in", 5 * D, D),
           ("ln_v_g", 0, D), ("ln_v_b", 0, D), ("b_b", 0, D), ("ln_a_g", 0, D), ("ln_a_b", 0, D), ("b_a", 0, D),
           ("b_mod", 2 * D, D), ("b_out", 0, D), ("post1_g", 0, D), ("post1_b", 0, D),
           ("b_mod", 4 * D, D), ("b_mod", 3 * D, D), ("b_mod", 5 * D, D),
           ("post2_g", 0, D), ("post2_b", 0, D), ("norm_in_g_2", 0, D), ("norm_out_g_2", 0, D),
           ("gla_norm_3", 0, D), ("gla_head_gain_3", 0, GLA_DV), ("s5_norm_3", 0, D), ("final_norm_3", 0, D)]


def build(nc, A, out):
    units = plan()
    pre = sum(len(u[2]) for u in units[:[u[0] for u in units].index("moe")])
    assert pre % RING == 0
    UNIT, first_chunk, no, n = {}, {}, 0, 0
    for name, kind, chunks in units:
        if kind == "moe":
            n += 6 * NE
            continue
        UNIT[name] = (no, kind, chunks, n)
        no += 1
        n += len(chunks)
    TB, n = {}, 0
    for name, banks in TRANSPOSES:
        TB[name] = n
        n += banks

    mats = {k: A[k][0] for k in ("w_mod", "w_in", "w_b", "w_a", "w_out", "gla_w_in_3", "gla_w_out_3",
                                 "s5_w_in_3", "s5_w_glu_3", "s5_w_out_3")}
    mats["w_in_2"], mats["w_out_2"] = A["w_in_2"], A["w_out_2"]

    with ExitStack() as ctx:
        def sb(name, shape, dt=F32):
            return ctx.enter_context(nc.sbuf_tensor(name, shape, dt))

        def sem(name):
            return ctx.enter_context(nc.semaphore(name))

        W = sb("W", [P, RING, KT, CH])
        V = sb("V", [P, NV, D])
        BIG = sb("BIG", [P, 10 * ROW])
        X = sb("X", [P, TT, D])[:]
        K = sb("K", [P, C_N])
        PC = sb("PC", [P, 5, P])
        ST = sb("ST", [P, TT, 12])
        MV = sb("MV", [P, TT, 2])
        VE = sb("VE", [P, TT])
        SD = sb("SD", [P, TT])
        RS = sb("RS", [P, TT])
        HST = sb("HST", [P, 16, 6])
        HMV = sb("HMV", [P, 16, 2])
        HVE = sb("HVE", [P, 16])
        HSD = sb("HSD", [P, 16])
        HRS = sb("HRS", [P, 16])
        OW = sb("OW", [P, T])
        ONES, WGR = OW[:, 0:P], OW[:, P:T].rearrange("p (k r) -> p k r", k=KT)
        TAB2 = sb("TAB2", [P, D])
        CTW2 = sb("CTW2", [P, 2, 3, PAIRS, 2, S5_I])
        LS = sb("LS", [P, 6, KT])
        DC4 = sb("DC4", [P, GLA_H, T // GLA_C])
        PS = ctx.enter_context(nc.psum_tensor("PS", [P, 8, CH], F32))

        def flat(i, n=1):
            return BIG[:, i * ROW:(i + n) * ROW]

        def row(i):
            return flat(i).rearrange("p (t d) -> p t d", t=TT)

        def col(i, n=1):
            return flat(i, n).rearrange("p (k t) -> p k t", t=T)

        def half(i, h):
            return BIG[:, i * ROW + h * D:i * ROW + (h + 1) * D]

        ident = K[:, C_ID:C_ID + P]

        def pcol(r, n=1):
            return PC[:, r // P, r % P:r % P + n]

        x_landed, const_landed, param_landed = sem("x_landed"), sem("const_landed"), sem("param_landed")
        w_landed = [sem(f"w_landed{i}") for i in range(RING)]
        v_landed = [sem(f"v_landed{i}") for i in range(NV)]
        v_used = sem("v_used")
        chunk_done = sem("chunk_done")
        unit_free = [sem("unit_free0"), sem("unit_free1")]
        tp_ready, tp_copied = sem("tp_ready"), sem("tp_copied")
        var_ready, std_ready = sem("var_ready"), sem("std_ready")
        S = {}

        def ev(name):
            if name not in S:
                S[name] = sem(name)
            return S[name]

        block = ctx.enter_context(nc.Block())

        def slot(n):
            return W[:, n % RING]

        def unit_ps(name):
            u = UNIT[name][0]
            return PS[:, 2 * (u % 2):2 * (u % 2) + 2, :]

        def wait_unit(eng, name):
            _, _, chunks, c0 = UNIT[name]
            eng.wait_ge(chunk_done, c0 + len(chunks))

        def free_unit(ins, name):
            ins.then_inc(unit_free[UNIT[name][0] % 2], 1)

        vec_at = [0]

        def vector(dve, name):
            n = vec_at[0]
            assert VECTORS[n][0] == name, (VECTORS[n], name)
            vec_at[0] += 1
            dve.wait_ge(v_landed[n % NV], 16 * (n // NV + 1))
            return V[:, n % NV, 0:VECTORS[n][2]]

        def bt(v):
            return v.unsqueeze(1).to_broadcast([P, TT, v.shape[1]])

        ln_no = [0, 0]

        def norm_stats(dve, src):
            for t in range(TT):
                for h in range(2):
                    dve.bn_stats(ST[:, t, 6 * h:6 * h + 6], src[:, t, h * CH:(h + 1) * CH])
            dve.drain()
            for t in range(TT):
                dve.bn_aggr(MV[:, t, :], ST[:, t, :])
            dve.drain()

        def layer_norm(dve, dst, src):
            norm_stats(dve, src)
            dve.tensor_scalar_add(VE[:], MV[:, :, 1], LN_EPS).then_inc(var_ready, 1)
            ln_no[0] += 1
            dve.wait_ge(std_ready, ln_no[0])
            dve.reciprocal(RS[:], SD[:])
            dve.drain()
            for t in range(TT):
                dve.tensor_scalar(dst[:, t, :], src[:, t, :], MV[:, t, 0:1], RS[:, t:t + 1],
                                  ALU.subtract, ALU.mult)
            dve.drain()

        def rms_norm(dve, dst, src, gain):
            norm_stats(dve, src)
            dve.tensor_tensor(VE[:], MV[:, :, 0], MV[:, :, 0], ALU.mult)
            dve.drain()
            dve.scalar_tensor_tensor(VE[:], VE[:], RMS_EPS, MV[:, :, 1], ALU.add, ALU.add).then_inc(var_ready, 1)
            ln_no[0] += 1
            dve.wait_ge(std_ready, ln_no[0])
            dve.reciprocal(RS[:], SD[:])
            dve.drain()
            for t in range(TT):
                ins = dve.scalar_tensor_tensor(dst[:, t, :], src[:, t, :], RS[:, t:t + 1], gain, ALU.mult, ALU.mult)
            return ins

        def act_std(act):
            ln_no[1] += 1
            act.wait_ge(var_ready, ln_no[1])
            act.activation(SD[:], VE[:], ACT.Sqrt).then_inc(std_ready, 1)

        def copy_columns(act, name, dst, kts=KT):
            per = kts // 4
            for b in range(TT * per):
                t, h = b // per, b % per
                act.wait_ge(tp_ready, TB[name] + b + 1)
                act.activation(dst[:, 4 * h:4 * h + 4, t * P:(t + 1) * P],
                               PS[:, 4 + (TB[name] + b) % 2, :].rearrange("p (k t) -> p k t", k=4),
                               ACT.Copy).then_inc(tp_copied, 1)

        @block.sync
        def _(sp):
            sp.dma_start(K[:], A["k_const"]).then_inc(const_landed, 16)
            sp.dma_start(X, A["x"][0].rearrange("(t p) d -> p t d", p=P)).then_inc(x_landed, 16)
            sp.wait_ge(param_landed, 16 * N_PARAM)
            sp.wait_ge(ev("ws_landed"), 16)
            for name, kind, chunks in units:
                if kind == "moe":
                    with sp.Fori(0, NE) as e:
                        gu = A["w_gu"][0, bass.ds(e, 1)].rearrange("e (k p) n -> p (e k) n", p=P)
                        dn = A["w_dn"][0, bass.ds(e, 1)].rearrange("e (k p) n -> p (e k) n", p=P)
                        for j in range(6):
                            sp.wait_ge(chunk_done, e * 6 + (pre + j - RING + 1))
                            src = gu[:, :, j * CH:(j + 1) * CH] if j < 4 else dn[:, :, (j - 4) * CH:(j - 3) * CH]
                            sp.dma_start(W[:, j], src).then_inc(w_landed[j], 16)
                    continue
                c0 = UNIT[name][3]
                for i, (mat, r, c) in enumerate(chunks):
                    n = c0 + i
                    if n >= RING:
                        sp.wait_ge(chunk_done, n - RING + 1)
                    sp.dma_start(slot(n), mats[mat][r:r + D, c:c + CH].rearrange("(k p) n -> p k n", p=P)) \
                        .then_inc(w_landed[n % RING], 16)
            sp.wait_ge(ev("result_ready"), 1)
            sp.dma_start(out[0].rearrange("(t p) d -> p t d", p=P), X).then_inc(ev("result_stored"), 16)
            sp.wait_ge(ev("result_stored"), 16)

        HT, HT2, HN, AUX, CV, U, VV, GA, GB = 0, 1, 2, 3, 4, 5, 6, 7, 8
        WST = half(AUX, 0).rearrange("p (g i) -> p g i", g=8)
        CB = half(AUX, 1).rearrange("p (k m) -> p k m", k=KT)
        WSR = half(GB, 0).rearrange("p (g i) -> p g i", g=8)
        PVR = BIG[:, CV * ROW:CV * ROW + 5 * P].rearrange("p (a b) -> p a b", a=5)
        LDT = BIG[:, CV * ROW + 5 * P:CV * ROW + 5 * P + 2]
        MA, MB = half(9, 0), half(9, 1)
        H2, H2T, YACC = row(0), col(1), row(2)
        BGU = BIG[0:NE, 4 * ROW:5 * ROW]
        E5 = 5 * ROW
        XET = BIG[:, E5:E5 + 512].rearrange("p (k s) -> p k s", k=KT)
        ACTT = BIG[:, E5 + 512:E5 + 1024].rearrange("p (k s) -> p k s", k=KT)
        YE = BIG[:, E5 + 1024:E5 + 1536]
        G = BIG[:, E5 + 1536:E5 + 1664].rearrange("p (t s) -> p t s", t=TT)
        GW = BIG[:, E5 + 1664:E5 + 1920].rearrange("p (t s) -> p t s", t=TT)
        SELB = BIG[0:NE, E5 + 1920:E5 + 1984]
        XR, XETX, ACTV = BIG[:, ROW:ROW + 512], BIG[:, ROW + 512:ROW + 1024].rearrange("p (k s) -> p k s", k=KT), \
            BIG[:, ROW + 1024:ROW + 1536]
        SCX = BIG[:, ROW + 1536:ROW + 1792]
        GX = BIG[:, 3 * ROW:3 * ROW + 128].rearrange("p (t s) -> p t s", t=TT)
        GWX = BIG[:, 3 * ROW + 128:3 * ROW + 384].rearrange("p (t s) -> p t s", t=TT)
        E6 = 6 * ROW
        GT, SG, UP = (BIG[:, E6 + i * 512:E6 + (i + 1) * 512] for i in range(3))
        SC = BIG[:, E6 + 1536:E6 + 1792]
        WR = BIG[:, E6 + 1792:E6 + 2048].rearrange("p (k e) -> p k e", k=KT)
        BDN = BIG[0:NE, 7 * ROW:7 * ROW + D]
        E7 = 7 * ROW + D

        def small(i, n=NE, tt=TT):
            return BIG[:, E7 + 64 * i:E7 + 64 * i + n * tt].rearrange("p (t e) -> p t e", t=tt)
        LG, SEL, WM, POS, OH, BRT = (small(i) for i in range(6))
        SUMS, PW, V8, F8 = small(6), small(7, 2, 2), small(8, 8), small(9, 8)
        I8 = BIG[:, E7 + 640:E7 + 656].rearrange("p (t e) -> p t e", t=TT).bitcast(U32)
        NM, ES, ER = (BIG[:, E7 + 660 + 4 * i:E7 + 662 + 4 * i] for i in range(3))
        E4 = small(11, 4)
        TABF = BIG[0:1, E7 + 768:E7 + 768 + 3 * NE].rearrange("p (a e) -> p a e", a=3)
        TABI = BIG[0:1, E7 + 896:E7 + 896 + 2 * NE].rearrange("p (a e) -> p a e", a=2).bitcast(I32)
        WMT = BIG[0:NE, 8 * ROW:8 * ROW + T].rearrange("p (t s) -> p t s", t=TT)
        XC, R2, I2, QT, GLC = col(8), col(9), col(1), col(1), col(7)
        XLC, Q2, K2, V2 = col(5), row(2), row(3), row(4)
        GW2 = BIG[:, 6 * ROW:7 * ROW].rearrange("p (a n o) -> p a n o", a=2, n=8)
        KT2, GR, O2, YRT = col(8), row(5), row(0), col(3)
        DEC = BIG[:, 6 * ROW:6 * ROW + 8 * 384].rearrange("p (h q) -> p h q", h=8)
        SCT = BIG[:, 6 * ROW + 3072:6 * ROW + 3072 + 768].rearrange("p (b q) -> p b q", b=2)
        GQ = BIG[:, ROW:ROW + D].rearrange("p (h t) -> p h t", h=4)
        GK = BIG[:, ROW + D:2 * ROW].rearrange("p (h t) -> p h t", h=4)
        GV = BIG[:, 2 * ROW:4 * ROW].rearrange("p (t d) -> p t d", t=TT)
        GZ = BIG[:, 4 * ROW:6 * ROW].rearrange("p (t d) -> p t d", t=TT)
        LA = half(6, 0).rearrange("p (h t) -> p h t", h=4)
        BC = half(6, 1).rearrange("p (h t) -> p h t", h=4)
        TE = half(7, 0).rearrange("p (h t) -> p h t", h=4)
        KE = half(7, 1).rearrange("p (h t) -> p h t", h=4)
        KR = half(8, 0).rearrange("p (t f) -> p t f", t=TT)
        ATT = BIG[:, 8 * ROW + D:8 * ROW + D + 512].rearrange("p (t h c) -> p t h c", t=TT, h=4)
        GS = BIG[:, 9 * ROW:10 * ROW].rearrange("p (h e) -> p h e", h=4)
        OG = [BIG[:, 0:ROW], BIG[:, ROW:2 * ROW]]
        OGT = BIG[:, 2 * ROW:4 * ROW].rearrange("p (k t) -> p k t", t=T)
        MASK = CTW2[:, 0, 0].rearrange("p q b i -> p (q b i)")[:, 0:GLA_C].bitcast(I32)
        ROT = TAB2[:, 0:2 * P].rearrange("p (t c) -> p t c", t=TT)
        SEG = TAB2[:, 256:512]
        WGU = TAB2[0:GLA_R, 512:1024]
        RT = BIG[0:GLA_R, 7 * ROW:7 * ROW + T]
        U16, Z16, G16 = col(1, 2), col(3, 2), col(5, 2)
        BB = BIG[:, 7 * ROW:8 * ROW].rearrange("p (a g i) -> p a g i", a=2, g=64)
        CC = BIG[:, 8 * ROW:9 * ROW].rearrange("p (a c q) -> p a c q", a=2, c=S5_CT)
        B9 = 9 * ROW

        def cell(i):
            return BIG[:, B9 + 64 * i:B9 + 64 * i + 64]
        THR = BIG[:, B9:B9 + 128].rearrange("p (a g) -> p a g", a=2)
        TH, RR, CRE, CIM = (cell(i) for i in range(4))
        UC = [BIG[:, B9 + 256:B9 + 512], OW[:]]
        BTW = [BIG[:, B9 + 512 + i * 256:B9 + 768 + i * 256].rearrange("p (a m) -> p a m", a=2) for i in range(2)]
        CTW = [CTW2[:, i] for i in range(2)]
        TC = [BIG[:, B9 + 128 + 8 * i:B9 + 136 + 8 * i].rearrange("p (a q) -> p a q", a=2) for i in range(2)]
        DCOL = [BIG[:, B9 + 144 + i:B9 + 145 + i] for i in range(2)]
        iota_t = K[:, C_T:C_T + T]
        BD = K[:, C_SLOT:C_SLOT + 256].rearrange("p (a q b i) -> p a q b i", a=2, q=PAIRS, b=2)
        CS = K[:, C_SLOT + 256:C_SLOT + 512].rearrange("p (a b q) -> p a b q", a=2, b=2)
        free_v = V[:, (len(VECTORS) - 2) % NV, :]
        halves = [BIG[:, i * 512:(i + 1) * 512] for i in range(4)] + \
            [BIG[:, 5 * ROW + i * 512:5 * ROW + (i + 1) * 512] for i in range(8)] + \
            [TAB2[:, 0:512], TAB2[:, 512:1024], free_v[:, 0:512], free_v[:, 512:1024]] + \
            [BIG[:, B9 + D + i * 512:B9 + D + (i + 1) * 512] for i in range(2)]
        halves = [o.rearrange("p (q t) -> p q t", q=2) for o in halves]
        ANG, RND = halves[16], halves[17]
        IC, IS, JC, JS = halves[0:4]
        SCOS, SSIN = halves[4:6], halves[6:8]
        SA, SB, PA, PB = halves[8:10], halves[10:12], halves[12:14], halves[14:16]
        work = [BIG[:, 5 * ROW + i * 64:5 * ROW + (i + 1) * 64] for i in range(16)]

        @block.gpsimd
        def _(pool):
            for n, (name, off, length) in enumerate(VECTORS):
                src = A[name] if len(A[name].shape) == 1 else A[name][0]
                if n >= NV:
                    pool.wait_ge(v_used, n - NV + 1)
                pool.dma_start(V[:, n % NV, 0:length], src[off:off + length].unsqueeze(0).to_broadcast([P, length])) \
                    .then_inc(v_landed[n % NV], 16)
                if n == 16:
                    pool.wait_ge(ev("x1_ready"), 1)
                    pool.dma_start(BGU, A["b_gu"][0]).then_inc(ev("moe_small_landed"), 16)
                    pool.dma_start(BDN, A["b_dn"][0]).then_inc(ev("moe_small_landed"), 16)
                    pool.dma_start(WR, A["w_router"][0].rearrange("(k p) e -> p k e", p=P)).then_inc(ev("moe_small_landed"), 16)
                    pool.dma_start(BRT[:, 0, :], A["b_router"][0].unsqueeze(0).to_broadcast([P, NE])) \
                        .then_inc(ev("moe_small_landed"), 16)
                if n == 21:
                    pool.wait_ge(ev("block1_done"), 1)
                    for a, w in enumerate(("gate_a_w_2", "gate_x_w_2")):
                        pool.dma_start(GW2[:, a], A[w].rearrange("n i o -> i n o")).then_inc(ev("gate_w_landed"), 16)
                    pool.dma_start(ROT, A["k_rot"].rearrange("(t p) c -> p t c", p=P)).then_inc(ev("tables_landed"), 16)
                    pool.dma_start(SEG, A["k_seg"]).then_inc(ev("tables_landed"), 16)
                    pool.dma_start(WGU, A["gla_w_gate_up_3"][0]).then_inc(ev("tables_landed"), 16)
                    pool.dma_start(WGR, A["gla_w_in_3"][0][:, 5 * D:5 * D + GLA_R].rearrange("(k p) r -> p k r", p=P)) \
                        .then_inc(ev("tables_landed"), 16)
                    pool.dma_start(MASK, A["k_causal"]).then_inc(ev("tables_landed"), 16)
                if n == 22:
                    pool.wait_ge(ev("yl_ready"), 1)
                    pool.dma_start(DEC, A["k_decay"].rearrange("p (h q) -> p h q", h=8)).then_inc(ev("decay_landed"), 16)
                if n == 25:
                    pool.wait_ge(ev("og_ready"), 1)
                    for a, w in enumerate(("s5_b_re_3", "s5_b_im_3")):
                        for g in range(2):
                            pool.dma_start(BB[64 * g:64 * g + 64, a], A[w][0].rearrange("(a b) p i -> b p a i", b=2)[g]) \
                                .then_inc(ev("s5_bc_landed"), 16)
                    for a, w in enumerate(("s5_c_re_3", "s5_c_im_3")):
                        pool.dma_start(CC[:, a], A[w][0].rearrange("(c g) i q -> (g i) c q", g=8)).then_inc(ev("s5_bc_landed"), 16)
            pool.wait_ge(ev("coef_ready"), 1)
            pool.memset(K[:, C_SLOT:C_SLOT + 256], 0.0)
            pool.memset(CTW2[:].rearrange("p n a q b i -> p (n a q b i)"), 0.0).then_inc(ev("zeroed"), 1)
            pool.wait_ge(ev("zeroed"), 1)

            def rates(ct, par):
                pool.tensor_copy(TC[par], THR[:, :, bass.ds(ct * PAIRS, PAIRS)]).then_inc(ev("s5_copied"), 1)

            def sums(g):
                pool.wait_ge(ev("s5_in"), g + 1)
                pool.tensor_tensor(IC, IC, JS, ALU.add)
                pool.tensor_tensor(JC, JC, IS, ALU.subtract).then_inc(ev("s5_sums"), 1)

            def tile(ct, par, last):
                for hb in range(2):
                    g = ct * 2 + hb
                    if not last and hb == 0:
                        pool.wait_ge(ev("s5_scanned"), ct * 2 + 1)
                        rates(ct + 1, 1 - par)
                    pool.wait_ge(ev("s5_scanned"), g + 2)
                    pool.tensor_tensor(PB[hb], SCOS[hb], SB[hb], ALU.mult)
                    pool.drain()
                    pool.tensor_tensor(SB[hb], SSIN[hb], SB[hb], ALU.mult).then_inc(ev("s5_imag_out"), 1)
                    if not (last and hb == 1):
                        sums(g + 1)
                    if not last and hb == 1:
                        pool.wait_ge(ev("s5_y"), ct + 2)
                        pool.tensor_copy(DCOL[1 - par], PC[:, 4, bass.ds(ct + 65, 1)]).then_inc(ev("s5_skip"), 1)

            rates(0, 0)
            pool.tensor_copy(DCOL[0], PC[:, 4, 64:65]).then_inc(ev("s5_skip"), 1)
            sums(0)
            with pool.Fori(0, S5_CT // 2 - 1) as i:
                tile(i * 2, 0, False)
                tile(i * 2 + 1, 1, False)
            tile(S5_CT - 2, 0, False)
            tile(S5_CT - 1, 1, True)

        @block.tensor
        def _(pe):
            def dense(name, lhs):
                u, kind, chunks, c0 = UNIT[name]
                ps = unit_ps(name)
                if u >= 2:
                    pe.wait_ge(unit_free[u % 2], u // 2)
                if kind == "col":
                    for i in range(len(chunks)):
                        pe.wait_ge(w_landed[(c0 + i) % RING], 16 * ((c0 + i) // RING + 1))
                    for m in range(4):
                        for i in range(len(chunks)):
                            for k in range(KT):
                                ins = pe.matmul(ps[:, m // 2, (m % 2) * T:(m % 2 + 1) * T],
                                                slot(c0 + i)[:, k, m * P:(m + 1) * P], lhs(i * KT + k), start=i + k == 0,
                                                stop=i == len(chunks) - 1 and k == KT - 1, skip_group_check=True)
                    ins.then_inc(chunk_done, len(chunks))
                    return
                for i in range(len(chunks)):
                    n = c0 + i
                    pe.wait_ge(w_landed[n % RING], 16 * (n // RING + 1))
                    w = slot(n)
                    last_chunk = i == len(chunks) - 1
                    if kind == "mod":
                        for k in range(KT):
                            ins = pe.matmul(ps[:, i, :], CB[:, k, :], w[:, k, :], start=k == 0, stop=k == KT - 1)
                    else:
                        for t in range(TT):
                            for k in range(KT):
                                ins = pe.matmul(ps[:, t, :], lhs(i * KT + k)[:, t * P:(t + 1) * P], w[:, k, :],
                                                start=i + k == 0, stop=last_chunk and k == KT - 1)
                    ins.then_inc(chunk_done, 1)

            def turn(name, tiles):
                for b, bank in enumerate(tiles):
                    n = TB[name] + b
                    if n >= 2:
                        pe.wait_ge(tp_copied, n - 1)
                    for j, a in enumerate(bank):
                        r, c = a.shape
                        ins = pe.transpose(PS[0:c, 4 + n % 2, j * P:j * P + r], a, ident[0:r, 0:r])
                    ins.then_inc(tp_ready, 1)

            def rows_to_columns(name, src, kts=KT):
                turn(name, [[src[t][:, (4 * h + j) * P:(4 * h + j + 1) * P] for j in range(4)]
                            for t in range(TT) for h in range(kts // 4)])

            def columns_ready(name):
                pe.wait_ge(tp_copied, TB[name] + dict(TRANSPOSES)[name])

            pe.wait_ge(const_landed, 16)
            pe.wait_ge(param_landed, 16 * N_PARAM)
            pe.wait_ge(ev("log_dt_ready"), 1)
            turn("params", [[PVR[0:R_N0, 0, :], PVR[:, 1, :], PVR[0:120, 2, :], PVR[:, 3, :]], [PVR[0:80, 4, :]]])
            pe.wait_ge(ev("ws_landed"), 16)
            turn("ws", [[WSR[:, 4 * b + j, :] for j in range(4)] for b in range(2)])
            pe.wait_ge(ev("cond_ready"), 1)
            dense("sc1", None)
            dense("sh1", None)
            pe.wait_ge(ev("h1_ready"), 1)
            h1 = row(HN)
            rows_to_columns("h1", [h1[:, 0], h1[:, 1]])
            columns_ready("h1")
            hT = col(HT)
            lhs = lambda k: hT[:, k, :]
            for i in range(2):
                dense(f"ag{i}", lhs)
                dense(f"av{i}", lhs)
            for n_ in ("v", "u", "ga", "gb"):
                for i in range(2):
                    dense(f"{n_}{i}", lhs)
            pe.wait_ge(ev("wst_ready"), 1)
            pe.wait_ge(ev("vn_ready"), 1)
            vv = row(VV)
            for t in range(TT):
                if t:
                    pe.wait_ge(ev("mix_read"), t)
                for g in range(8):
                    ins = pe.matmul(PS[:, 6 + g // 4, (g % 4) * P:(g % 4 + 1) * P], WST[:, g, :],
                                    vv[:, t, g * P:(g + 1) * P], start=True, stop=True)
                ins.then_inc(ev("mix_done"), 1)
            pe.wait_ge(ev("conv_done"), 1)
            cv = col(CV)
            turn("conv", [[cv[:, 4 * h + j, t * P:(t + 1) * P] for j in range(4)] for t in range(TT) for h in range(2)])
            pe.wait_ge(ev("yb_ready"), 1)
            u = row(U)
            rows_to_columns("yb", [u[:, 0], u[:, 1]])
            columns_ready("yb")
            for i in range(2):
                dense(f"wb{i}", lhs)
            pe.wait_ge(ev("ya_ready"), 1)
            rows_to_columns("ya", [vv[:, 0], vv[:, 1]])
            columns_ready("ya")
            hT2 = col(HT2)
            for i in range(2):
                dense(f"wa{i}", lambda k: hT2[:, k, :])
            dense("g1", None)
            pe.wait_ge(ev("m_ready"), 1)
            ga = row(GA)
            rows_to_columns("m", [ga[:, 0], ga[:, 1]])
            columns_ready("m")
            for i in range(2):
                dense(f"wo{i}", lhs)
            dense("sc2", None)
            dense("sh2", None)
            dense("g2", None)
            pe.wait_ge(ev("h2_ready"), 1)
            rows_to_columns("h2", [H2[:, 0], H2[:, 1]])
            columns_ready("h2")
            pe.wait_ge(ev("moe_small_landed"), 64)
            for t in range(TT):
                for k in range(KT):
                    ins = pe.matmul(PS[:, 6, t * NE:(t + 1) * NE], H2T[:, k, t * P:(t + 1) * P], WR[:, k, :],
                                    start=k == 0, stop=k == KT - 1)
            ins.then_inc(ev("logits_done"), 1)
            pe.wait_ge(ev("sel_ready"), 1)
            pos = PS[:, 7, 0:3 * NE].rearrange("p (a e) -> p a e", a=3)
            pe.matmul(pos[:, 0, :], K[:, C_TRI:C_TRI + P], SEL[:, 0, :], start=True, stop=True)
            pe.matmul(pos[:, 1, :], K[:, C_TRI:C_TRI + P], SEL[:, 1, :], start=True, stop=False)
            pe.matmul(pos[:, 1, :], ONES, SEL[:, 0, :], start=False, stop=True)
            pe.matmul(pos[:, 2, :], ONES, SEL[:, 0, :], start=True, stop=False)
            pe.matmul(pos[:, 2, :], ONES, SEL[:, 1, :], start=False, stop=True)
            for t in range(TT):
                ins = pe.transpose(PS[0:NE, 7, P + t * P:P + (t + 1) * P], WM[:, t, :], ident)
            ins.then_inc(ev("pos_done"), 1)
            pe.wait_ge(ev("wmt_ready"), 1)
            pe.wait_ge(ev("table_ready"), 1)
            for t in range(TT):
                if t:
                    pe.wait_ge(ev("acc_started"), t)
                for h in range(2):
                    ins = pe.matmul(PS[:, 6 + h, :], WMT[:, t, :], BDN[:, h * CH:(h + 1) * CH], start=True, stop=True)
                ins.then_inc(ev("bias_sum_done"), 1)

            def turn_scatter(gw, done):
                for t in range(TT):
                    ins = pe.transpose(PS[:, 5, t * P:(t + 1) * P], gw[:, t, :], ident)
                ins.then_inc(done, 1)

            def gather_rows(e):
                pe.wait_ge(ev("g_ready"), e + 1)
                for t in range(TT):
                    for h in range(2):
                        ins = pe.matmul(PS[h * BLK:(h + 1) * BLK, 4, :], G[:, t, :], H2[:, t, h * CH:(h + 1) * CH],
                                        start=t == 0, stop=t == TT - 1, skip_group_check=True)
                ins.then_inc(ev("gathered"), 1)

            def turn_rows(e):
                pe.wait_ge(ev("xr_copied"), e + 1)
                for c in range(4):
                    ins = pe.transpose(PS[:, 4, c * P:(c + 1) * P], XR[:, c * P:(c + 1) * P], ident)
                ins.then_inc(ev("xr_turned"), 1)

            def projection(bank, w0, lhsT, c0, done, release):
                if c0 is not None:
                    for h in range(2):
                        ins = pe.matmul(PS[h * BLK:(h + 1) * BLK, bank, :], SELB, BGU[:, c0 + h * CH:c0 + (h + 1) * CH],
                                        start=True, stop=False, skip_group_check=True)
                        if release and h == 0:
                            ins.then_inc(chunk_done, 2)
                for k in range(KT):
                    for h in range(2):
                        ins = pe.matmul(PS[h * BLK:(h + 1) * BLK, bank, :], lhsT[:, k, :], W[:, w0 + h, k, :],
                                        start=c0 is None and k == 0, stop=k == KT - 1, skip_group_check=True)
                ins.then_inc(done, 1)

            def landed(e, part):
                for h in range(2):
                    pe.wait_ge(w_landed[2 * part + h], e * 16 + 16 * (pre // RING + 1))

            def extra_block(x, e):
                pe.wait_ge(ev("x_g_ready"), x + 1)
                for k in range(KT):
                    for t in range(TT):
                        ins = pe.matmul(PS[:, 4, k * BLK:(k + 1) * BLK], H2[:, t, k * P:(k + 1) * P], GX[:, t, :],
                                        start=t == 0, stop=t == TT - 1, skip_group_check=True)
                ins.then_inc(ev("x_gathered"), 1)
                turn_scatter(GWX, ev("x_scatter_turned"))
                pe.wait_ge(ev("x_xet_copied"), x + 1)
                landed(e, 0)
                projection(0, 0, XETX, 0, ev("x_gate_done"), False)
                landed(e, 1)
                projection(1, 2, XETX, D, ev("x_up_done"), False)
                pe.wait_ge(ev("x_act_ready"), x + 1)
                for c in range(4):
                    ins = pe.transpose(PS[:, 2, c * P:(c + 1) * P], ACTV[:, c * P:(c + 1) * P], ident)
                ins.then_inc(ev("x_act_turned"), 1)
                pe.wait_ge(ev("x_actt_copied"), x + 1)
                landed(e, 2)
                projection(3, 4, ACTT, None, ev("x_down_done"), False)
                pe.wait_ge(ev("x_ye_copied"), x + 1)
                for t in range(TT):
                    for h in range(2):
                        ins = pe.matmul(PS[:, 6 + h if t == 0 else h, :], SCX[h * BLK:(h + 1) * BLK, t * P:(t + 1) * P],
                                        YE[h * BLK:(h + 1) * BLK, :], start=True, stop=True)
                    ins.then_inc(ev("x_scattered"), 1)
                pe.wait_ge(ev("x_acc_added"), x * 2 + 2)

            def extras(e):
                lo = pe.value_load(TABI[0:1, 0, bass.ds(e, 1)], min_val=0, max_val=64)
                hi = pe.value_load(TABI[0:1, 1, bass.ds(e, 1)], min_val=0, max_val=64)
                with pe.If(hi - lo > 0):
                    with pe.Fori(lo, hi) as x:
                        pe.wait_ge(ev("acc_added"), e * 2 + 1)
                        pe.wait_ge(ev("sc_ready"), e + 1)
                        extra_block(x, e)

            def expert(e, last):
                extras(e)
                pe.wait_ge(ev("xet_ready"), e + 1)
                pe.wait_ge(ev("acc_added"), e * 2 + 1)
                landed(e, 0)
                projection(0, 0, XET, 0, ev("gate_done"), False)
                landed(e, 1)
                projection(1, 2, XET, D, ev("up_done"), True)
                if not last:
                    gather_rows(e + 1)
                    pe.wait_ge(ev("sc_ready"), e + 1)
                    turn_scatter(GW, ev("scatter_turned"))
                pe.wait_ge(ev("act_ready"), e + 1)
                for c in range(4):
                    ins = pe.transpose(PS[:, 2, c * P:(c + 1) * P], ACTV[:, c * P:(c + 1) * P], ident)
                    if c == 0:
                        ins.then_inc(chunk_done, 2)
                ins.then_inc(ev("act_turned"), 1)
                if not last:
                    turn_rows(e + 1)
                pe.wait_ge(ev("actt_copied"), e + 1)
                landed(e, 2)
                projection(3, 4, ACTT, None, ev("down_done"), False)
                pe.wait_ge(ev("ye_copied"), e + 1)
                pe.wait_ge(ev("sc_ready"), e + 1)
                for t in range(TT):
                    for h in range(2):
                        ins = pe.matmul(PS[:, 6 + h if t == 0 else h, :], SC[h * BLK:(h + 1) * BLK, t * P:(t + 1) * P],
                                        YE[h * BLK:(h + 1) * BLK, :], start=True, stop=True)
                        if t == 0 and h == 0:
                            ins.then_inc(chunk_done, 2)
                    ins.then_inc(ev("scattered"), 1)

            gather_rows(0)
            turn_scatter(GW, ev("scatter_turned"))
            turn_rows(0)
            with pe.Fori(0, NE - 1) as e:
                expert(e, False)
            expert(NE - 1, True)
            pe.wait_ge(ev("xn_ready"), 1)
            rows_to_columns("xn", [row(2)[:, 0], row(2)[:, 1]])
            columns_ready("xn")
            for n_ in ("xl0", "xl1", "gl0", "gl1", "q20", "q21"):
                dense(n_, lhs)
            pe.wait_ge(ev("gate_w_landed"), 32)
            pe.wait_ge(ev("xc_ready"), 1)
            for g in range(8):
                if g >= 2:
                    pe.wait_ge(ev("gates_read"), g - 1)
                for j in range(2):
                    n_ = 2 * (g % 4) + j
                    ins = pe.matmul(PS[:, 6 + g % 2, j * T:(j + 1) * T], GW2[:, g // 4, n_, :], XC[:, n_, :], start=True, stop=True)
                ins.then_inc(ev("gates_done"), 1)
            for n_ in ("k20", "k21", "v20", "v21", "gr0", "gr1"):
                dense(n_, lhs)
            pe.wait_ge(ev("q_ready"), 1)
            rows_to_columns("q", [Q2[:, 0], Q2[:, 1]])
            pe.wait_ge(ev("k_ready"), 1)
            rows_to_columns("k", [K2[:, 0], K2[:, 1]])
            columns_ready("k")
            pe.wait_ge(ev("v_ready"), 1)

            def scores(h):
                if h >= 2:
                    pe.wait_ge(ev("scores_masked"), h - 1)
                b = 6 + h % 2
                pe.matmul(PS[:, b, 0:T], KT2[:, h, 0:P], QT[:, h, :], start=True, stop=True)
                pe.matmul(PS[:, b, T:T + P], KT2[:, h, P:T], QT[:, h, P:T], start=True, stop=True) \
                    .then_inc(ev("scores_done"), 1)

            scores(0)
            for h in range(8):
                if h + 1 < 8:
                    scores(h + 1)
                pe.wait_ge(ev("scores_masked"), h + 1)
                if h >= 2:
                    pe.wait_ge(ev("o_copied"), h - 1)
                s_ = SCT[:, h % 2, :]
                o = PS[:, 4 + h % 2, 0:T]
                c = slice(h * P, (h + 1) * P)
                pe.matmul(o[:, 0:P], s_[:, 0:P], V2[:, 0, c], start=True, stop=True)
                pe.matmul(o[:, P:T], s_[:, P:T], V2[:, 0, c], start=True, stop=False)
                pe.matmul(o[:, P:T], s_[:, T:T + P], V2[:, 1, c], start=False, stop=True).then_inc(ev("o_done"), 1)
            pe.wait_ge(ev("o_copied"), 8)
            pe.wait_ge(ev("yr_ready"), 1)
            rows_to_columns("yr", [O2[:, 0], O2[:, 1]])
            columns_ready("yr")
            pe.wait_ge(ev("yl_ready"), 1)
            for i in range(2):
                dense(f"w2o{i}", lambda k: YRT[:, k, :] if k < KT else R2[:, k - KT, :])
            pe.wait_ge(ev("hg_ready"), 1)
            rows_to_columns("hg", [row(9)[:, 0], row(9)[:, 1]])
            columns_ready("hg")
            pe.wait_ge(ev("tables_landed"), 80)
            for k in range(KT):
                ins = pe.matmul(PS[0:GLA_R, 6, 0:T], WGR[:, k, :], hT[:, k, :], start=k == 0, stop=k == KT - 1)
            ins.then_inc(ev("r_done"), 1)
            dense("gq", lhs)
            pe.wait_ge(ev("r_copied"), 1)
            for h in range(GLA_H):
                ins = pe.matmul(PS[:, 6 + h // 2, (h % 2) * T:(h % 2 + 1) * T], WGU[:, h * P:(h + 1) * P], RT,
                                start=True, stop=True)
            ins.then_inc(ev("gla_gate_done"), 1)
            dense("gk", lhs)
            for i in range(4):
                dense(f"gv{i}", lhs)
            pe.wait_ge(ev("kend_ready"), 1)
            turn("kend", [[KE[:, h, t * P:(t + 1) * P] for h in range(GLA_H)] for t in range(TT)])
            pe.wait_ge(ev("qk_ready"), 1)
            for n_ in range(4):
                t, r = n_ // 2, (n_ % 2) * GLA_C
                c = slice(n_ * GLA_C, (n_ + 1) * GLA_C)
                for h in range(GLA_H):
                    o = PS[r:r + GLA_C, 6, (t * 4 + h) * GLA_C:(t * 4 + h + 1) * GLA_C]
                    ins = pe.matmul(o, GK[:, h, c], GQ[:, h, c], start=True, stop=True, skip_group_check=True)
            ins.then_inc(ev("att_done"), 1)
            for i in range(4):
                dense(f"gz{i}", lhs)
            columns_ready("kend")
            pe.wait_ge(ev("att_masked"), 1)
            pe.wait_ge(ev("gv_ready"), 4)
            pe.wait_ge(ev("gz_ready"), 4)
            for n_ in range(4):
                t, r = n_ // 2, (n_ % 2) * GLA_C
                c = slice(n_ * GLA_C, (n_ + 1) * GLA_C)
                if n_ == 2:
                    pe.wait_ge(ev("og_copied"), 4)
                for h in range(GLA_H):
                    vh = GV[r:r + GLA_C, t, h * GLA_DV:(h + 1) * GLA_DV]
                    ins = pe.matmul(PS[r:r + GLA_C, h, :], ATT[r:r + GLA_C, t, h, :], vh, start=True, stop=n_ == 0,
                                    skip_group_check=True)
                    if n_ > 0:
                        pe.wait_ge(ev("state_ready"), (n_ - 1) * GLA_H + h + 1)
                        ins = pe.matmul(PS[r:r + GLA_C, h, :], GQ[:, h, c], GS[:, h, :], start=False, stop=True,
                                        skip_group_check=True)
                    if n_ == 3:
                        ins.then_inc(ev("go_done"), 1)
                    if n_ < 3:
                        ins = pe.matmul(PS[:, 4 + h, :], KR[r:r + GLA_C, t, h * P:(h + 1) * P], vh, start=True, stop=True)
                        ins.then_inc(ev("kv_done"), 1)
            pe.wait_ge(ev("og_ready"), 1)
            rows_to_columns("og", OG, 16)
            columns_ready("og")
            for i in range(2):
                dense(f"go{i}", lambda k: OGT[:, k, :])
            pe.wait_ge(ev("hs_ready"), 1)
            rows_to_columns("hs", [row(9)[:, 0], row(9)[:, 1]])
            columns_ready("hs")
            for i in range(4):
                dense(f"su{i}", lhs)
            for i in range(4):
                dense(f"sz{i}", lhs)
            for n_ in ("sz2", "sz3"):
                pe.wait_ge(unit_free[UNIT[n_][0] % 2], UNIT[n_][0] // 2 + 1)
            pe.sem_inc(ev("s5_turned"), 1)
            pe.sem_inc(ev("s5_bu_done"), 1)
            pe.sem_inc(ev("s5_half_done"), 2)

            def turn_bc(ct):
                pe.wait_ge(ev("s5_bc_copied"), ct + 1)
                for a in range(2):
                    pe.transpose(PS[:, 4, a * P:(a + 1) * P], BD[:, a].rearrange("p q b i -> p (q b i)"), ident)
                for a in range(2):
                    ins = pe.transpose(PS[:, 4, (2 + a) * P:(3 + a) * P], CS[:, a].rearrange("p b q -> p (b q)"), ident)
                ins.then_inc(ev("s5_turned"), 1)

            def drive(ct, par, hb):
                if hb == 0:
                    pe.wait_ge(ev("s5_lhs_ready"), ct + 1)
                for a in range(2):
                    for j in range(2):
                        q = 2 * hb + j
                        r = slice(32 * q, 32 * q + 32)
                        ins = pe.matmul(PS[:, q, a * T:(a + 1) * T], BTW[par][r, a, :], UC[par][r, :], start=True, stop=True)
                ins.then_inc(ev("s5_bu_done"), 1)

            def tile(ct, par, last):
                if not last:
                    turn_bc(ct + 1)
                for hb in range(2):
                    if not last:
                        pe.wait_ge(ev("s5_in"), ct * 2 + (hb + 1))
                        drive(ct + 1, 1 - par, hb)
                    pe.wait_ge(ev("s5_real_out"), ct * 2 + (hb + 1))
                    pe.wait_ge(ev("s5_imag_out"), ct * 2 + (hb + 1))
                    if hb == 0:
                        pe.wait_ge(ev("s5_y"), ct + 1)
                    for m, (w_, r_) in enumerate(((0, PA), (2, SA), (2, PB), (1, SB))):
                        for j in range(2):
                            q = 2 * hb + j
                            ins = pe.matmul(PS[32 * q:32 * q + 32, 6 + par, 0:T],
                                            CTW[par][:, w_, q].rearrange("p b i -> p (b i)"), r_[hb][:, j, :],
                                            start=m == 0, stop=m == 3, skip_group_check=True)
                    ins.then_inc(ev("s5_half_done"), 1)

            turn_bc(0)
            drive(0, 0, 0)
            drive(0, 0, 1)
            with pe.Fori(0, S5_CT // 2 - 1) as i:
                tile(i * 2, 0, False)
                tile(i * 2 + 1, 1, False)
            tile(S5_CT - 2, 0, False)
            tile(S5_CT - 1, 1, True)
            for i in range(4):
                if i == 0:
                    pe.wait_ge(ev("s5_gelu"), 2)
                dense(f"sg{i}", lambda k: U16[:, k, :])
            pe.wait_ge(ev("glu_ready"), 1)
            for i in range(2):
                dense(f"so{i}", lambda k: G16[:, k, :])

        @block.scalar
        def _(act):

            def param(dst, src):
                act.dma_start(dst, src).then_inc(param_landed, 16)

            def v128(a):
                return a.rearrange("(r q) -> r q", q=P)

            param(PVR[R_C:R_C + 8, 0, :], v128(A["c"][0]))
            param(PVR[R_AV:R_AV + 8, 0, :], v128(A["b_in"][0, 0:D]))
            param(PVR[R_AG:R_AG + 8, 0, :], v128(A["b_in"][0, D:2 * D]))
            param(PVR[R_CB:R_CB + 8, 0, :], v128(A["conv_b"][0]))
            param(PVR[R_BS:R_BS + 8, 0, :], A["b_s"][0])
            param(PVR[R_CW2:R_CW2 + 32, 0, :], A["conv_w_2"].rearrange("j (k q) -> (j k) q", q=P))
            param(PVR[R_CB2:R_CB2 + 8, 0, :], v128(A["conv_b_2"]))
            param(PVR[R_GAB:R_GAB + 8, 0, :], A["gate_a_b_2"])
            param(PVR[R_GXB:R_GXB + 8, 0, :], A["gate_x_b_2"])
            param(PVR[R_LAM:R_LAM + 8, 0, :], v128(A["lru_lambda_2"]))
            param(PVR[R_BG:R_BG + 4, 0, :], v128(A["gla_b_gate_3"][0]))
            param(PVR[R_GLU:R_GLU + 16, 0, :], v128(A["s5_b_glu_3"][0]))
            param(PVR[:, 1, :], A["conv_w"][0, 0:16].rearrange("j (k q) -> (j k) q", q=P))
            param(PVR[0:120, 2, :], A["conv_w"][0, 16:31].rearrange("j (k q) -> (j k) q", q=P))
            param(PVR[0:64, 3, :], A["s5_lam_re_3"][0].rearrange("(a b) p -> a (b p)", b=2))
            param(PVR[64:128, 3, :], A["s5_lam_im_3"][0].rearrange("(a b) p -> a (b p)", b=2))
            param(LDT[0:64], A["s5_log_dt_3"][0].rearrange("(a b) -> a b", b=2))
            param(PVR[64:80, 4, :], A["s5_d_3"][0].rearrange("(a b) i -> a (b i)", b=8))
            act.dma_start(WSR, A["w_s"][0].rearrange("g i j -> i g j")).then_inc(ev("ws_landed"), 16)

            def unit_act(name, dst, func, **kw):
                wait_unit(act, name)
                free_unit(act.activation(dst, unit_ps(name), func, **kw), name)

            for b in range(2):
                act.wait_ge(tp_ready, TB["params"] + b + 1)
                n_ = 4 if b == 0 else 1
                if b == 0:
                    act.activation(PC[:, 0, 0:R_N0], PS[:, 4, 0:R_N0], ACT.Copy)
                    act.activation(PC[:, 1, :], PS[:, 4, P:2 * P], ACT.Copy)
                    act.activation(PC[:, 2, 0:120], PS[:, 4, 2 * P:2 * P + 120], ACT.Copy)
                    act.activation(PC[:, 3, :], PS[:, 4, 3 * P:4 * P], ACT.Copy).then_inc(tp_copied, 1)
                else:
                    act.activation(PC[:, 4, 0:80], PS[:, 5, 0:80], ACT.Copy).then_inc(tp_copied, 1)
            act.drain()
            act.activation(pcol(R_C, 8), pcol(R_C, 8), ACT.Silu).then_inc(ev("silu_c_ready"), 1)
            for b in range(2):
                act.wait_ge(tp_ready, TB["ws"] + b + 1)
                act.activation(WST[:, 4 * b:4 * b + 4, :], PS[:, 4 + b, :].rearrange("p (k t) -> p k t", k=4),
                               ACT.Copy).then_inc(tp_copied, 1)
            act_std(act)
            copy_columns(act, "h1", col(HT))
            sg = col(U)
            for i in range(2):
                name = f"ag{i}"
                wait_unit(act, name)
                for m in range(4):
                    k = 4 * i + m
                    ins = act.activation(sg[:, k, :], unit_ps(name)[:, m // 2, (m % 2) * T:(m % 2 + 1) * T], ACT.Sigmoid,
                                         bias=pcol(R_AG + k))
                    if m == 3:
                        free_unit(ins, name)
            act.drain()
            act.wait_ge(ev("branch_raw"), 1)
            act.activation(row(VV), row(VV), ACT.Gelu).then_inc(ev("v_gelu"), 1)
            act.wait_ge(ev("branch_raw"), 2)
            act.activation(row(U), row(U), ACT.Gelu).then_inc(ev("u_gelu"), 1)
            act.wait_ge(ev("branch_raw"), 3)
            act.activation(row(GA), row(GA), ACT.Sigmoid).then_inc(ev("ga_sig"), 1)
            act.wait_ge(ev("branch_raw"), 4)
            act.activation(row(GB), row(GB), ACT.Sigmoid).then_inc(ev("gb_sig"), 1)
            act_std(act)
            act.wait_ge(ev("mix_done"), 2)
            vv = row(VV)
            for b in range(4):
                act.wait_ge(tp_ready, TB["conv"] + b + 1)
                ins = act.activation(vv[:, b // 2, (b % 2) * CH:(b % 2 + 1) * CH], PS[:, 4 + (TB["conv"] + b) % 2, :], ACT.Copy)
                ins.then_inc(tp_copied, 1)
            copy_columns(act, "yb", col(HT))
            act_std(act)
            act.wait_ge(ev("ya_norm"), 1)
            act.activation(vv, vv, ACT.Silu).then_inc(ev("ya_ready"), 1)
            copy_columns(act, "ya", col(HT2))
            copy_columns(act, "m", col(HT))
            act_std(act)
            act_std(act)
            copy_columns(act, "h2", H2T)
            act.wait_ge(ev("neg_max"), 1)
            for t in range(TT):
                ins = act.activation(E4[:, t, :], V8[:, t, 0:4], ACT.Exp, bias=NM[:, t:t + 1], accum_out=ES[:, t:t + 1])
            ins.then_inc(ev("exp_ready"), 1)
            act.wait_ge(ev("pos_done"), 1)
            act.activation(WMT, PS[0:NE, 7, P:P + T].rearrange("p (t s) -> p t s", t=TT), ACT.Copy).then_inc(ev("wmt_ready"), 1)
            act.wait_ge(ev("table_ready"), 1)

            def copy_rows(e):
                act.wait_ge(ev("gathered"), e + 1)
                act.activation(XR, PS[:, 4, :], ACT.Copy).then_inc(ev("xr_copied"), 1)

            def copy_scatter(e):
                act.wait_ge(ev("scatter_turned"), e + 1)
                act.activation(SC, PS[:, 5, 0:T], ACT.Copy).then_inc(ev("sc_ready"), 1)

            def extra_block(x):
                act.wait_ge(ev("x_gathered"), x + 1)
                act.activation(XETX, PS[:, 4, :].rearrange("p (k s) -> p k s", k=KT), ACT.Copy).then_inc(ev("x_xet_copied"), 1)
                act.wait_ge(ev("x_gate_clipped"), x + 1)
                act.activation(SG, GT, ACT.Sigmoid, scale=1.702).then_inc(ev("x_sig"), 1)
                act.wait_ge(ev("x_act_turned"), x + 1)
                act.activation(ACTT.rearrange("p (h c) s -> p c h s", h=2),
                               PS[:, 2, :].rearrange("p (c h s) -> p c h s", c=4, h=2), ACT.Copy).then_inc(ev("x_actt_copied"), 1)
                act.wait_ge(ev("x_scatter_turned"), x + 1)
                act.activation(SCX, PS[:, 5, 0:T], ACT.Copy)
                act.wait_ge(ev("x_down_done"), x + 1)
                act.activation(YE, PS[:, 3, :], ACT.Copy).then_inc(ev("x_ye_copied"), 1)
                act.wait_ge(ev("x_acc_added"), x * 2 + 2)

            def extras(e):
                lo = act.value_load(TABI[0:1, 0, bass.ds(e, 1)], min_val=0, max_val=64)
                hi = act.value_load(TABI[0:1, 1, bass.ds(e, 1)], min_val=0, max_val=64)
                with act.If(hi - lo > 0):
                    with act.Fori(lo, hi) as x:
                        act.wait_ge(ev("acc_added"), e * 2 + 1)
                        extra_block(x)

            def expert(e, last):
                extras(e)
                act.wait_ge(ev("gate_clipped"), e + 1)
                act.activation(SG, GT, ACT.Sigmoid, scale=1.702).then_inc(ev("sig_gate"), 1)
                if not last:
                    copy_rows(e + 1)
                act.wait_ge(ev("act_turned"), e + 1)
                act.activation(ACTT.rearrange("p (h c) s -> p c h s", h=2),
                               PS[:, 2, :].rearrange("p (c h s) -> p c h s", c=4, h=2), ACT.Copy).then_inc(ev("actt_copied"), 1)
                act.wait_ge(ev("down_done"), e + 1)
                act.activation(YE, PS[:, 3, :], ACT.Copy).then_inc(ev("ye_copied"), 1)
                if not last:
                    act.wait_ge(ev("scattered"), e * 2 + 2)
                    copy_scatter(e + 1)

            copy_rows(0)
            copy_scatter(0)
            with act.Fori(0, NE - 1) as e:
                expert(e, False)
            expert(NE - 1, True)
            act_std(act)
            act.wait_ge(ev("lam_in"), 1)
            act.activation(LS[:, 0], pcol(R_LAM, 8), ACT.Abs)
            act.drain()
            act.activation(LS[:, 0], LS[:, 0], ACT.Exp, scale=-1.0)
            act.drain()
            act.activation(LS[:, 1], LS[:, 0], ACT.Ln, bias=1.0).then_inc(ev("lam_ln"), 1)
            act_std(act)
            copy_columns(act, "xn", col(HT))

            def quarter(name):
                return unit_ps(name).rearrange("p a (b t) -> p (a b) t", b=2)

            for i in range(2):
                wait_unit(act, f"xl{i}")
                ins = act.activation(XLC[:, 4 * i:4 * i + 4, :], quarter(f"xl{i}"), ACT.Copy)
                free_unit(ins, f"xl{i}")
            for i in range(2):
                wait_unit(act, f"gl{i}")
                free_unit(act.activation(GLC[:, 4 * i:4 * i + 4, :], quarter(f"gl{i}"), ACT.Silu), f"gl{i}")
            for g in range(8):
                act.wait_ge(ev("gates_done"), g + 1)
                for j in range(2):
                    n_ = 2 * (g % 4) + j
                    dst = (R2 if g < 4 else I2)[:, n_, :]
                    ins = act.activation(dst, PS[:, 6 + g % 2, j * T:(j + 1) * T], ACT.Sigmoid,
                                         bias=pcol((R_GAB if g < 4 else R_GXB) + n_))
                ins.then_inc(ev("gates_read"), 1)
            act.wait_ge(ev("rates_ready"), 1)
            act.wait_ge(ev("ix_ready"), 1)
            for k in range(KT):
                act.activation(XC[:, k, :], R2[:, k, :], ACT.Exp, scale=LS[:, 4, k:k + 1])
            act.drain()
            for k in range(KT):
                ins = act.activation(R2[:, k, :], R2[:, k, :], ACT.Exp, scale=LS[:, 5, k:k + 1])
            ins.then_inc(ev("a_ready"), 1)
            act.wait_ge(ev("a2_clipped"), 1)
            act.activation(R2, R2, ACT.Sqrt, scale=-1.0, bias=1.0).then_inc(ev("mult_ready"), 1)
            act.wait_ge(ev("k_ready"), 1)
            for i in range(2):
                wait_unit(act, f"v2{i}")
                ins = act.activation(V2[:, :, i * CH:(i + 1) * CH], unit_ps(f"v2{i}"), ACT.Copy)
                free_unit(ins, f"v2{i}")
            for i in range(2):
                wait_unit(act, f"gr{i}")
                ins = act.activation(GR[:, :, i * CH:(i + 1) * CH], unit_ps(f"gr{i}"), ACT.Silu)
                free_unit(ins, f"gr{i}")
            act.drain()
            act.sem_inc(ev("v_ready"), 1)
            act.wait_ge(ev("yl_ready"), 1)
            copy_columns(act, "q", QT)
            copy_columns(act, "k", KT2)
            for h in range(8):
                act.wait_ge(ev("o_done"), h + 1)
                act.activation(O2[:, :, h * P:(h + 1) * P], PS[:, 4 + h % 2, 0:T].rearrange("p (t e) -> p t e", t=TT),
                               ACT.Copy).then_inc(ev("o_copied"), 1)
            act.wait_ge(ev("hvar_ready"), 1)
            act.activation(HSD[:], HVE[:], ACT.Sqrt).then_inc(ev("hstd_ready"), 1)
            copy_columns(act, "yr", YRT)
            act_std(act)
            act_std(act)
            copy_columns(act, "hg", col(HT))
            act.wait_ge(ev("r_done"), 1)
            act.activation(RT, PS[0:GLA_R, 6, 0:T], ACT.Copy).then_inc(ev("r_copied"), 1)
            wait_unit(act, "gq")
            free_unit(act.activation(GQ, quarter("gq"), ACT.Copy, scale=GLA_DK ** -0.5), "gq")
            wait_unit(act, "gk")
            free_unit(act.activation(GK, quarter("gk"), ACT.Copy), "gk")
            act.wait_ge(ev("gate_x"), 1)
            act.activation(BC, LA, ACT.Abs)
            act.drain()
            act.activation(BC, BC, ACT.Exp, scale=-1.0)
            act.drain()
            act.activation(BC, BC, ACT.Ln, bias=1.0).then_inc(ev("gate_ln"), 1)
            act.wait_ge(ev("bcum_ready"), 1)
            act.activation(TE, BC, ACT.Exp)
            act.activation(DC4[:], BC[:, :, GLA_C - 1:T:GLA_C], ACT.Exp)
            act.activation(LA, LA, ACT.Exp).then_inc(ev("exps_ready"), 1)
            act.wait_ge(ev("qg_ready"), 1)
            act.activation(TE, BC, ACT.Exp, scale=-1.0).then_inc(ev("expn_ready"), 1)
            for i in range(4):
                wait_unit(act, f"gv{i}")
                free_unit(act.activation(GV[:, :, i * CH:(i + 1) * CH], unit_ps(f"gv{i}"), ACT.Copy), f"gv{i}")
            act.drain()
            act.sem_inc(ev("gv_ready"), 4)
            for b in range(TT):
                act.wait_ge(tp_ready, TB["kend"] + b + 1)
                act.activation(KR[:, b, :], PS[:, 4 + (TB["kend"] + b) % 2, :], ACT.Copy).then_inc(tp_copied, 1)
            for i in range(4):
                wait_unit(act, f"gz{i}")
                free_unit(act.activation(GZ[:, :, i * CH:(i + 1) * CH], unit_ps(f"gz{i}"), ACT.Silu), f"gz{i}")
            act.drain()
            act.sem_inc(ev("gz_ready"), 4)
            for t in range(TT):
                for h in range(GLA_H):
                    if t == 0:
                        act.wait_ge(ev("kv_done"), GLA_H + h + 1)
                    else:
                        act.wait_ge(ev("go_done"), GLA_H)
                    act.activation(OG[t][:, h * GLA_DV:(h + 1) * GLA_DV], PS[:, h, :], ACT.Copy).then_inc(ev("og_copied"), 1)
            act.wait_ge(ev("hvar_ready"), 2)
            act.activation(HSD[:, 0:8], HVE[:, 0:8], ACT.Sqrt).then_inc(ev("hstd_ready"), 1)
            copy_columns(act, "og", OGT, 16)
            act_std(act)
            copy_columns(act, "hs", col(HT))
            act.activation(work[0], PC[:, 4, 0:64], ACT.Exp).then_inc(ev("s5_setup"), 1)
            act.wait_ge(ev("turns_ready"), 1)
            act.activation(work[3], work[1], ACT.Exp)
            act.activation(work[4], TH, ACT.Sin, scale=TWO_PI)
            act.activation(work[5], TH, ACT.Sin, scale=TWO_PI / 2).then_inc(ev("s5_setup"), 1)
            for i in range(4):
                wait_unit(act, f"su{i}")
                free_unit(act.activation(U16[:, 4 * i:4 * i + 4, :], quarter(f"su{i}"), ACT.Copy), f"su{i}")
            for i in range(4):
                wait_unit(act, f"sz{i}")
                free_unit(act.activation(Z16[:, 4 * i:4 * i + 4, :], quarter(f"sz{i}"), ACT.Silu), f"sz{i}")
            act.wait_ge(ev("zeroed"), 1)

            def stationary(ct, par, used_before):
                for a in range(2):
                    for g in range(2):
                        r = slice(64 * g, 64 * g + 64)
                        ins = act.activation(BD[r, a, :, g, :], BB[r, a, bass.ds(ct * PAIRS, PAIRS), :], ACT.Copy)
                for a in range(2):
                    ins = act.activation(CS[:, a], CC[:, a, bass.ds(ct, 1), :].to_broadcast([P, 2, 64]), ACT.Copy)
                ins.then_inc(ev("s5_bc_copied"), 1)
                if used_before:
                    act.wait_ge(ev("s5_bu_done"), ct * 2 - 1)
                act.activation(UC[par], U16[:, bass.ds(ct, 1), :].rearrange("p a t -> p (a t)"), ACT.Copy)
                act.wait_ge(ev("s5_turned"), ct + 2)
                if used_before:
                    act.wait_ge(ev("s5_half_done"), ct * 2)
                act.activation(BTW[par], PS[:, 4, 0:T].rearrange("p (a m) -> p a m", a=2), ACT.Copy)
                cps = PS[:, 4, T:2 * T].rearrange("p (a q b i) -> p a q b i", a=2, q=PAIRS, b=2)
                for g in range(2):
                    r = slice(64 * g, 64 * g + 64)
                    act.activation(CTW[par][r, 0, :, g, :], cps[r, 0, :, g, :], ACT.Copy)
                    act.activation(CTW[par][r, 1, :, g, :], cps[r, 0, :, g, :], ACT.Copy, scale=-1.0)
                    ins = act.activation(CTW[par][r, 2, :, g, :], cps[r, 1, :, g, :], ACT.Copy, scale=-1.0)
                ins.then_inc(ev("s5_lhs_ready"), 1)

            def rounded(par, hb):
                for j in range(2):
                    act.activation(RND[:, j, :], iota_t, ACT.Identity, bias=MAGIC, scale=TC[par][:, 0, 2 * hb + j:2 * hb + j + 1])
                act.drain()
                act.activation(RND, RND, ACT.Copy, bias=-MAGIC).then_inc(ev("s5_rounded"), 1)

            def trig(g, hb, used_before):
                act.wait_ge(ev("s5_angles"), g + 1)
                act.activation(RND, ANG, ACT.Abs)
                if used_before:
                    act.wait_ge(ev("s5_real_out"), g - 1)
                    act.wait_ge(ev("s5_imag_out"), g - 1)
                act.activation(SSIN[hb], ANG, ACT.Sin, scale=TWO_PI)
                act.drain()
                act.activation(SCOS[hb], RND, ACT.Sin, scale=-TWO_PI, bias=HALF_PI).then_inc(ev("s5_trig"), 1)
                act.drain()

            def tile(ct, par):
                act.wait_ge(ev("s5_copied"), ct + 2)
                rounded(1 - par, 0)
                act.wait_ge(ev("s5_turned"), ct + 2)
                stationary(ct + 1, 1 - par, True)
                trig(ct * 2 + 2, 0, True)
                rounded(1 - par, 1)
                trig(ct * 2 + 3, 1, True)

            act.wait_ge(ev("s5_copied"), 1)
            rounded(0, 0)
            stationary(0, 0, False)
            trig(0, 0, False)
            rounded(0, 1)
            trig(1, 1, False)
            with act.Fori(0, S5_CT // 2 - 1) as i:
                tile(i * 2, 0)
                tile(i * 2 + 1, 1)
            tile(S5_CT - 2, 0)
            act.wait_ge(ev("s5_y"), S5_CT)
            act.activation(U16[:, 0:S5_CT - 2, :], U16[:, 0:S5_CT - 2, :], ACT.Gelu_apprx_tanh).then_inc(ev("s5_gelu"), 1)
            act.wait_ge(ev("s5_y"), S5_CT + 2)
            act.activation(U16[:, S5_CT - 2:S5_CT, :], U16[:, S5_CT - 2:S5_CT, :], ACT.Gelu_apprx_tanh).then_inc(ev("s5_gelu"), 1)
            for i in range(4):
                wait_unit(act, f"sg{i}")
                for m in range(4):
                    ins = act.activation(G16[:, 4 * i + m, :], quarter(f"sg{i}")[:, m, :], ACT.Sigmoid, bias=pcol(R_GLU + 4 * i + m))
                free_unit(ins, f"sg{i}")
            act.drain()
            act.sem_inc(ev("glu_sig"), 1)
            act_std(act)

        @block.vector
        def _(dve):
            def rows_from(name, dst, vec, j):
                wait_unit(dve, name)
                free_unit(dve.tensor_tensor(dst[:, :, j * CH:(j + 1) * CH], unit_ps(name),
                                            bt(vec[:, j * CH:(j + 1) * CH]), ALU.add), name)

            def mod_from(name, dst):
                vec = vector(dve, "b_mod")
                wait_unit(dve, name)
                free_unit(dve.tensor_tensor(dst, unit_ps(name).rearrange("p a b -> p (a b)"), vec, ALU.add), name)
                dve.drain()

            def used(ins):
                ins.then_inc(v_used, 1)

            dve.memset(ONES, 1.0)
            dve.wait_ge(param_landed, 16 * N_PARAM)
            dve.tensor_copy(PVR[0:64, 4, :].rearrange("p (b q) -> p b q", b=2),
                            LDT[0:64].unsqueeze(2).to_broadcast([64, 2, 64])).then_inc(ev("log_dt_ready"), 1)
            dve.wait_ge(ev("silu_c_ready"), 1)
            dve.tensor_copy(CB, pcol(R_C, 8).unsqueeze(2).to_broadcast([P, KT, P])).then_inc(ev("cond_ready"), 1)
            dve.wait_ge(tp_copied, TB["ws"] + 2)
            dve.memset(WST[64:128, :, 0:64], 0.0).then_inc(ev("wst_ready"), 1)
            dve.wait_ge(x_landed, 16)
            h1 = row(HN)
            layer_norm(dve, h1, X)

            def modulate(dst, src, sc_name, sh_name, done):
                vec = vector(dve, "b_mod")
                wait_unit(dve, sc_name)
                ins = dve.scalar_tensor_tensor(MA, unit_ps(sc_name).rearrange("p a b -> p (a b)"), 1.0, vec, ALU.add, ALU.add)
                free_unit(ins, sc_name)
                dve.drain()
                used(dve.tensor_tensor(dst, src, bt(MA), ALU.mult))
                vec = vector(dve, "b_mod")
                wait_unit(dve, sh_name)
                ins = dve.tensor_tensor(MB, unit_ps(sh_name).rearrange("p a b -> p (a b)"), vec, ALU.add)
                free_unit(ins, sh_name)
                dve.drain()
                used(dve.tensor_tensor(dst[:, 0], dst[:, 0], MB, ALU.add))
                dve.tensor_tensor(dst[:, 1], dst[:, 1], MB, ALU.add).then_inc(done, 1)

            modulate(h1, h1, "sc1", "sh1", ev("h1_ready"))
            ya, sg = col(HN), col(U)
            dve.wait_ge(tp_ready, TB["h1"] + 4)
            for i in range(2):
                name = f"av{i}"
                wait_unit(dve, name)
                dve.wait_ge(unit_free[UNIT[f"ag{i}"][0] % 2], UNIT[f"ag{i}"][0] // 2 + 1)
                for m in range(4):
                    k = 4 * i + m
                    ins = dve.scalar_tensor_tensor(ya[:, k, :], unit_ps(name)[:, m // 2, (m % 2) * T:(m % 2 + 1) * T],
                                                   pcol(R_AV + k), sg[:, k, :], ALU.add, ALU.mult)
                free_unit(ins, name)
            dve.drain()
            cv = col(CV)
            raw = [("v0", VV, 0), ("v1", VV, 1), ("u0", U, 0), ("u1", U, 1), ("ga0", GA, 0), ("ga1", GA, 1),
                   ("gb0", GB, 0), ("gb1", GB, 1)]
            vec = None
            for lag in range(CONV1):
                for k in range(KT):
                    r = P + (CONV1 - 1 - lag) * KT + k
                    if lag == 0:
                        dve.tensor_scalar(cv[:, k, :], ya[:, k, :], pcol(r), pcol(R_CB + k), ALU.mult, ALU.add)
                    else:
                        ins = dve.scalar_tensor_tensor(cv[:, k, lag:], ya[:, k, 0:T - lag], pcol(r), cv[:, k, lag:],
                                                       ALU.mult, ALU.add)
                if lag == CONV1 - 1:
                    ins.then_inc(ev("conv_done"), 1)
                if lag >= 3 and lag % 3 == 0 and lag // 3 <= 8:
                    name, area, j = raw[lag // 3 - 1]
                    if j == 0:
                        vec = vector(dve, "b_in")
                    rows_from(name, row(area), vec, j)
                    dve.drain()
                    if j == 1:
                        dve.sem_inc(v_used, 1)
                        dve.sem_inc(ev("branch_raw"), 1)
                else:
                    dve.drain()
            vv, u = row(VV), row(U)
            dve.wait_ge(ev("v_gelu"), 1)
            layer_norm(dve, vv, vv)

            def gain_bias(dst, gname, bname, done):
                vec = vector(dve, gname)
                used(dve.tensor_tensor(dst, dst, bt(vec), ALU.mult))
                dve.drain()
                vec = vector(dve, bname)
                used(dve.tensor_tensor(dst, dst, bt(vec), ALU.add))
                dve.drain()
                if done is not None:
                    dve.sem_inc(done, 1)

            gain_bias(vv, "ln_v_g", "ln_v_b", ev("vn_ready"))
            dve.wait_ge(ev("u_gelu"), 1)
            for t in range(TT):
                dve.wait_ge(ev("mix_done"), t + 1)
                for g in range(8):
                    ins = dve.scalar_tensor_tensor(u[:, t, g * P:(g + 1) * P], PS[:, 6 + g // 4, (g % 4) * P:(g % 4 + 1) * P],
                                                   pcol(R_BS + g), u[:, t, g * P:(g + 1) * P], ALU.add, ALU.mult)
                ins.then_inc(ev("mix_read"), 1)
            dve.drain()
            dve.sem_inc(ev("yb_ready"), 1)
            dve.wait_ge(tp_copied, TB["conv"] + 4)
            layer_norm(dve, vv, vv)
            gb = row(GB)
            ga = row(GA)
            vec = vector(dve, "b_b")
            dve.wait_ge(ev("gb_sig"), 1)
            cvr = row(CV)
            for i in range(2):
                rows_from(f"wb{i}", cvr, vec, i)
            dve.drain()
            used(dve.tensor_tensor(gb, gb, cvr, ALU.mult))
            gain_bias(vv, "ln_a_g", "ln_a_b", ev("ya_norm"))
            vec = vector(dve, "b_a")
            dve.wait_ge(ev("ga_sig"), 1)
            for i in range(2):
                rows_from(f"wa{i}", cvr, vec, i)
            dve.drain()
            used(dve.tensor_tensor(ga, ga, cvr, ALU.mult))
            dve.drain()
            dve.tensor_tensor(ga, ga, gb, ALU.add).then_inc(ev("m_ready"), 1)
            vec = vector(dve, "b_mod")
            wait_unit(dve, "g1")
            free_unit(dve.tensor_tensor(MA, unit_ps("g1").rearrange("p a b -> p (a b)"), vec, ALU.add), "g1")
            dve.drain()
            dve.sem_inc(v_used, 1)
            vec = vector(dve, "b_out")
            for i in range(2):
                rows_from(f"wo{i}", cvr, vec, i)
            dve.drain()
            used(dve.tensor_tensor(cvr, cvr, bt(MA), ALU.mult))
            dve.drain()

            def residual(y):
                dve.scalar_tensor_tensor(X[:, 0], X[:, 0], ALPHA, y[:, 0], ALU.mult, ALU.add)
                dve.scalar_tensor_tensor(X[:, 1], X[:, 1], ALPHA, y[:, 1], ALU.mult, ALU.add)
                dve.drain()

            residual(cvr)
            layer_norm(dve, X, X)
            gain_bias(X, "post1_g", "post1_b", ev("x1_ready"))
            layer_norm(dve, H2, X)
            modulate(H2, H2, "sc2", "sh2", ev("h2_ready"))
            vec = vector(dve, "b_mod")
            wait_unit(dve, "g2")
            free_unit(dve.tensor_tensor(MA, unit_ps("g2").rearrange("p a b -> p (a b)"), vec, ALU.add), "g2")
            dve.drain()
            dve.sem_inc(v_used, 1)
            dve.wait_ge(ev("moe_small_landed"), 64)
            dve.wait_ge(ev("logits_done"), 1)
            dve.tensor_tensor(LG, PS[:, 6, 0:2 * NE].rearrange("p (t e) -> p t e", t=TT),
                              BRT[:, 0:1, :].to_broadcast([P, TT, NE]), ALU.add)
            dve.drain()
            for t in range(TT):
                dve.max(V8[:, t, :], LG[:, t, :])
            dve.drain()
            for t in range(TT):
                dve.max_index(I8[:, t, :], V8[:, t, :], LG[:, t, :])
            dve.tensor_scalar(NM, V8[:, :, 0], -1.0, None, ALU.mult)
            dve.drain()
            dve.tensor_copy(F8, I8).then_inc(ev("neg_max"), 1)
            dve.wait_ge(ev("exp_ready"), 1)
            dve.reciprocal(ER, ES)
            dve.drain()
            for t in range(TT):
                dve.tensor_scalar(E4[:, t, :], E4[:, t, :], ER[:, t:t + 1], None, ALU.mult)
            dve.drain()
            iota_e = K[:, C_E:C_E + NE]
            for j in range(TOPK):
                for t in range(TT):
                    if j == 0:
                        dve.tensor_scalar(SEL[:, t, :], iota_e, F8[:, t, j:j + 1], None, ALU.is_equal)
                        dve.tensor_scalar(WM[:, t, :], iota_e, F8[:, t, j:j + 1], E4[:, t, j:j + 1], ALU.is_equal, ALU.mult)
                    else:
                        dve.tensor_scalar(OH[:, t, :], iota_e, F8[:, t, j:j + 1], None, ALU.is_equal)
                dve.drain()
                if j:
                    dve.tensor_tensor(SEL, SEL, OH, ALU.add)
                    for t in range(TT):
                        dve.scalar_tensor_tensor(WM[:, t, :], OH[:, t, :], E4[:, t, j:j + 1], WM[:, t, :], ALU.mult, ALU.add)
                    dve.drain()
            dve.sem_inc(ev("sel_ready"), 1)
            dve.wait_ge(ev("pos_done"), 1)
            dve.wait_ge(ev("wmt_ready"), 1)
            pos = PS[:, 7, 0:3 * NE].rearrange("p (a e) -> p a e", a=3)
            dve.scalar_tensor_tensor(POS, pos[:, 0:2, :], 1.0, SEL, ALU.add, ALU.mult)
            cnt, nx = pos[0:1, 2, :], TABF[:, 0, :]
            dve.tensor_scalar(nx, cnt, float(BLK), None, ALU.is_gt)
            dve.tensor_scalar(TABF[:, 1, :], cnt, float(2 * BLK), None, ALU.is_gt)
            dve.tensor_scalar(TABF[:, 2, :], cnt, float(3 * BLK), None, ALU.is_gt)
            dve.drain()
            dve.tensor_scalar_add(POS, POS, -1.0)
            dve.tensor_tensor(nx, nx, TABF[:, 1, :], ALU.add)
            dve.drain()
            dve.tensor_tensor(nx, nx, TABF[:, 2, :], ALU.add)
            dve.drain()
            dve.tensor_tensor_scan(TABF[:, 1, :], ONES[0:1, 0:NE], nx, 0.0, ALU.mult, ALU.add)
            dve.drain()
            dve.tensor_tensor(TABI[:, 0, :], TABF[:, 1, :], nx, ALU.subtract)
            dve.tensor_copy(TABI[:, 1, :], TABF[:, 1, :])
            dve.drain()
            dve.sem_inc(ev("table_ready"), 1)
            for t in range(TT):
                dve.wait_ge(ev("bias_sum_done"), t + 1)
                dve.tensor_copy(YACC[:, t, :], PS[:, 6:8, :].rearrange("p a b -> p (a b)")).then_inc(ev("acc_started"), 1)
            dve.drain()

            def one_hot(e, io, g, gw, done):
                dve.tensor_copy(PW[:, 0, :], POS[:, :, bass.ds(e, 1)].rearrange("p t e -> p (t e)"))
                dve.tensor_copy(PW[:, 1, :], WM[:, :, bass.ds(e, 1)].rearrange("p t e -> p (t e)"))
                dve.drain()
                for t in range(TT):
                    dve.tensor_scalar(g[:, t, :], io[:, 0:BLK], PW[:, 0, t:t + 1], None, ALU.is_equal)
                    ins = dve.tensor_scalar(gw[:, t, :], io, PW[:, 0, t:t + 1], PW[:, 1, t:t + 1], ALU.is_equal, ALU.mult)
                ins.then_inc(done, 1)

            def columns_of(e):
                dve.tensor_copy(SELB, ident[0:NE, bass.ds(e, 1)].to_broadcast([NE, BLK]))
                dve.wait_ge(ev("xr_turned"), e + 1)
                dve.tensor_copy(XET.rearrange("p (h c) s -> p c h s", h=2),
                                PS[:, 4, :].rearrange("p (c h s) -> p c h s", c=4, h=2)).then_inc(ev("xet_ready"), 1)

            def accumulate(t, done):
                bank = 6 if t == 0 else 0
                dve.tensor_tensor(YACC[:, t, :], YACC[:, t, :], PS[:, bank:bank + 2, :].rearrange("p a b -> p (a b)"),
                                  ALU.add).then_inc(done, 1)

            def swiglu(gate, clipped, sig, up, n, ready):
                dve.wait_ge(gate, n)
                dve.tensor_scalar(GT, PS[:, 0, :], 7.0, None, ALU.min).then_inc(clipped, 1)
                dve.wait_ge(sig, n)
                dve.tensor_tensor(GT, GT, SG, ALU.mult)
                dve.wait_ge(up, n)
                dve.tensor_scalar(UP, PS[:, 1, :], -7.0, 7.0, ALU.max, ALU.min)
                dve.drain()
                dve.scalar_tensor_tensor(ACTV, UP, 1.0, GT, ALU.add, ALU.mult).then_inc(ready, 1)

            def extra_block(x, e, j):
                one_hot(e, K[:, bass.ds(j * P + C_SLOT, P)], GX, GWX, ev("x_g_ready"))
                swiglu(ev("x_gate_done"), ev("x_gate_clipped"), ev("x_sig"), ev("x_up_done"), x + 1, ev("x_act_ready"))
                for t in range(TT):
                    dve.wait_ge(ev("x_scattered"), x * 2 + (t + 1))
                    accumulate(t, ev("x_acc_added"))
                dve.drain()

            def extras(e):
                lo = dve.value_load(TABI[0:1, 0, bass.ds(e, 1)], min_val=0, max_val=64)
                hi = dve.value_load(TABI[0:1, 1, bass.ds(e, 1)], min_val=0, max_val=64)
                with dve.If(hi - lo > 0):
                    with dve.Fori(lo, hi) as x:
                        extra_block(x, e, nc.s_assert_within(x - lo + 1, 1, 3))

            def expert(e, last):
                extras(e)
                if not last:
                    one_hot(e + 1, K[:, C_SLOT:C_SLOT + P], G, GW, ev("g_ready"))
                swiglu(ev("gate_done"), ev("gate_clipped"), ev("sig_gate"), ev("up_done"), e + 1, ev("act_ready"))
                if not last:
                    columns_of(e + 1)
                for t in range(TT):
                    dve.wait_ge(ev("scattered"), e * 2 + (t + 1))
                    accumulate(t, ev("acc_added"))
                dve.drain()

            dve.sem_inc(ev("acc_added"), 1)
            one_hot(0, K[:, C_SLOT:C_SLOT + P], G, GW, ev("g_ready"))
            columns_of(0)
            with dve.Fori(0, NE - 1) as e:
                expert(e, False)
            expert(NE - 1, True)
            dve.tensor_tensor(YACC, YACC, bt(MA), ALU.mult)
            dve.drain()
            residual(YACC)
            layer_norm(dve, X, X)
            gain_bias(X, "post2_g", "post2_b", None)
            dve.sem_inc(ev("block1_done"), 1)
            dve.sem_inc(ev("lam_in"), 1)
            used(rms_norm(dve, row(2), X, vector(dve, "norm_in_g_2")))
            dve.drain()
            dve.sem_inc(ev("xn_ready"), 1)
            dve.wait_ge(ev("lam_ln"), 1)
            dve.tensor_scalar(LS[:, 2], LS[:, 0], 1.0, -1.0, ALU.add, ALU.add)
            dve.tensor_tensor(LS[:, 1], LS[:, 1], LS[:, 0], ALU.mult)
            dve.drain()
            dve.tensor_scalar(LS[:, 3], LS[:, 2], 0.0, None, ALU.is_equal)
            dve.drain()
            dve.tensor_tensor(LS[:, 2], LS[:, 2], LS[:, 3], ALU.add)
            dve.tensor_tensor(LS[:, 3], LS[:, 3], LS[:, 0], ALU.mult)
            dve.drain()
            dve.reciprocal(LS[:, 2], LS[:, 2])
            dve.drain()
            dve.tensor_tensor(LS[:, 1], LS[:, 1], LS[:, 2], ALU.mult)
            dve.tensor_scalar(LS[:, 4], pcol(R_LAM, 8), -1.0, 0.0, ALU.mult, ALU.max)
            dve.drain()
            dve.tensor_tensor(LS[:, 1], LS[:, 1], LS[:, 3], ALU.add)
            dve.drain()
            dve.tensor_tensor(LS[:, 1], LS[:, 1], LS[:, 4], ALU.add)
            dve.drain()
            dve.tensor_scalar(LS[:, 4], LS[:, 1], -8.0, None, ALU.mult)
            dve.tensor_scalar(LS[:, 5], LS[:, 1], -16.0, None, ALU.mult).then_inc(ev("rates_ready"), 1)
            dve.wait_ge(unit_free[UNIT["xl0"][0] % 2], UNIT["xl0"][0] // 2 + 1)
            dve.wait_ge(unit_free[UNIT["xl1"][0] % 2], UNIT["xl1"][0] // 2 + 1)
            for lag in range(CONV2):
                for k in range(KT):
                    w_ = pcol(R_CW2 + (CONV2 - 1 - lag) * KT + k)
                    if lag == 0:
                        ins = dve.tensor_scalar(XC[:, k, :], XLC[:, k, :], w_, pcol(R_CB2 + k), ALU.mult, ALU.add)
                    else:
                        ins = dve.scalar_tensor_tensor(XC[:, k, lag:], XLC[:, k, 0:T - lag], w_, XC[:, k, lag:],
                                                       ALU.mult, ALU.add)
                if lag == CONV2 - 1:
                    ins.then_inc(ev("xc_ready"), 1)
                dve.drain()
            dve.wait_ge(ev("tables_landed"), 80)

            def rotary(name, dst, i):
                wait_unit(dve, name)
                for t in range(TT):
                    x = unit_ps(name)[:, t, :].rearrange("p (h d) -> p h d", h=4)
                    d = dst[:, t, i * CH:(i + 1) * CH].rearrange("p (h d) -> p h d", h=4)
                    tm = V2[:, t, :].rearrange("p (a h d) -> p a h d", a=4, h=4)
                    cos = ROT[:, t, 0:64].unsqueeze(1).to_broadcast([P, 4, 64])
                    sin = ROT[:, t, 64:128].unsqueeze(1).to_broadcast([P, 4, 64])
                    dve.tensor_tensor(tm[:, 0], x[:, :, 0:64], cos, ALU.mult)
                    dve.tensor_tensor(tm[:, 1], x[:, :, 64:128], sin, ALU.mult)
                    dve.tensor_tensor(tm[:, 2], x[:, :, 0:64], sin, ALU.mult)
                    ins = dve.tensor_tensor(tm[:, 3], x[:, :, 64:128], cos, ALU.mult)
                    if t == 1:
                        free_unit(ins, name)
                    dve.drain()
                    dve.tensor_tensor(d[:, :, 0:64], tm[:, 0], tm[:, 1], ALU.subtract)
                    dve.tensor_tensor(d[:, :, 64:128], tm[:, 2], tm[:, 3], ALU.add)
                    dve.drain()

            rotary("q20", Q2, 0)
            rotary("q21", Q2, 1)
            dve.sem_inc(ev("q_ready"), 1)
            dve.wait_ge(ev("gates_read"), 8)
            dve.tensor_tensor(I2, I2, XC, ALU.mult).then_inc(ev("ix_ready"), 1)
            rotary("k20", K2, 0)
            dve.wait_ge(ev("a_ready"), 1)
            dve.tensor_scalar(R2, R2, 1.0, None, ALU.min).then_inc(ev("a2_clipped"), 1)
            rotary("k21", K2, 1)
            dve.sem_inc(ev("k_ready"), 1)
            dve.wait_ge(ev("mult_ready"), 1)
            dve.tensor_tensor(I2, I2, R2, ALU.mult)
            dve.drain()
            for k in range(KT):
                dve.tensor_tensor_scan(R2[:, k, :], XC[:, k, :], I2[:, k, :], 0.0, ALU.mult, ALU.add)
            dve.drain()
            dve.tensor_tensor(R2, R2, GLC, ALU.mult).then_inc(ev("yl_ready"), 1)
            dve.wait_ge(ev("decay_landed"), 16)
            for h in range(8):
                dve.wait_ge(ev("scores_done"), h + 1)
                if h >= 2:
                    dve.wait_ge(ev("o_done"), h - 1)
                dve.tensor_tensor(SCT[:, h % 2, :], PS[:, 6 + h % 2, 0:T + P], DEC[:, h, :], ALU.mult) \
                    .then_inc(ev("scores_masked"), 1)
                if h >= 1:
                    dve.wait_ge(ev("o_copied"), h)
                    for t in range(TT):
                        dve.bn_stats(HST[:, 2 * (h - 1) + t, :], O2[:, t, (h - 1) * P:h * P])
            dve.wait_ge(ev("o_copied"), 8)
            for t in range(TT):
                dve.bn_stats(HST[:, 14 + t, :], O2[:, t, 7 * P:8 * P])
            dve.drain()
            for j in range(16):
                dve.bn_aggr(HMV[:, j, :], HST[:, j, :])
            dve.drain()
            dve.tensor_scalar_add(HVE[:], HMV[:, :, 1], RMS_EPS).then_inc(ev("hvar_ready"), 1)
            dve.wait_ge(ev("hstd_ready"), 1)
            dve.reciprocal(HRS[:], HSD[:])
            dve.drain()
            for j in range(16):
                o = O2[:, j % 2, (j // 2) * P:(j // 2 + 1) * P]
                dve.tensor_scalar(o, o, HMV[:, j, 0:1], HRS[:, j:j + 1], ALU.subtract, ALU.mult)
            dve.drain()
            dve.tensor_tensor(O2, O2, GR, ALU.mult).then_inc(ev("yr_ready"), 1)

            def add_to_x(name, i):
                wait_unit(dve, name)
                xs = X[:, :, i * CH:(i + 1) * CH]
                free_unit(dve.tensor_tensor(xs, xs, unit_ps(name), ALU.add), name)

            add_to_x("w2o0", 0)
            add_to_x("w2o1", 1)
            dve.drain()
            used(rms_norm(dve, X, X, vector(dve, "norm_out_g_2")))
            dve.drain()
            used(rms_norm(dve, row(9), X, vector(dve, "gla_norm_3")))
            dve.drain()
            dve.sem_inc(ev("hg_ready"), 1)
            dve.memset(ATT, 0.0)
            dve.wait_ge(ev("gla_gate_done"), 1)
            for h in range(GLA_H):
                ins = dve.tensor_scalar(LA[:, h, :], PS[:, 6 + h // 2, (h % 2) * T:(h % 2 + 1) * T], pcol(R_BG + h), None, ALU.add)
            ins.then_inc(ev("gate_x"), 1)
            dve.wait_ge(ev("gate_ln"), 1)
            dve.scalar_tensor_tensor(LA, LA, 0.0, BC, ALU.min, ALU.subtract)
            dve.drain()
            dve.tensor_scalar(LA, LA, 1.0 / GLA_TAU, None, ALU.mult)
            dve.drain()
            for h in range(GLA_H):
                dve.tensor_tensor_scan(BC[:, h, :], SEG, LA[:, h, :], 0.0, ALU.mult, ALU.add)
            dve.drain()
            for h in range(GLA_H):
                b = BC[:, h, :].rearrange("p (n c) -> p n c", c=GLA_C)
                ins = dve.tensor_tensor(LA[:, h, :].rearrange("p (n c) -> p n c", c=GLA_C),
                                        b[:, :, GLA_C - 1:GLA_C].to_broadcast([P, 4, GLA_C]), b, ALU.subtract)
            ins.then_inc(ev("bcum_ready"), 1)
            dve.wait_ge(ev("exps_ready"), 1)
            dve.tensor_tensor(GQ, GQ, TE, ALU.mult).then_inc(ev("qg_ready"), 1)
            dve.tensor_tensor(KE, GK, LA, ALU.mult).then_inc(ev("kend_ready"), 1)
            dve.wait_ge(ev("expn_ready"), 1)
            dve.tensor_tensor(GK, GK, TE, ALU.mult).then_inc(ev("qk_ready"), 1)
            dve.wait_ge(ev("att_done"), 1)
            dve.copy_predicated(ATT.rearrange("p t h c -> p (t h) c"), MASK.unsqueeze(1).to_broadcast([P, 8, GLA_C]),
                                PS[:, 6, :].rearrange("p (a c) -> p a c", a=8)).then_inc(ev("att_masked"), 1)
            for n_ in range(3):
                for h in range(GLA_H):
                    dve.wait_ge(ev("kv_done"), n_ * GLA_H + h + 1)
                    if n_ == 0:
                        ins = dve.tensor_copy(GS[:, h, :], PS[:, 4 + h, :])
                    else:
                        ins = dve.scalar_tensor_tensor(GS[:, h, :], GS[:, h, :], DC4[:, h, n_:n_ + 1], PS[:, 4 + h, :],
                                                       ALU.mult, ALU.add)
                    ins.then_inc(ev("state_ready"), 1)
                dve.drain()
            for t in range(TT):
                for h in range(GLA_H):
                    dve.wait_ge(ev("og_copied"), t * GLA_H + h + 1)
                    dve.bn_stats(HST[:, t * GLA_H + h, :], OG[t][:, h * GLA_DV:(h + 1) * GLA_DV])
            dve.drain()
            for j in range(8):
                dve.bn_aggr(HMV[:, j, :], HST[:, j, :])
            dve.drain()
            dve.tensor_tensor(HVE[:, 0:8], HMV[:, 0:8, 0], HMV[:, 0:8, 0], ALU.mult)
            dve.drain()
            dve.scalar_tensor_tensor(HVE[:, 0:8], HVE[:, 0:8], RMS_EPS, HMV[:, 0:8, 1], ALU.add, ALU.add) \
                .then_inc(ev("hvar_ready"), 1)
            dve.wait_ge(ev("hstd_ready"), 2)
            dve.reciprocal(HRS[:, 0:8], HSD[:, 0:8])
            dve.drain()
            vec = vector(dve, "gla_head_gain_3")
            for t in range(TT):
                for h in range(GLA_H):
                    o = OG[t][:, h * GLA_DV:(h + 1) * GLA_DV]
                    j = t * GLA_H + h
                    ins = dve.scalar_tensor_tensor(o, o, HRS[:, j:j + 1], vec, ALU.mult, ALU.mult)
            used(ins)
            dve.drain()
            dve.wait_ge(ev("gz_ready"), 4)
            for t in range(TT):
                ins = dve.tensor_tensor(OG[t], OG[t], GZ[:, t, :], ALU.mult)
            ins.then_inc(ev("og_ready"), 1)
            add_to_x("go0", 0)
            add_to_x("go1", 1)
            dve.drain()
            used(rms_norm(dve, row(9), X, vector(dve, "s5_norm_3")))
            dve.drain()
            dve.sem_inc(ev("hs_ready"), 1)
            dve.wait_ge(ev("s5_setup"), 1)
            dt, xr, xt, ex, s1, sh = work[0:6]
            re, im = PC[:, 3, 0:64], PC[:, 3, 64:128]
            dve.tensor_tensor(xr, re, dt, ALU.mult)
            dve.tensor_tensor(xt, im, dt, ALU.mult)
            dve.drain()
            dve.tensor_scalar(xt, xt, INV_2PI, None, ALU.mult)
            dve.drain()
            dve.tensor_scalar(TH, xt, MAGIC, None, ALU.add)
            dve.drain()
            dve.tensor_scalar(TH, TH, MAGIC, None, ALU.subtract)
            dve.drain()
            dve.tensor_tensor(TH, xt, TH, ALU.subtract).then_inc(ev("turns_ready"), 1)
            xc, po, mk = work[6], work[7], work[8]
            dve.tensor_scalar(xc, xr, -0.5, 0.5, ALU.max, ALU.min)
            dve.drain()
            dve.tensor_scalar(po, xc, 1.0 / 9, 1.0, ALU.mult, ALU.add)
            dve.drain()
            for j in range(8, 1, -1):
                dve.tensor_tensor(po, po, xc, ALU.mult)
                dve.drain()
                dve.tensor_scalar(po, po, 1.0 / j, 1.0, ALU.mult, ALU.add)
                dve.drain()
            dve.tensor_tensor(po, po, xc, ALU.mult)
            dve.tensor_tensor(mk, xr, xc, ALU.is_equal)
            dve.wait_ge(ev("s5_setup"), 2)
            dve.tensor_scalar_add(ex, ex, -1.0)
            dve.drain()
            dve.copy_predicated(ex, mk.bitcast(I32), po)
            dve.drain()
            dve.tensor_scalar_add(RR, ex, 1.0)
            s2, a_, b_, m_, t_ = work[9:14]
            dve.tensor_tensor(s2, sh, sh, ALU.mult)
            dve.drain()
            dve.tensor_tensor(b_, RR, s1, ALU.mult)
            dve.tensor_tensor(a_, RR, s2, ALU.mult)
            dve.drain()
            dve.scalar_tensor_tensor(a_, a_, -2.0, ex, ALU.mult, ALU.add)
            dve.tensor_tensor(m_, re, re, ALU.mult)
            dve.tensor_tensor(t_, im, im, ALU.mult)
            dve.drain()
            dve.tensor_tensor(m_, m_, t_, ALU.add)
            dve.drain()
            dve.reciprocal(m_, m_)
            dve.tensor_tensor(CRE, a_, re, ALU.mult)
            dve.tensor_tensor(t_, b_, im, ALU.mult)
            dve.tensor_tensor(CIM, b_, re, ALU.mult)
            dve.tensor_tensor(a_, a_, im, ALU.mult)
            dve.drain()
            dve.tensor_tensor(CRE, CRE, t_, ALU.add)
            dve.tensor_tensor(CIM, CIM, a_, ALU.subtract)
            dve.drain()
            dve.tensor_tensor(CRE, CRE, m_, ALU.mult)
            dve.tensor_tensor(CIM, CIM, m_, ALU.mult)
            dve.drain()
            dve.wait_ge(ev("s5_bc_landed"), 96)
            b3 = [CRE.unsqueeze(2).to_broadcast([P, 64, S5_I]), CIM.unsqueeze(2).to_broadcast([P, 64, S5_I])]
            t1 = half(5, 1).rearrange("p (g i) -> p g i", g=64)
            t2 = half(6, 0).rearrange("p (g i) -> p g i", g=64)
            dve.tensor_tensor(t1, BB[:, 0], b3[1], ALU.mult)
            dve.tensor_tensor(t2, BB[:, 1], b3[1], ALU.mult)
            dve.tensor_tensor(BB[:, 0], BB[:, 0], b3[0], ALU.mult)
            dve.tensor_tensor(BB[:, 1], BB[:, 1], b3[0], ALU.mult)
            dve.drain()
            dve.tensor_tensor(BB[:, 0], BB[:, 0], t2, ALU.subtract)
            dve.tensor_tensor(BB[:, 1], BB[:, 1], t1, ALU.add)
            dve.drain()
            dve.sem_inc(ev("coef_ready"), 1)
            dve.sem_inc(ev("s5_scanned"), 1)
            dve.sem_inc(ev("s5_y"), 2)

            def turn_back(g, hb):
                dve.wait_ge(ev("s5_bu_done"), g + 2)
                dve.wait_ge(ev("s5_trig"), g + 1)
                bre, bim = PS[:, 2 * hb:2 * hb + 2, 0:T], PS[:, 2 * hb:2 * hb + 2, T:2 * T]
                dve.tensor_tensor(IC, bre, SCOS[hb], ALU.mult)
                dve.tensor_tensor(JS, bim, SSIN[hb], ALU.mult)
                dve.tensor_tensor(JC, bim, SCOS[hb], ALU.mult)
                dve.tensor_tensor(IS, bre, SSIN[hb], ALU.mult).then_inc(ev("s5_in"), 1)

            def angles(g, par, hb):
                dve.wait_ge(ev("s5_rounded"), g + 1)
                for j in range(2):
                    ins = dve.scalar_tensor_tensor(ANG[:, j, :], iota_t, TC[par][:, 0, 2 * hb + j:2 * hb + j + 1],
                                                   RND[:, j, :], ALU.mult, ALU.subtract)
                ins.then_inc(ev("s5_angles"), 1)

            def output(ct, par):
                dve.wait_ge(ev("s5_half_done"), ct * 2 + 4)
                dve.wait_ge(ev("s5_skip"), ct + 1)
                u = U16[:, bass.ds(ct, 1), :].rearrange("p a t -> p (a t)")
                dve.scalar_tensor_tensor(u, u, DCOL[par], PS[:, 6 + par, 0:T], ALU.mult, ALU.add).then_inc(ev("s5_y"), 1)

            def tile(ct, par, first, last):
                for hb in range(2):
                    g = ct * 2 + hb
                    dve.wait_ge(ev("s5_sums"), g + 1)
                    dve.wait_ge(ev("s5_half_done"), g + 1)
                    for j in range(2):
                        r_ = TC[par][:, 1, 2 * hb + j:2 * hb + j + 1].to_broadcast([P, T])
                        dve.tensor_tensor_scan(SB[hb][:, j, :], r_, JC[:, j, :], 0.0, ALU.mult, ALU.add)
                        ins = dve.tensor_tensor_scan(SA[hb][:, j, :], r_, IC[:, j, :], 0.0, ALU.mult, ALU.add)
                    ins.then_inc(ev("s5_scanned"), 1)
                    dve.drain()
                    if not (last and hb == 1):
                        turn_back(g + 1, 1 - hb)
                    if not last:
                        angles(g + 2, 1 - par, hb)
                    dve.tensor_tensor(PA[hb], SCOS[hb], SA[hb], ALU.mult)
                    dve.drain()
                    dve.tensor_tensor(SA[hb], SSIN[hb], SA[hb], ALU.mult).then_inc(ev("s5_real_out"), 1)
                    if hb == 0 and not first:
                        output(ct - 1, 1 - par)

            angles(0, 0, 0)
            dve.wait_ge(ev("s5_trig"), 1)
            angles(1, 0, 1)
            turn_back(0, 0)
            tile(0, 0, True, False)
            tile(1, 1, False, False)
            with dve.Fori(1, S5_CT // 2 - 1) as i:
                tile(i * 2, 0, False, False)
                tile(i * 2 + 1, 1, False, False)
            tile(S5_CT - 2, 0, False, False)
            tile(S5_CT - 1, 1, False, True)
            output(S5_CT - 1, 1)
            dve.wait_ge(ev("glu_sig"), 1)
            dve.tensor_tensor(G16, U16, G16, ALU.mult)
            dve.drain()
            dve.tensor_tensor(G16, G16, Z16, ALU.mult).then_inc(ev("glu_ready"), 1)
            add_to_x("so0", 0)
            add_to_x("so1", 1)
            dve.drain()
            used(rms_norm(dve, X, X, vector(dve, "final_norm_3")))
            dve.drain()
            dve.sem_inc(ev("result_ready"), 1)


INPUTS = ["x", "c", "w_mod", "b_mod", "w_in", "b_in", "conv_w", "conv_b", "ln_a_g", "ln_a_b", "w_a", "b_a",
          "ln_v_g", "ln_v_b", "w_s", "b_s", "w_b", "b_b", "w_out", "b_out", "post1_g", "post1_b", "w_router",
          "b_router", "w_gu", "b_gu", "w_dn", "b_dn", "post2_g", "post2_b", "norm_in_g_2", "w_in_2", "conv_w_2",
          "conv_b_2", "gate_a_w_2", "gate_a_b_2", "gate_x_w_2", "gate_x_b_2", "lru_lambda_2", "w_out_2",
          "norm_out_g_2", "gla_norm_3", "gla_w_in_3", "gla_w_gate_up_3", "gla_b_gate_3", "gla_head_gain_3",
          "gla_w_out_3", "s5_norm_3", "s5_w_in_3", "s5_lam_re_3", "s5_lam_im_3", "s5_log_dt_3", "s5_b_re_3",
          "s5_b_im_3", "s5_c_re_3", "s5_c_im_3", "s5_d_3", "s5_w_glu_3", "s5_b_glu_3", "s5_w_out_3", "final_norm_3"]


def kernel(**inputs):
    import concourse.bacc as bacc
    from concourse.bass_utils import run_bass_kernel_spmd

    nc = bacc.Bacc("TRN2", target_bir_lowering=False, num_devices=1)
    arrays, A = {}, {}
    for name, a in [(n, inputs[n]) for n in INPUTS] + list(constants().items()):
        a = np.ascontiguousarray(a)
        arrays[f"in_{name}"] = a
        A[name] = nc.dram_tensor(f"in_{name}", a.shape, mybir.dt.from_np(a.dtype), kind="ExternalInput").ap()
    out = nc.dram_tensor("out", (1, T, D), F32, kind="ExternalOutput").ap()
    build(nc, A, out)
    r = run_bass_kernel_spmd(nc, [arrays], core_ids=[0])
    return r.results[0]["out"]
```
